# Optimizing a Trainium2 kernel written in Bass

```python
import jax, jax.numpy as jnp
from jax import lax
import numpy as np

D_MODEL = 1024
BATCH = 1
SEQ = 1024
DEPTH = 2
DEC_BATCH = 8
DEC_SEQ = 8
PAST_LEN = 1024
PAGE_SIZE = 128

N_SB_LAYERS = (DEPTH + 1) // 2
N_RET_LAYERS = DEPTH // 2
H_A = 8
HD_A = 64
W_A = H_A * HD_A
SB_BIAS_INIT = -6.0
H_B = 4
DK_B = 128
DV_B = 128
F_B = H_B * DK_B
W_B = H_B * DV_B
H_C = 4
DK_C = 256
DV_C = 512
QK_C = H_C * DK_C
W_C = H_C * DV_C

W_EVEN_IN = 4 * W_A + 2 * F_B + 2 * W_B
W_EVEN_MIX = W_A + W_B
W_ODD_IN = 2 * QK_C + 2 * W_C
SPLITS_EVEN = (W_A, 2 * W_A, 3 * W_A, 4 * W_A, 4 * W_A + F_B, 4 * W_A + 2 * F_B, 4 * W_A + 2 * F_B + W_B)
SPLITS_ODD = (QK_C, 2 * QK_C, 2 * QK_C + W_C)

Q_BLOCK = 128
HGRN_CHUNK = 64
RET_CHUNK = 128
ROPE_BASE = 10000.0
NORM_EPS = 1e-6

kernel_name = 'stickbreak_hgrn2_retention_decoder_step'

def rms_norm(x, g=None):
    xf = x.astype(jnp.float32)
    y = xf * lax.rsqrt(jnp.mean(xf * xf, axis=-1, keepdims=True) + NORM_EPS)
    if g is not None:
        y = y * g.astype(jnp.float32)
    return y.astype(x.dtype)

def rotary(x, pos):
    half = x.shape[-1] // 2
    inv = 1.0 / (ROPE_BASE ** jnp.linspace(0.0, 1.0, half, dtype=jnp.float32))
    ang = pos[:, None] * inv[None, :]
    cos = jnp.cos(ang)[None, :, None, :]
    sin = jnp.sin(ang)[None, :, None, :]
    xf = x.astype(jnp.float32)
    x1, x2 = xf[..., :half], xf[..., half:]
    return jnp.concatenate([x1 * cos - x2 * sin, x2 * cos + x1 * sin], axis=-1)

def to_chunks(a, chunk):
    b, t, h, d = a.shape
    return a.reshape(b, t // chunk, chunk, h, d).transpose(1, 0, 3, 2, 4)

def from_chunks(a):
    n, b, h, c, d = a.shape
    return a.transpose(1, 0, 3, 2, 4).reshape(b, n * c, h, d)

def sb_attend(q, k, v, qpos, kpos, bias):
    scale = q.shape[-1] ** -0.5
    z = jnp.einsum('bqhd,bkhd->bhqk', q.astype(jnp.float32), k.astype(jnp.float32)) * scale
    z = z + bias.astype(jnp.float32)[None, :, None, None]
    mask = (kpos[None, :] < qpos[:, None])[None, None]
    log_keep = jnp.where(mask, jax.nn.log_sigmoid(-z), 0.0)
    log_between = lax.cumsum(log_keep, axis=3, reverse=True) - log_keep
    w = jnp.where(mask, jnp.exp(jax.nn.log_sigmoid(z) + log_between), 0.0)
    return jnp.einsum('bhqk,bkhd->bqhd', w, v.astype(jnp.float32))

def sb_prompt(q, k, v, bias):
    b, t, h, d = q.shape
    nb = t // Q_BLOCK
    q_blocks = q.reshape(b, nb, Q_BLOCK, h, d).transpose(1, 0, 2, 3, 4)
    kpos = jnp.arange(t)
    qpos_blocks = kpos.reshape(nb, Q_BLOCK)
    o = lax.map(lambda a: sb_attend(a[0], k, v, a[1], kpos, bias), (q_blocks, qpos_blocks))
    return o.transpose(1, 0, 2, 3, 4).reshape(b, t, h, d)

def gla_chunk_scan(q, k, v, log_f, s0, chunk):
    mask = jnp.tril(jnp.ones((chunk, chunk), dtype=bool))[None, None, :, :, None]

    def step(S, inp):
        qc, kc, vc, gc = inp
        bcum = jnp.cumsum(gc, axis=2)
        o_inter = jnp.einsum('bhtk,bhkv->bhtv', qc * jnp.exp(bcum), S)
        diff = bcum[:, :, :, None, :] - bcum[:, :, None, :, :]
        decay = jnp.exp(jnp.where(mask, diff, -jnp.inf))
        scores = jnp.einsum('bhtk,bhsk,bhtsk->bhts', qc, kc, decay)
        o_intra = jnp.einsum('bhts,bhsv->bhtv', scores, vc)
        blast = bcum[:, :, -1, :]
        S_new = jnp.exp(blast)[..., None] * S + jnp.einsum('bhsk,bhsv->bhkv', kc * jnp.exp(blast[:, :, None, :] - bcum), vc)
        return S_new, o_inter + o_intra

    S_fin, o = lax.scan(step, s0, (to_chunks(q, chunk), to_chunks(k, chunk), to_chunks(v, chunk), to_chunks(log_f, chunk)))
    return from_chunks(o), S_fin

def retention_chunk_scan(q, k, v, log_gamma, s0, chunk):
    idx = jnp.arange(chunk, dtype=jnp.float32)
    rel = idx[:, None] - idx[None, :]
    causal = rel >= 0
    intra_decay = jnp.exp(jnp.where(causal[None], rel[None] * log_gamma[:, None, None], -jnp.inf))
    q_decay = jnp.exp((idx[None, :] + 1.0) * log_gamma[:, None])[None, :, :, None]
    k_decay = jnp.exp((chunk - 1.0 - idx[None, :]) * log_gamma[:, None])[None, :, :, None]
    chunk_decay = jnp.exp(chunk * log_gamma)[None, :, None, None]

    def step(S, inp):
        qc, kc, vc = inp
        o_inter = jnp.einsum('bhtk,bhkv->bhtv', qc, S) * q_decay
        scores = jnp.einsum('bhtk,bhsk->bhts', qc, kc) * intra_decay[None]
        o_intra = jnp.einsum('bhts,bhsv->bhtv', scores, vc)
        S_new = chunk_decay * S + jnp.einsum('bhsk,bhsv->bhkv', kc * k_decay, vc)
        return S_new, o_inter + o_intra

    S_fin, o = lax.scan(step, s0, (to_chunks(q, chunk), to_chunks(k, chunk), to_chunks(v, chunk)))
    return from_chunks(o), S_fin

def even_mixer(h, w_in, w_out, qg, kg, sbb, lb, og, s0, past_k, past_v, chunk):
    f32 = jnp.float32
    b, t, _ = h.shape
    qa, ka, va, ga, qb, fb, ib, gb = jnp.split(h @ w_in, SPLITS_EVEN, axis=-1)
    qa = rms_norm(qa.reshape(b, t, H_A, HD_A), qg)
    ka = rms_norm(ka.reshape(b, t, H_A, HD_A), kg)
    va = va.reshape(b, t, H_A, HD_A)
    if past_k is None:
        oa = sb_prompt(qa, ka, va, sbb)
    else:
        p = past_k.shape[1]
        keys = jnp.concatenate([past_k, ka.astype(past_k.dtype)], axis=1)
        vals = jnp.concatenate([past_v, va.astype(past_v.dtype)], axis=1)
        oa = sb_attend(qa, keys, vals, p + jnp.arange(t), jnp.arange(p + t), sbb)
    fb32 = fb.astype(f32).reshape(b, t, H_B, DK_B)
    lb = lb.reshape(H_B, DK_B)
    log_f = jnp.log(lb + (1.0 - lb) * jax.nn.sigmoid(fb32))
    k_b = (1.0 - lb) * jax.nn.sigmoid(-fb32)
    q_b = jax.nn.silu(qb.astype(f32)).reshape(b, t, H_B, DK_B)
    v_b = ib.astype(f32).reshape(b, t, H_B, DV_B)
    ob, s_new = gla_chunk_scan(q_b, k_b, v_b, log_f, s0, chunk)
    ob = rms_norm(ob, og)
    mix = jnp.concatenate([oa.reshape(b, t, W_A) * jax.nn.silu(ga.astype(f32)),
                           ob.reshape(b, t, W_B) * jax.nn.silu(gb.astype(f32))], axis=-1)
    return mix.astype(h.dtype) @ w_out, ka, va, s_new

def odd_mixer(h, pos, w_in, w_out, s0, chunk):
    f32 = jnp.float32
    b, t, _ = h.shape
    q, k, v, g = jnp.split(h @ w_in, SPLITS_ODD, axis=-1)
    q = rotary(q.reshape(b, t, H_C, DK_C), pos)
    k = rotary(k.reshape(b, t, H_C, DK_C), pos) * (DK_C ** -0.5)
    v = v.astype(f32).reshape(b, t, H_C, DV_C)
    log_gamma = jnp.log1p(-jnp.exp2(-5.0 - jnp.arange(H_C, dtype=f32)))
    o, s_new = retention_chunk_scan(q, k, v, log_gamma, s0, chunk)
    o = rms_norm(o).reshape(b, t, W_C) * jax.nn.silu(g.astype(f32))
    return o.astype(h.dtype) @ w_out, s_new

def setup_inputs(seed: int = 0) -> dict:
    key = jax.random.key(seed)
    ks = jax.random.split(key, 17)
    f32 = jnp.float32
    n_pages = PAST_LEN // PAGE_SIZE
    n_used = DEC_BATCH * n_pages
    n_pool = (5 * n_used + 3) // 4
    nrm = jax.random.normal
    x_prompt = nrm(ks[0], (BATCH, SEQ, D_MODEL), f32)
    x_sample = nrm(ks[1], (DEC_BATCH, DEC_SEQ, D_MODEL), f32)
    cache_k = nrm(ks[2], (N_SB_LAYERS, n_pool, PAGE_SIZE, H_A, HD_A), f32)
    cache_v = nrm(ks[3], (N_SB_LAYERS, n_pool, PAGE_SIZE, H_A, HD_A), f32)
    page_table = jax.random.permutation(ks[4], n_pool)[:n_used].reshape(DEC_BATCH, n_pages).astype(jnp.int32)
    state_hgrn = 0.5 * nrm(ks[5], (N_SB_LAYERS, DEC_BATCH, H_B, DK_B, DV_B), f32)
    state_ret = 0.5 * nrm(ks[6], (N_RET_LAYERS, DEC_BATCH, H_C, DK_C, DV_C), f32)
    norm_g = 1.0 + 0.1 * nrm(ks[7], (DEPTH, D_MODEL), f32)
    w_in_even = nrm(ks[8], (N_SB_LAYERS, D_MODEL, W_EVEN_IN), f32) * D_MODEL ** -0.5
    w_out_even = nrm(ks[9], (N_SB_LAYERS, W_EVEN_MIX, D_MODEL), f32) * W_EVEN_MIX ** -0.5
    q_norm_g = 1.0 + 0.1 * nrm(ks[10], (N_SB_LAYERS, HD_A), f32)
    k_norm_g = 1.0 + 0.1 * nrm(ks[11], (N_SB_LAYERS, HD_A), f32)
    sb_logit_bias = SB_BIAS_INIT + 0.1 * nrm(ks[16], (N_SB_LAYERS, H_A), f32)
    hgrn_lower_bounds = 0.5 * nrm(ks[12], (N_SB_LAYERS + 1, F_B), f32)
    hgrn_out_norm_g = 1.0 + 0.1 * nrm(ks[13], (N_SB_LAYERS, DV_B), f32)
    w_in_odd = nrm(ks[14], (N_RET_LAYERS, D_MODEL, W_ODD_IN), f32) * D_MODEL ** -0.5
    w_out_odd = nrm(ks[15], (N_RET_LAYERS, W_C, D_MODEL), f32) * W_C ** -0.5
    return {'x_prompt': x_prompt, 'x_sample': x_sample, 'cache_k': cache_k, 'cache_v': cache_v,
            'page_table': page_table, 'state_hgrn': state_hgrn, 'state_ret': state_ret,
            'norm_g': norm_g, 'w_in_even': w_in_even, 'w_out_even': w_out_even,
            'q_norm_g': q_norm_g, 'k_norm_g': k_norm_g, 'sb_logit_bias': sb_logit_bias,
            'hgrn_lower_bounds': hgrn_lower_bounds,
            'hgrn_out_norm_g': hgrn_out_norm_g, 'w_in_odd': w_in_odd, 'w_out_odd': w_out_odd}

def reference(x_prompt, x_sample, cache_k, cache_v, page_table, state_hgrn, state_ret, norm_g,
              w_in_even, w_out_even, q_norm_g, k_norm_g, sb_logit_bias, hgrn_lower_bounds,
              hgrn_out_norm_g, w_in_odd, w_out_odd):
    f32 = jnp.float32
    bp, tp, _ = x_prompt.shape
    bs, ts, _ = x_sample.shape
    past_len = page_table.shape[1] * cache_k.shape[2]
    pos_p = jnp.arange(tp, dtype=f32)
    pos_s = past_len + jnp.arange(ts, dtype=f32)
    lower_bounds = jnp.cumsum(jax.nn.softmax(hgrn_lower_bounds.astype(f32), axis=0), axis=0)
    yp, ys = x_prompt, x_sample
    k_p, v_p, k_s, v_s, hg_p, hg_s, rt_p, rt_s = [], [], [], [], [], [], [], []
    for layer in range(DEPTH):
        e = layer // 2
        hp = rms_norm(yp, norm_g[layer])
        hs = rms_norm(ys, norm_g[layer])
        if layer % 2 == 0:
            wts = (w_in_even[e], w_out_even[e], q_norm_g[e], k_norm_g[e], sb_logit_bias[e],
                   lower_bounds[e], hgrn_out_norm_g[e])
            past_k = jnp.take(cache_k[e], page_table, axis=0).reshape(bs, past_len, H_A, HD_A)
            past_v = jnp.take(cache_v[e], page_table, axis=0).reshape(bs, past_len, H_A, HD_A)
            s0p = jnp.zeros((bp, H_B, DK_B, DV_B), f32)
            op, kn, vn, sn = even_mixer(hp, *wts, s0p, None, None, HGRN_CHUNK)
            os_, kn2, vn2, sn2 = even_mixer(hs, *wts, state_hgrn[e].astype(f32), past_k, past_v, ts)
            k_p.append(kn.astype(cache_k.dtype)); v_p.append(vn.astype(cache_v.dtype))
            k_s.append(kn2.astype(cache_k.dtype)); v_s.append(vn2.astype(cache_v.dtype))
            hg_p.append(sn.astype(state_hgrn.dtype)); hg_s.append(sn2.astype(state_hgrn.dtype))
        else:
            s0p = jnp.zeros((bp, H_C, DK_C, DV_C), f32)
            op, sn = odd_mixer(hp, pos_p, w_in_odd[e], w_out_odd[e], s0p, RET_CHUNK)
            os_, sn2 = odd_mixer(hs, pos_s, w_in_odd[e], w_out_odd[e], state_ret[e].astype(f32), ts)
            rt_p.append(sn.astype(state_ret.dtype)); rt_s.append(sn2.astype(state_ret.dtype))
        yp = yp + op
        ys = ys + os_
    return (yp, ys, jnp.stack(k_p), jnp.stack(v_p), jnp.stack(k_s), jnp.stack(v_s),
            jnp.stack(hg_p), jnp.stack(hg_s), jnp.stack(rt_p), jnp.stack(rt_s))


_drawn_inputs = setup_inputs


def setup_inputs(seed=0):
    import zlib

    import numpy as np

    out = dict(_drawn_inputs(seed))
    spreads = {}
    factors = {'q_norm_g': 64.0, 'sb_logit_bias': 64.0, 'cache_k': 8.0, 'cache_v': 8.0}
    for name, (base, spread) in spreads.items():
        noise = np.random.default_rng([zlib.crc32(name.encode()), seed]).standard_normal(out[name].shape)
        drawn = base * np.exp(spread * noise) if base else spread * noise
        out[name] = __import__('jax').numpy.asarray(drawn.astype(out[name].dtype))
    for name, factor in factors.items():
        out[name] = (out[name] * factor).astype(out[name].dtype)
    return out
```

```python
from contextlib import ExitStack, contextmanager

import numpy as np

import concourse.bass as bass
from concourse import mybir

F32 = mybir.dt.float32
F32R = mybir.dt.float32r
I32 = mybir.dt.int32
ACT = mybir.ActivationFunctionType
ALU = mybir.AluOpType
AX_X = mybir.AxisListType.X

P = 128
D = 1024
KD = D // P
TP = 1024
NS, LS = 8, 8
TS = NS * LS
T = TP + TS
NT = TP // P + 1
HA, DA = 8, 64
WA = HA * DA
HB, DB = 4, 128
WB = HB * DB
HC, DK, DV = 4, 256, 512
WC = HC * DV
PAGE = 128
NPAGE = 8
W_EVEN = 4 * WA + 4 * WB
W_ODD = 2 * HC * DK + 2 * WC
EPS = 1e-6
MASKED = -1e30

WBLK = 256
GROUPS = [(0, 364), (364, 362), (726, 362)]


@contextmanager
def repeat(engine, n):
    if n == 1:
        yield 0
    else:
        with engine.Fori(0, n) as i:
            yield i


def load_exp_ln(nc):
    nc.scalar.add_instruction(mybir.InstLoadActFuncSet(
        name=nc.get_next_instruction_name(), engine=mybir.EngineType.Activation, ins=[], outs=[], act_func_set_id=6))


def rows_of(t):
    return P if t < NT - 1 else TS



UNITS = {"norm": 2 * NT, "copy": 2 * NT, "silu_tm": 2 * NT, "silu": 12, "plain": 12, "rotary": 12}
BY_VECTOR = ("norm", "copy", "rotary")
NBANK = 6
NSTAGE = 3


def project_in(nc, tag, x_of, gain_dram, weight, segments, consts, qk_gain_dram=None):
    with nc.cleanup_on_exit(), ExitStack() as ctx:
        sb = lambda n, s, d=F32: ctx.enter_context(nc.sbuf_tensor(f"{tag}_{n}", s, d))
        sem = lambda n: nc.alloc_semaphore(f"{tag}_{n}")
        even = tag == "even"
        bank = [ctx.enter_context(nc.psum_tensor(f"{tag}_bank{i}", [P, 512], F32)) for i in range(NBANK)]
        turn = [ctx.enter_context(nc.psum_tensor(f"{tag}_turn{i}", [P, 4, P], F32)) for i in range(2)]

        h_hi = sb("h_hi", [P, KD, T], F32R)
        h_lo = sb("h_lo", [P, KD, T], F32R)
        x_in = sb("x_in", [P, 2, D])
        x_n = sb("x_n", [P, 2, D])
        square = sb("square", [P, D])
        ssum = sb("ssum", [P, NT])
        std = sb("std", [P, NT])
        rstd = sb("rstd", [P, NT])
        gain = sb("gain", [P, KD])
        h_f = sb("h_f", [P, 2, 4, P])
        ident = sb("ident", [P, P])
        eps = sb("eps", [P, 1])
        raw = sb("raw", [P, 2, KD // 2, WBLK])
        w_hi = sb("w_hi", [P, 2, KD, WBLK], F32R)
        w_lo = sb("w_lo", [P, 2, KD, WBLK], F32R)
        stage_tm = sb("stage_tm", [P, NSTAGE, WBLK])
        if even:
            stage_fm = sb("stage_fm", [P, 2, T])
            qk_gain = sb("qk_gain", [P, 2, DA])
            head_sq = sb("head_sq", [P, 2, WBLK])
            head_ss = sb("head_ss", [P, 2, 4])
            head_std = sb("head_std", [P, 2, 4])
            head_rstd = sb("head_rstd", [P, 2, 4])
            head_n = sb("head_n", [P, 2, WBLK])
        else:
            stage_rot = sb("stage_rot", [P, 2, 2, T])
            cos = sb("cos", [P, T])
            sin = sb("sin", [P, T])
            rot = sb("rot", [P, 4, 364])

        const_in = sem("const_in")
        x_load = [sem("x_load0"), sem("x_load1")]
        sumsq_done, std_done, rstd_done, xn_done = sem("sumsq"), sem("std"), sem("rstd"), sem("xn")
        turned, gained, hi_done, lo_done = sem("turned"), sem("gained"), sem("hi"), sem("lo")
        raw_in = [sem("raw0"), sem("raw1")]
        w_hi_done, w_split, w_used = sem("w_hi"), sem("w_split"), sem("w_used")
        w_at_hand = sem("w_at_hand")
        full = sem("full")
        free = sem("free")
        staged = sem("staged")
        left_tm = [sem(f"left_tm{i}") for i in range(NSTAGE)]
        left_fm = [sem("left_fm0"), sem("left_fm1")]
        eps_set = sem("eps_set")
        head_sq_done, head_ss_done, head_std_done, head_rstd_done, head_n_done = (
            sem("hsq"), sem("hss"), sem("hstd"), sem("hrstd"), sem("hn"))

        NBLK = 2 * sum(n for _, n, _ in segments)
        NCONST = 16 * 4
        w_rows = weight.rearrange("(c p) n -> p c n", p=P)
        block = ctx.enter_context(nc.Block())

        def starts():
            at = dict(unit=0, tm=0, fm=0, norm=0, staged=0)
            for kind, n, place in segments:
                yield kind, n, place, dict(at)
                at["unit"] += n * UNITS[kind]
                at["tm"] += n * UNITS[kind] * (kind in ("norm", "copy", "silu_tm"))
                at["fm"] += {"silu": 4, "plain": 4, "rotary": 2}.get(kind, 0) * n
                at["norm"] += n * UNITS[kind] * (kind == "norm")
                at["staged"] += {"norm": UNITS[kind], "rotary": 12}.get(kind, 0) * n

        @block.sync
        def _(sp):
            sp.dma_start(ident[:], consts["ident"]).then_inc(const_in, 16)
            sp.dma_start(gain[:], gain_dram, allow_slow_non_contiguous=True).then_inc(const_in, 16)
            if even:
                for i in range(2):
                    sp.dma_start(qk_gain[:, i, :], qk_gain_dram[i].to_broadcast([P, DA])).then_inc(const_in, 16)
            else:
                sp.dma_start(cos[:], consts["cos"]).then_inc(const_in, 16)
                sp.dma_start(sin[:], consts["sin"]).then_inc(const_in, 16)
            for t in range(NT):
                if t >= 2:
                    sp.wait_ge(xn_done, t - 1)
                sp.dma_start(x_in[0:rows_of(t), t % 2, :], x_of(t)).then_inc(x_load[t % 2], 16)
                if t in (1, 2):
                    sp.dma_start(raw[:, t - 1, :, :], w_rows[:, 4 * (t - 1):4 * t, 0:WBLK]).then_inc(raw_in[t - 1], 16)
            with sp.Fori(1, NBLK) as b:
                for half in range(2):
                    sp.wait_ge(w_split, 2 * b + half - 1)
                    sp.dma_start(raw[:, half, :, :],
                                 w_rows[:, half * 4:half * 4 + 4, bass.ds(b * WBLK, WBLK)]).then_inc(raw_in[half], 16)

        @block.gpsimd
        def _(pool):
            pool.sem_inc(w_used, 1)
            with pool.Fori(0, NBLK // 2) as pair:
                for slot in range(2):
                    pool.wait_ge(w_used, 2 * pair + slot + 1)
                    for half in range(2):
                        r = raw[:, half, :, :]
                        hi = w_hi[:, slot, half * 4:half * 4 + 4, :]
                        lo = w_lo[:, slot, half * 4:half * 4 + 4, :]
                        pool.wait_ge(raw_in[half], 32 * pair + 16 * slot + 16)
                        pool.sem_inc(w_at_hand, 1)
                        nc.gpsimd.tensor_copy(hi, r).then_inc(w_hi_done, 1)
                        pool.wait_ge(w_hi_done, 4 * pair + 2 * slot + half + 1)
                        nc.gpsimd.tensor_tensor(lo, r, hi.bitcast(F32), ALU.subtract).then_inc(w_split, 1)

        @block.tensor
        def _(pe):
            pe.sem_inc(free, NBANK)
            pe.wait_ge(const_in, NCONST)
            for t in range(NT):
                r = rows_of(t)
                pe.wait_ge(xn_done, t + 1)
                for k in range(2):
                    if t >= 1:
                        pe.wait_ge(gained, 2 * t + k - 1)
                    for c in range(4):
                        mm = pe.transpose(turn[k][:, c, 0:r], x_n[0:r, t % 2, (4 * k + c) * P:(4 * k + c + 1) * P],
                                          ident[0:r, 0:r])
                    mm.then_inc(turned, 1)
            pe.wait_ge(lo_done, 2 * NT)

            def product(out, pairs, opens_block):
                for j, (stationary, moving) in enumerate(pairs):
                    mm = pe.matmul(out, stationary, moving, start=(j == 0), stop=(j == len(pairs) - 1))
                    if j == 0 and opens_block:
                        mm.then_inc(w_used, 1)
                return mm.then_inc(full, 1)

            def parts(h, w):
                return ((h[0], w[0]), (h[0], w[1]), (h[1], w[0]))

            pairs_before, was_by_vector = 0, True
            for kind, n, _, at in starts():
                if (kind in BY_VECTOR) != was_by_vector:
                    pe.wait_ge(free, at["unit"] + NBANK)
                was_by_vector = kind in BY_VECTOR
                with repeat(pe, n) as it:
                    for s in range(2):
                        pe.wait_ge(w_split, 4 * it + 4 * pairs_before + 2 * s + 2)
                        for j in range(UNITS[kind] // 2):
                            u = s * (UNITS[kind] // 2) + j
                            pe.wait_ge(free, it * UNITS[kind] + (at["unit"] + u + 1))
                            if kind in ("norm", "copy", "silu_tm"):
                                tok = slice(j * P, j * P + rows_of(j))
                                out = bank[u % NBANK][0:rows_of(j), 0:WBLK]
                                ops = [(h, w) for c in range(KD)
                                       for h, w in parts((h_hi[:, c, tok], h_lo[:, c, tok]), (w_hi[:, s, c, :], w_lo[:, s, c, :]))]
                            else:
                                g, f = (j // 2, j % 2) if kind == "rotary" else (j % 3, j // 3)
                                g0, gn = GROUPS[g]
                                out = bank[u % NBANK][:, 0:gn]
                                cols = slice(f * P, f * P + P)
                                ops = [(w, h) for c in range(KD)
                                       for h, w in parts((h_hi[:, c, g0:g0 + gn], h_lo[:, c, g0:g0 + gn]),
                                                         (w_hi[:, s, c, cols], w_lo[:, s, c, cols]))]
                            product(out, ops, j == 0)
                pairs_before += n

        @block.scalar
        def _(act):
            for i in range(NSTAGE):
                act.sem_inc(left_tm[i], 16)
            for i in range(2):
                act.sem_inc(left_fm[i], 16)

            def cast_hi(t, k):
                r = rows_of(t)
                act.wait_ge(gained, 2 * t + k + 1)
                nc.scalar.copy(h_hi[:, 4 * k:4 * k + 4, t * P:t * P + r], h_f[:, k, :, 0:r]).then_inc(hi_done, 1)

            act.wait_ge(eps_set, 1)
            for t in range(NT):
                r = rows_of(t)
                act.wait_ge(x_load[t % 2], 16 * (t // 2 + 1))
                nc.scalar.activation(square[0:r, :], x_in[0:r, t % 2, :], ACT.Square,
                                     accum_out=ssum[0:r, t:t + 1]).then_inc(sumsq_done, 1)
                act.wait_ge(sumsq_done, t + 1)
                nc.scalar.activation(std[0:r, t:t + 1], ssum[0:r, t:t + 1], ACT.Sqrt,
                                     bias=eps[0:r, :], scale=1.0 / D).then_inc(std_done, 1)
                if t >= 1:
                    cast_hi(t - 1, 0)
                    cast_hi(t - 1, 1)
            cast_hi(NT - 1, 0)
            cast_hi(NT - 1, 1)

            for kind, n, place, at in starts():
                with repeat(act, n) as it:
                    for u in range(UNITS[kind]):
                        s, j = divmod(u, UNITS[kind] // 2)
                        r = rows_of(j) if kind in ("norm", "copy", "silu_tm") else P
                        src = bank[u % NBANK]
                        this = it * UNITS[kind] + (at["unit"] + u + 1)
                        slot = u % NSTAGE
                        if kind == "norm":
                            nth = it * UNITS[kind] + (at["norm"] + u + 1)
                            act.wait_ge(full, this)
                            act.wait_ge(head_ss_done, nth)
                            nc.scalar.activation(head_sq[0:r, u % 2, :], src[0:r, 0:WBLK], ACT.Square).then_inc(head_sq_done, 1)
                            act.wait_ge(head_ss_done, nth + 2)
                            nc.scalar.activation(head_std[0:r, u % 2, :], head_ss[0:r, u % 2, :], ACT.Sqrt,
                                                 bias=eps[0:r, :], scale=1.0 / DA).then_inc(head_std_done, 1)
                            act.wait_ge(staged, it * UNITS[kind] + (at["staged"] + u + 1))
                        elif kind == "copy":
                            act.wait_ge(free, this + NBANK)
                        elif kind == "silu_tm":
                            act.wait_ge(full, this)
                            act.wait_ge(left_tm[slot], it * (16 * UNITS[kind] // NSTAGE) + 16 * ((at["tm"] + u) // NSTAGE) + 16)
                            nc.scalar.activation(stage_tm[0:r, slot, :], src[0:r, 0:WBLK], ACT.Silu).then_inc(free, 1)
                            act.wait_ge(free, this + NBANK)
                        if kind in ("norm", "copy", "silu_tm"):
                            act.dma_start(place(j, it * 2 * WBLK + s * WBLK), stage_tm[0:r, slot, :]).then_inc(left_tm[slot], 16)
                        if kind in ("silu", "plain"):
                            f, g = j // 3, j % 3
                            row = 2 * s + f
                            slot = row % 2
                            g0, gn = GROUPS[g]
                            act.wait_ge(full, this)
                            if g == 0:
                                act.wait_ge(left_fm[slot], it * 32 + 16 * ((at["fm"] + row) // 2) + 16)
                            nc.scalar.activation(stage_fm[:, slot, g0:g0 + gn], src[:, 0:gn],
                                                 ACT.Silu if kind == "silu" else ACT.Copy).then_inc(free, 1)
                            if g == 2:
                                act.wait_ge(free, this + NBANK)
                                act.dma_start(place(it * 4 + row), stage_fm[:, slot, :]).then_inc(left_fm[slot], 16)
                        if kind == "rotary" and j == 5:
                            act.wait_ge(staged, it * 12 + (at["staged"] + 6 * s + 6))
                            act.dma_start(place(it * 2 + s), stage_rot[:, s, :, :]).then_inc(left_fm[s], 16)
            tm = sum(n * UNITS[k] for k, n, _ in segments if k in ("norm", "copy", "silu_tm"))
            fm = sum(n * {"silu": 4, "plain": 4, "rotary": 2}.get(k, 0) for k, n, _ in segments)
            for i in range(NSTAGE):
                act.wait_ge(left_tm[i], 16 * (tm // NSTAGE) + 16)
            for i in range(2):
                act.wait_ge(left_fm[i], 16 * (fm // 2) + 16)

        @block.vector
        def _(dve):
            nc.vector.memset(eps[:], EPS).then_inc(eps_set, 1)
            dve.sem_inc(head_ss_done, 2)

            def gain_and_split(t):
                r = rows_of(t)
                for k in range(2):
                    dve.wait_ge(turned, 2 * t + k + 1)
                    if t >= 1:
                        dve.wait_ge(lo_done, 2 * t + k - 1)
                        dve.wait_ge(hi_done, 2 * t + k - 1)
                    dve.tensor_tensor(h_f[:, k, :, 0:r], turn[k][:, :, 0:r],
                                      gain[:, 4 * k:4 * k + 4].unsqueeze(2).to_broadcast([P, 4, r]), ALU.mult).then_inc(gained, 1)
                for k in range(2):
                    hi = h_hi[:, 4 * k:4 * k + 4, t * P:t * P + r]
                    dve.wait_ge(hi_done, 2 * t + k + 1)
                    dve.tensor_tensor(h_lo[:, 4 * k:4 * k + 4, t * P:t * P + r], h_f[:, k, :, 0:r],
                                      hi.bitcast(F32), ALU.subtract).then_inc(lo_done, 1)

            dve.wait_ge(const_in, NCONST)
            for t in range(NT):
                r = rows_of(t)
                dve.wait_ge(std_done, t + 1)
                dve.reciprocal(rstd[0:r, t:t + 1], std[0:r, t:t + 1]).then_inc(rstd_done, 1)
                dve.wait_ge(rstd_done, t + 1)
                if t >= 2:
                    dve.wait_ge(turned, 2 * t - 2)
                dve.tensor_scalar(x_n[0:r, t % 2, :], x_in[0:r, t % 2, :], rstd[0:r, t:t + 1], None,
                                  ALU.mult).then_inc(xn_done, 1)
                if t >= 1:
                    gain_and_split(t - 1)
            gain_and_split(NT - 1)

            norm_segments = 0
            for kind, n, _, at in starts():
                if kind in ("silu", "silu_tm", "plain"):
                    continue
                with repeat(dve, n) as it:
                    for u in range(UNITS[kind]):
                        s, j = divmod(u, UNITS[kind] // 2)
                        r = rows_of(j) if kind != "rotary" else P
                        src = bank[u % NBANK]
                        this = it * UNITS[kind] + (at["unit"] + u + 1)
                        slot = u % NSTAGE
                        slot_left = it * (16 * UNITS[kind] // NSTAGE) + 16 * ((at["tm"] + u) // NSTAGE) + 16
                        if kind == "norm":
                            nth = it * UNITS[kind] + (at["norm"] + u + 1)
                            heads = lambda x: x.rearrange("p (h d) -> p h d", d=DA)
                            dve.wait_ge(head_sq_done, nth)
                            dve.tensor_reduce(head_ss[0:r, u % 2, :], heads(head_sq[0:r, u % 2, :]), AX_X, ALU.add).then_inc(head_ss_done, 1)
                            dve.wait_ge(head_std_done, nth)
                            dve.reciprocal(head_rstd[0:r, u % 2, :], head_std[0:r, u % 2, :]).then_inc(head_rstd_done, 1)
                            dve.wait_ge(head_rstd_done, nth)
                            dve.tensor_tensor(heads(head_n[0:r, u % 2, :]), heads(src[0:r, 0:WBLK]),
                                              head_rstd[0:r, u % 2, :].unsqueeze(2).to_broadcast([r, 4, DA]), ALU.mult).then_inc(free, 1)
                            dve.wait_ge(free, this + NBANK)
                            dve.wait_ge(left_tm[slot], slot_left)
                            dve.tensor_tensor(heads(stage_tm[0:r, slot, :]), heads(head_n[0:r, u % 2, :]),
                                              qk_gain[0:r, norm_segments, :].unsqueeze(1).to_broadcast([r, 4, DA]), ALU.mult).then_inc(staged, 1)
                        elif kind == "copy":
                            dve.wait_ge(full, this)
                            dve.wait_ge(left_tm[slot], slot_left)
                            dve.tensor_copy(stage_tm[0:r, slot, :], src[0:r, 0:WBLK]).then_inc(free, 1)
                        elif j % 2 == 1:
                            g0, gn = GROUPS[j // 2]
                            scale = 1.0 if at["unit"] == 0 else DK ** -0.5
                            c, sn = cos[:, g0:g0 + gn], sin[:, g0:g0 + gn]
                            x1, x2 = bank[(u - 1) % NBANK][:, 0:gn], src[:, 0:gn]
                            before = it * 12 + (at["staged"] + 6 * s + (j // 2) * 2)
                            dve.wait_ge(full, this)
                            dve.wait_ge(staged, before)
                            dve.scalar_tensor_tensor(rot[:, 0, 0:gn], x1, scale, c, ALU.mult, ALU.mult)
                            dve.scalar_tensor_tensor(rot[:, 1, 0:gn], x1, scale, sn, ALU.mult, ALU.mult).then_inc(free, 1)
                            dve.scalar_tensor_tensor(rot[:, 2, 0:gn], x2, scale, sn, ALU.mult, ALU.mult)
                            dve.scalar_tensor_tensor(rot[:, 3, 0:gn], x2, scale, c, ALU.mult, ALU.mult).then_inc(free, 1)
                            dve.wait_ge(free, this + NBANK)
                            if j == 1:
                                dve.wait_ge(left_fm[s], it * 16 + 16 * (at["fm"] // 2) + 16)
                            dve.tensor_tensor(stage_rot[:, s, 0, g0:g0 + gn], rot[:, 0, 0:gn], rot[:, 2, 0:gn], ALU.subtract).then_inc(staged, 1)
                            dve.tensor_tensor(stage_rot[:, s, 1, g0:g0 + gn], rot[:, 3, 0:gn], rot[:, 1, 0:gn], ALU.add).then_inc(staged, 1)
                if kind == "norm":
                    norm_segments += 1



def attend_prompt(nc, q_tm, k_tm, v_tm, gate_fm, bias_dram, mix_fm, consts):
    with nc.cleanup_on_exit(), ExitStack() as ctx:
        sb = lambda n, s, d=F32: ctx.enter_context(nc.sbuf_tensor(f"ap_{n}", s, d))
        sem = lambda n: nc.alloc_semaphore(f"ap_{n}")
        NQ = 512
        z = [ctx.enter_context(nc.psum_tensor(f"ap_z{i}", [P, NQ], F32)) for i in range(4)]
        o = [ctx.enter_context(nc.psum_tensor(f"ap_o{i}", [P, NQ], F32)) for i in range(2)]
        turn = [ctx.enter_context(nc.psum_tensor(f"ap_turn{i}", [P, 4, P], F32)) for i in range(2)]
        ident, tri, ones, mask = sb("ident", [P, P]), sb("tri", [P, P]), sb("ones", [P, P]), sb("mask", [P, P])
        qk_in = sb("qk_in", [P, 2, 8, P])
        v_in, v = sb("v_in", [P, 8, P]), sb("v", [P, 8, P])
        gate = sb("gate", [P, TP])
        qk = sb("qk", [P, 2, TP])
        biases = sb("biases", [P, HA])
        bias = sb("bias", [P, 2])
        soft = sb("soft", [P, 2, NQ])
        relu = sb("relu", [P, 2, NQ])
        keep = sb("keep", [P, 3, NQ])
        carry = sb("carry", [P, 3, NQ])
        w = sb("w", [P, 2, NQ])
        mix = sb("mix", [P, TP])

        head_steps = [(1, kb, max(0, kb - 4) * P) for kb in range(7, -1, -1)] + [(0, kb, kb * P) for kb in range(3, -1, -1)]
        steps = [(e, half, kb, lo) for e in range(2) for half, kb, lo in head_steps]
        NSTEP = len(steps)
        opens = [kb == (7 if half else 3) for _, half, kb, _ in steps]
        closes = [kb == 0 for _, _, kb, _ in steps]
        run = [2 * e + 1 - half for e, half, _, _ in steps]
        run_end = [i + 1 for i in range(NSTEP) if closes[i]]

        const_in = sem("const_in")
        qk_load, v_load, gate_load = sem("qk_load"), sem("v_load"), sem("gate_load")
        turned, turn_read = sem("turned"), sem("turn_read")
        v_held, bias_held = sem("v_held"), sem("bias_held")
        logits, abs_done, exp_done, soft_done = sem("logits"), sem("abs"), sem("exp"), sem("soft")
        relu_done, keep_done, carry_done = sem("relu"), sem("keep"), sem("carry")
        summed, w_done, pv_done = sem("summed"), sem("w"), sem("pv")
        mixed, mix_left = sem("mixed"), sem("mix_left")
        block = ctx.enter_context(nc.Block())
        NPAIR = HA // 2
        v_tiles = v_tm.rearrange("(t p) n -> p t n", p=P)
        q_tiles = q_tm[0:TP].rearrange("(t p) n -> p t n", p=P)
        k_tiles = k_tm.rearrange("(t p) n -> p t n", p=P)

        @block.sync
        def _(sp):
            for dst, name in ((ident, "ident"), (tri, "tri"), (ones, "ones"), (mask, "mask")):
                sp.dma_start(dst[:], consts[name]).then_inc(const_in, 16)
            sp.dma_start(biases[:], bias_dram.to_broadcast([P, HA])).then_inc(const_in, 16)
            with sp.Fori(0, NPAIR) as p:
                sp.wait_ge(turned, 4 * p)
                sp.dma_start(qk_in[:, 0, :, :], q_tiles[:, :, bass.ds(p * P, P)]).then_inc(qk_load, 16)
                sp.dma_start(qk_in[:, 1, :, :], k_tiles[:, :, bass.ds(p * P, P)]).then_inc(qk_load, 16)
                sp.wait_ge(v_held, p)
                sp.dma_start(v_in[:], v_tiles[:, :, bass.ds(p * P, P)]).then_inc(v_load, 16)
                sp.wait_ge(mixed, 4 * p + 2)
                sp.dma_start(gate[:], gate_fm[bass.ds(p * P, P), 0:TP]).then_inc(gate_load, 16)
            sp.wait_ge(mix_left, 16 * NPAIR + 16)

        @block.tensor
        def _(pe):
            pe.wait_ge(const_in, 80)
            with pe.Fori(0, NPAIR) as p:
                pe.wait_ge(qk_load, 32 * p + 32)
                for i in range(4):
                    pe.wait_ge(turn_read, 4 * p + i + 1)
                    for c in range(4):
                        mm = pe.transpose(turn[i % 2][:, c, :], qk_in[:, i // 2, 4 * (i % 2) + c, :], ident[:])
                    mm.then_inc(turned, 1)
                pe.wait_ge(turn_read, 4 * p + 6)
                pe.wait_ge(v_held, p + 1)
                for i in range(NSTEP + 3):
                    if i < NSTEP:
                        e, half, kb, lo = steps[i]
                        rows = slice(DA * e, DA * e + DA)
                        pe.wait_ge(w_done, NSTEP * p + i + 1)
                        diagonal = kb >= 4 * half
                        mm = pe.matmul(z[i % 4][:, lo:NQ], qk[rows, 1, kb * P:kb * P + P],
                                       qk[rows, 0, half * NQ + lo:(half + 1) * NQ], start=True, stop=True)
                        if diagonal:
                            mm = pe.matmul(z[i % 4][:, lo:lo + P], ident[:], mask[:], start=False, stop=True,
                                           skip_group_check=True)
                        mm.then_inc(logits, 1)
                    j = i - 2
                    if 0 <= j < NSTEP:
                        lo = steps[j][3]
                        pe.wait_ge(keep_done, NSTEP * p + j + 1)
                        mm = pe.matmul(z[j % 4][:, lo:NQ], tri[:], keep[:, j % 3, lo:NQ], start=False, stop=True,
                                       skip_group_check=True)
                        if not opens[j]:
                            before = steps[j - 1][3]
                            pe.wait_ge(carry_done, NSTEP * p + j)
                            mm = pe.matmul(z[j % 4][:, before:NQ], ones[:], carry[:, (j - 1) % 3, before:NQ],
                                           start=False, stop=True, skip_group_check=True)
                        mm.then_inc(summed, 1)
                    j = i - 3
                    if 0 <= j < NSTEP:
                        e, half, kb, lo = steps[j]
                        rows = slice(DA * e, DA * e + DA)
                        pe.wait_ge(w_done, NSTEP * p + (j + 1 + 4))
                        if opens[j]:
                            pe.wait_ge(mixed, 4 * p + run[j] + 1)
                        pe.matmul(o[run[j] % 2][rows, lo:NQ], v[:, kb, rows], w[:, j % 2, lo:NQ], start=opens[j],
                                  stop=closes[j], skip_group_check=True).then_inc(pv_done, 1)

        @block.scalar
        def _(act):
            load_exp_ln(nc)
            act.sem_inc(turn_read, 2)
            act.sem_inc(w_done, 4)
            with act.Fori(0, NPAIR) as p:
                for i in range(4):
                    act.wait_ge(turned, 4 * p + i + 1)
                    if i == 0:
                        act.wait_ge(pv_done, NSTEP * p)
                    nc.scalar.activation(qk[:, i // 2, 4 * (i % 2) * P:4 * (i % 2 + 1) * P].rearrange("p (c n) -> p c n", n=P),
                                         turn[i % 2][:], ACT.Copy, scale=DA ** -0.5 if i < 2 else 1.0).then_inc(turn_read, 1)
                act.wait_ge(bias_held, p + 1)
                for i in range(NSTEP + 2):
                    if i < NSTEP:
                        e, _, _, lo = steps[i]
                        at = soft[:, i % 2, lo:NQ]
                        act.wait_ge(logits, NSTEP * p + i + 1)
                        act.wait_ge(keep_done, NSTEP * p + i - 1) if i >= 2 else act.wait_ge(keep_done, NSTEP * p)
                        nc.scalar.activation(at, z[i % 4][:, lo:NQ], ACT.Abs, bias=bias[:, e:e + 1]).then_inc(abs_done, 1)
                        act.wait_ge(abs_done, NSTEP * p + i + 1)
                        nc.scalar.activation(at, at, ACT.Exp, scale=-1.0).then_inc(exp_done, 1)
                        act.wait_ge(exp_done, NSTEP * p + i + 1)
                        nc.scalar.activation(at, at, ACT.Ln, bias=1.0).then_inc(soft_done, 1)
                    j = i - 2
                    if j >= 0:
                        e, _, _, lo = steps[j]
                        act.wait_ge(summed, NSTEP * p + j + 1)
                        act.wait_ge(pv_done, NSTEP * p + max(0, j - 1))
                        nc.scalar.activation(w[:, j % 2, lo:NQ], z[j % 4][:, lo:NQ], ACT.Exp,
                                             bias=bias[:, e:e + 1]).then_inc(w_done, 1)
                act.wait_ge(mixed, 4 * p + 4 + 2)
                act.dma_start(mix_fm[bass.ds(p * P, P), 0:TP], mix[:]).then_inc(mix_left, 16)

        @block.vector
        def _(dve):
            dve.sem_inc(mixed, 2)
            dve.sem_inc(mix_left, 16)
            dve.wait_ge(const_in, 80)
            with dve.Fori(0, NPAIR) as p:
                dve.wait_ge(v_load, 16 * p + 16)
                dve.wait_ge(pv_done, NSTEP * p)
                dve.tensor_copy(v[:], v_in[:]).then_inc(v_held, 1)
                dve.wait_ge(w_done, NSTEP * p + 4)
                dve.tensor_copy(bias[:], biases[:, bass.ds(2 * p, 2)]).then_inc(bias_held, 1)
                dve.wait_ge(bias_held, p + 1)
                for i in range(NSTEP + 3):
                    if i < NSTEP:
                        e, half, kb, lo = steps[i]
                        dve.wait_ge(abs_done, NSTEP * p + i + 1)
                        dve.tensor_scalar(relu[:, i % 2, lo:NQ], z[i % 4][:, lo:NQ], bias[:, e:e + 1], 0.0,
                                          ALU.add, ALU.max).then_inc(relu_done, 1)
                        dve.wait_ge(relu_done, NSTEP * p + i + 1)
                        dve.wait_ge(soft_done, NSTEP * p + i + 1)
                        dve.wait_ge(summed, NSTEP * p + max(0, i - 2))
                        dve.scalar_tensor_tensor(keep[:, i % 3, lo:NQ], relu[:, i % 2, lo:NQ], -1.0, soft[:, i % 2, lo:NQ],
                                                 ALU.mult, ALU.subtract).then_inc(keep_done, 1)
                        dve.wait_ge(keep_done, NSTEP * p + i + 1)
                        dve.wait_ge(summed, NSTEP * p + max(0, i - 1))
                        if opens[i]:
                            dve.tensor_copy(carry[:, i % 3, lo:NQ], keep[:, i % 3, lo:NQ]).then_inc(carry_done, 1)
                        else:
                            before = steps[i - 1][3]
                            dve.wait_ge(carry_done, NSTEP * p + i)
                            if lo < before:
                                dve.tensor_copy(carry[:, i % 3, lo:before], keep[:, i % 3, lo:before])
                            dve.tensor_tensor(carry[:, i % 3, before:NQ], carry[:, (i - 1) % 3, before:NQ],
                                              keep[:, i % 3, before:NQ], ALU.add).then_inc(carry_done, 1)
                    j = i - 3
                    if j >= 0 and closes[j]:
                        e, half, _, _ = steps[j]
                        rows = slice(DA * e, DA * e + DA)
                        cols = slice(half * NQ, half * NQ + NQ)
                        dve.wait_ge(pv_done, NSTEP * p + j + 1)
                        if run[j] == 0:
                            dve.wait_ge(gate_load, 16 * p + 16)
                            dve.wait_ge(mix_left, 16 * p + 16)
                        dve.tensor_tensor(mix[rows, cols], o[run[j] % 2][rows, :], gate[rows, cols], ALU.mult).then_inc(mixed, 1)



def attend_samples(nc, q_tm, k_tm, v_tm, gate_fm, bias_dram, cache_k, cache_v, page_table, mix_fm, consts):
    with nc.cleanup_on_exit(), ExitStack() as ctx:
        sb = lambda n, s, d=F32: ctx.enter_context(nc.sbuf_tensor(f"as_{n}", s, d))
        sem = lambda n: nc.alloc_semaphore(f"as_{n}")
        ps = lambda n, s: ctx.enter_context(nc.psum_tensor(f"as_{n}", s, F32))
        HP = HA // 2
        NC_ = NPAGE * HA * LS
        z = [ps("z0", [P, NC_]), ps("z1", [P, NC_])]
        z_new = ps("z_new", [TS, HA * TS])
        turn = [ps("turn0", [P, HP, P]), ps("turn1", [P, HP, P])]
        o = [ps("o0", [P, HP, 2, LS]), ps("o1", [P, HP, 2, LS])]
        ident, tri, ones = sb("ident", [P, P]), sb("tri", [P, P]), sb("ones", [P, P])
        mask = sb("mask", [TS, TS])
        table = sb("table", [1, NS * NPAGE], I32)
        biases = sb("biases", [1, HA])
        bias_cols = sb("bias_cols", [1, NPAGE, HA, LS])
        qkv_in = sb("qkv_in", [TS, 3, WA])
        qT, kT_new = sb("qT", [P, HP, TS]), sb("kT_new", [P, HP, TS])
        q_bd = sb("q_bd", [P, HP, NS, 2, LS])
        gate = sb("gate", [P, HP, TS])
        mix = sb("mix", [P, HP, TS])
        k_page = [sb("k_page0", [P, NPAGE, WA]), sb("k_page1", [P, NPAGE, WA])]
        v_page = [sb("v_page0", [P, NPAGE, WA]), sb("v_page1", [P, NPAGE, WA])]
        kT = sb("kT", [P, 4, HP, P])
        soft, relu = sb("soft", [P, 2, NC_]), sb("relu", [P, 2, NC_])
        keep, w = sb("keep", [P, 2, NC_]), sb("w", [P, 2, NC_])
        carry = sb("carry", [P, 2, NC_])
        soft_n, relu_n = sb("soft_n", [TS, HA * TS]), sb("relu_n", [TS, HA * TS])
        keep_n, w_n = sb("keep_n", [TS, HA * TS]), sb("w_n", [TS, HA * TS])

        const_in, table_in = sem("const_in"), sem("table_in")
        k_in, v_in = [sem("k_in0"), sem("k_in1")], [sem("v_in0"), sem("v_in1")]
        prep = sem("prep")
        new_turned, new_held = sem("new_turned"), sem("new_held")
        new_logits, new_abs, new_soft = sem("new_logits"), sem("new_abs"), sem("new_soft")
        new_relu, new_keep, new_summed, new_w = sem("new_relu"), sem("new_keep"), sem("new_summed"), sem("new_w")
        turned = sem("turned")
        held_a, held_d = sem("held_a"), sem("held_d")
        page_logits = sem("page_logits")
        abs_done, exp_done, soft_done, relu_done = sem("abs"), sem("exp"), sem("soft"), sem("relu")
        keep_done, carry_step, summed = sem("keep"), sem("carry"), sem("summed")
        w_done, o_done, mixed, mix_left = sem("w"), sem("o"), sem("mixed"), sem("mix_left")
        block = ctx.enter_context(nc.Block())
        NCONST = 16 * 9
        caches = {"k": cache_k.rearrange("n t h d -> n t (h d)"), "v": cache_v.rearrange("n t h d -> n t (h d)")}
        n_pool = cache_k.shape[0]
        pairs = lambda x: x.rearrange("p (g h q) -> p g h q", h=HA, q=LS)
        new = lambda x: x.rearrange("k (h b q) -> k h b q", h=HA, b=NS)

        @block.sync
        def _(sp):
            sp.dma_start(table[:], page_table.rearrange("(a b) n -> a (b n)", a=1)).then_inc(table_in, 16)
            for dst, name in ((ident, "ident"), (tri, "tri"), (ones, "ones"), (mask, "mask_s")):
                sp.dma_start(dst[:], consts[name]).then_inc(const_in, 16)
            sp.dma_start(biases[:], bias_dram).then_inc(const_in, 16)
            for i, x in enumerate((q_tm[TP:T], k_tm, v_tm)):
                sp.dma_start(qkv_in[:, i, :], x).then_inc(const_in, 16)
            sp.dma_start(gate[:], gate_fm[:, TP:T].rearrange("(c p) t -> p c t", p=P)).then_inc(const_in, 16)
            sp.wait_ge(table_in, 16)
            with sp.Fori(0, NS // 2) as pair:
                for s in range(2):
                    b = 2 * pair + s
                    for g in range(NPAGE):
                        page = sp.value_load(table[0:1, bass.ds(b * NPAGE + g, 1)], min_val=0, max_val=n_pool - 1)
                        if g == 0:
                            sp.wait_ge(page_logits, NPAGE * 2 * pair + NPAGE * s + 1)
                        sp.dma_start(k_page[s][:, g, :], caches["k"][bass.ds(page, 1)].rearrange("a t n -> (a t) n")).then_inc(k_in[s], 16)
                        if g == 0:
                            sp.wait_ge(o_done, b + 1)
                        sp.dma_start(v_page[s][:, g, :], caches["v"][bass.ds(page, 1)].rearrange("a t n -> (a t) n")).then_inc(v_in[s], 16)
            sp.wait_ge(mixed, NS * 2 + 4)
            sp.dma_start(mix_fm[0:WA, TP:T].rearrange("(c p) t -> p c t", p=P), mix[:]).then_inc(mix_left, 16)
            sp.wait_ge(mix_left, 16)

        @block.tensor
        def _(pe):
            pe.sem_inc(page_logits, 2 * NPAGE - NPAGE + 1)
            pe.sem_inc(o_done, 2)
            pe.wait_ge(const_in, NCONST)
            for i in range(2):
                for c in range(HP):
                    mm = pe.transpose(turn[i][:, c, 0:TS], qkv_in[:, i, c * P:c * P + P], ident[0:TS, 0:TS])
                mm.then_inc(new_turned, 1)
            pe.wait_ge(new_held, 2)
            pe.wait_ge(prep, 3)
            pe.matmul(z_new[:], ident[0:TS, 0:TS], mask[:].unsqueeze(1).to_broadcast([TS, HA, TS]), start=True, stop=True)
            pe.matmul(z_new[:], ones[0:1, 0:TS], bias_cols[0:1, :, :, :].rearrange("o g h q -> o h g q"), start=False, stop=True, skip_group_check=True)
            for c in range(HP):
                out = z_new[:, 2 * c * TS:2 * (c + 1) * TS].rearrange("k (e b q) -> k b e q", e=2, b=NS)
                mm = pe.matmul(out, kT_new[:, c, :], q_bd[:, c, :, :, :], start=False, stop=True, skip_group_check=True)
            mm.then_inc(new_logits, 1)
            pe.wait_ge(new_keep, 1)
            pe.matmul(z_new[:], tri[0:TS, 0:TS], keep_n[:], start=False, stop=True, skip_group_check=True).then_inc(new_summed, 1)
            pe.wait_ge(new_w, 1)

            with pe.Fori(0, NS // 2) as pair:
                for s in range(2):
                    b = 2 * pair + s
                    pe.wait_ge(k_in[s], 16 * NPAGE * pair + 16 * NPAGE)
                    pe.wait_ge(w_done, b + 1)
                    pe.matmul(z[s][:], ones[0:1, :], bias_cols[0:1, :, :, :].rearrange("o g h q -> o (g h q)"), start=True, stop=True)
                    for g in range(NPAGE + 1):
                        if g < NPAGE:
                            pe.wait_ge(held_a if g % 2 == 0 else held_d, 4 * b + g // 2 + 1)
                            for c in range(HP):
                                mm = pe.transpose(turn[g % 2][:, c, :], k_page[s][:, g, c * P:c * P + P], ident[:])
                            mm.then_inc(turned, 1)
                        if g >= 1:
                            f = g - 1
                            pe.wait_ge(held_a if f % 2 == 0 else held_d, 4 * b + f // 2 + 2)
                            for c in range(HP):
                                mm = pe.matmul(z[s][:, f * 64 + c * 16:f * 64 + c * 16 + 16], kT[:, f % 4, c, :],
                                               q_bd[:, c, bass.ds(b, 1), :, :].rearrange("p a e q -> p (a e q)"), start=False, stop=True, skip_group_check=True)
                            mm.then_inc(page_logits, 1)
                for s in range(2):
                    b = 2 * pair + s
                    mine = new(keep_n[:])[:, :, bass.ds(b, 1), :].rearrange("k h a q -> k (a h) q")
                    pe.wait_ge(keep_done, b + 1)
                    pe.matmul(z[s][:], tri[:], keep[:, s, :], start=False, stop=True, skip_group_check=True)
                    pe.matmul(z[s][:], ones[0:TS, :], mine.unsqueeze(1).to_broadcast([TS, NPAGE, HA, LS]),
                              start=False, stop=True, skip_group_check=True)
                    pe.wait_ge(carry_step, (NPAGE - 1) * (b + 1))
                    pe.matmul(z[s][:, 0:NC_ - 64], ones[:], carry[:, s, 0:NC_ - 64], start=False, stop=True,
                              skip_group_check=True).then_inc(summed, 1)
                    pe.wait_ge(v_in[s], 16 * NPAGE * pair + 16 * NPAGE)
                    pe.wait_ge(w_done, b + 3)
                    pe.wait_ge(mixed, 2 * b + 2)
                    for g in range(NPAGE + 1):
                        for c in range(HP):
                            if g < NPAGE:
                                l, r = v_page[s][:, g, c * P:c * P + P], w[:, s, g * 64 + c * 16:g * 64 + c * 16 + 16]
                            else:
                                l = qkv_in[:, 2, c * P:c * P + P]
                                r = new(w_n[:])[:, 2 * c:2 * c + 2, bass.ds(b, 1), :].rearrange("k h a q -> k (a h) q")
                            mm = pe.matmul(o[s][:, c, :, :], l, r, start=(g == 0 and c == 0), stop=(g == NPAGE), skip_group_check=True)
                    mm.then_inc(o_done, 1)

        @block.scalar
        def _(act):
            load_exp_ln(nc)
            act.sem_inc(held_a, 1)
            act.sem_inc(w_done, 2)
            for i, dst in enumerate((qT, kT_new)):
                act.wait_ge(new_turned, i + 1)
                nc.scalar.activation(dst[:], turn[i][:, :, 0:TS], ACT.Copy, scale=DA ** -0.5 if i == 0 else 1.0).then_inc(new_held, 1)
            act.wait_ge(new_logits, 1)
            nc.scalar.activation(soft_n[:], z_new[:], ACT.Abs).then_inc(new_abs, 1)
            act.wait_ge(new_abs, 1)
            nc.scalar.activation(soft_n[:], soft_n[:], ACT.Exp, scale=-1.0).then_inc(new_abs, 1)
            act.wait_ge(new_abs, 2)
            nc.scalar.activation(soft_n[:], soft_n[:], ACT.Ln, bias=1.0).then_inc(new_soft, 1)
            act.wait_ge(new_summed, 1)
            nc.scalar.activation(w_n[:], z_new[:], ACT.Exp).then_inc(new_w, 1)

            with act.Fori(0, NS // 2) as pair:
                for s in range(2):
                    b = 2 * pair + s
                    for g in range(0, NPAGE, 2):
                        act.wait_ge(turned, NPAGE * b + g + 1)
                        act.wait_ge(page_logits, NPAGE * b + (g + 1 + NPAGE + 1 - 4))
                        nc.scalar.copy(kT[:, g % 4, :, :], turn[0][:]).then_inc(held_a, 1)
                    act.wait_ge(page_logits, NPAGE * b + (2 * NPAGE + 1))
                    act.wait_ge(keep_done, 2 * pair)
                    at = soft[:, s, :]
                    nc.scalar.activation(at, z[s][:], ACT.Abs).then_inc(abs_done, 1)
                    act.wait_ge(abs_done, b + 1)
                    nc.scalar.activation(at, at, ACT.Exp, scale=-1.0).then_inc(exp_done, 1)
                    act.wait_ge(exp_done, b + 1)
                    nc.scalar.activation(at, at, ACT.Ln, bias=1.0).then_inc(soft_done, 1)
                for s in range(2):
                    b = 2 * pair + s
                    act.wait_ge(summed, b + 1)
                    act.wait_ge(o_done, b + 1)
                    nc.scalar.activation(w[:, s, :], z[s][:], ACT.Exp).then_inc(w_done, 1)

        @block.vector
        def _(dve):
            dve.sem_inc(held_d, 1)
            dve.sem_inc(mixed, 4)
            dve.wait_ge(const_in, NCONST)
            dve.tensor_copy(bias_cols[:], biases[:].unsqueeze(1).unsqueeze(3).to_broadcast([1, NPAGE, HA, LS])).then_inc(prep, 1)
            nc.vector.memset(q_bd[:], 0.0).then_inc(prep, 1)
            dve.wait_ge(prep, 2)
            dve.wait_ge(new_held, 1)
            for e in range(2):
                rows = slice(DA * e, DA * e + DA)
                ins = dve.tensor_copy(q_bd[rows, :, :, e, :], qT[rows, :, :].rearrange("p c (b q) -> p c b q", b=NS))
            ins.then_inc(prep, 1)
            dve.wait_ge(new_abs, 1)
            dve.tensor_scalar(relu_n[:], z_new[:], 0.0, None, ALU.max).then_inc(new_relu, 1)
            dve.wait_ge(new_relu, 1)
            dve.wait_ge(new_soft, 1)
            dve.scalar_tensor_tensor(keep_n[:], relu_n[:], -1.0, soft_n[:], ALU.mult, ALU.subtract).then_inc(new_keep, 1)

            with dve.Fori(0, NS // 2) as pair:
                for s in range(2):
                    b = 2 * pair + s
                    for g in range(1, NPAGE, 2):
                        dve.wait_ge(turned, NPAGE * b + g + 1)
                        dve.wait_ge(page_logits, NPAGE * b + (g + 1 + NPAGE + 1 - 4))
                        dve.tensor_copy(kT[:, g % 4, :, :], turn[1][:]).then_inc(held_d, 1)
                    dve.wait_ge(abs_done, b + 1)
                    dve.tensor_scalar(relu[:, s, :], z[s][:], 0.0, None, ALU.max).then_inc(relu_done, 1)
                    dve.wait_ge(relu_done, b + 1)
                    dve.wait_ge(soft_done, b + 1)
                    dve.wait_ge(summed, 2 * pair)
                    dve.scalar_tensor_tensor(keep[:, s, :], relu[:, s, :], -1.0, soft[:, s, :], ALU.mult, ALU.subtract).then_inc(keep_done, 1)
                    dve.wait_ge(keep_done, b + 1)
                    cols = lambda g: slice(g * 64, g * 64 + 64)
                    dve.tensor_copy(carry[:, s, cols(NPAGE - 2)], keep[:, s, cols(NPAGE - 1)]).then_inc(carry_step, 1)
                    for n, g in enumerate(range(NPAGE - 3, -1, -1)):
                        dve.wait_ge(carry_step, (NPAGE - 1) * b + n + 1)
                        dve.tensor_tensor(carry[:, s, cols(g)], carry[:, s, cols(g + 1)], keep[:, s, cols(g + 1)], ALU.add).then_inc(carry_step, 1)
                for s in range(2):
                    b = 2 * pair + s
                    dve.wait_ge(o_done, b + 3)
                    for e in range(2):
                        rows = slice(DA * e, DA * e + DA)
                        dve.tensor_tensor(mix[rows, :, bass.ds(b * LS, LS)], o[s][rows, :, e, :], gate[rows, :, bass.ds(b * LS, LS)],
                                          ALU.mult).then_inc(mixed, 1)



def hgrn(nc, q_fm, f_fm, v_tm, gate_fm, bounds, out_gain, state_in, state_prompt, state_samples, mix_fm, consts):
    with nc.cleanup_on_exit(), ExitStack() as ctx:
        sb = lambda n, s, d=F32: ctx.enter_context(nc.sbuf_tensor(f"hg_{n}", s, d))
        sem = lambda n: nc.alloc_semaphore(f"hg_{n}")
        ps = lambda n, s: ctx.enter_context(nc.psum_tensor(f"hg_{n}", s, F32))
        NL, NCH, NG = 7, TP // P, 2
        sc = [ps(f"sc{i}", [P, 4, P]) for i in range(4)]
        sx = ps("sx", [P, TS])
        ku = ps("ku", [P, 4, P])
        o = [ps("o0", [P, 4, P]), ps("o1", [P, 4, P])]

        ident, ones = sb("ident", [P, P]), sb("ones", [P, P])
        level_mask = sb("level_mask", [P, NL + 1, P], I32)
        own = sb("own", [TS, NS])
        reset = sb("reset", [P, T])
        ab = sb("ab", [P, 2, HB])
        diff, lb, om = sb("diff", [P, HB]), sb("lb", [P, HB]), sb("om", [P, HB])
        gain, eps = sb("gain", [P, 1]), sb("eps", [P, 1])
        q = [sb("q0", [P, T]), sb("q1", [P, T])]
        f = [sb("f0", [P, T]), sb("f1", [P, T])]
        v = [sb("v0", [P, NT, P]), sb("v1", [P, NT, P])]
        gate = [sb("gate0", [P, T]), sb("gate1", [P, T])]
        s0 = [sb("s00", [P, NS, P]), sb("s01", [P, NS, P])]
        nf, sf, logf = sb("nf", [P, T]), sb("sf", [P, T]), sb("logf", [P, T])
        k, b = sb("k", [P, T]), sb("b", [P, T])
        x = [sb("x0", [P, T]), sb("x1", [P, T])]
        scores, scores_s = sb("scores", [P, NCH, P]), sb("scores_s", [TS, TS])
        eb, tail = sb("eb", [P, T]), sb("tail", [P, T])
        qd, kd = sb("qd", [P, T]), sb("kd", [P, T])
        kd_tm = sb("kd_tm", [P, NT, P])
        state = sb("state", [P, NCH + 1, P])
        vx = sb("vx", [TS, NS, P])
        s1, s_dec = sb("s1", [P, NS, P]), sb("s_dec", [P, NS, P])
        sq, rs = sb("sq", [P, 4 * P]), sb("rs", [P, 4 * P])
        on, mix = sb("on", [P, 4 * P]), sb("mix", [P, T])

        const_in, prep = sem("const_in"), sem("prep")
        pool_go, dve_go, pe_go = sem("pool_go"), sem("dve_go"), sem("pe_go")
        q_in, f_in, v_in, gate_in, s0_in = ([sem(f"{n}{i}") for i in range(2)] for n in ("q_in", "f_in", "v_in", "g_in", "s_in"))
        sig_done, k_done, logf_done, b_done = sem("sig"), sem("k"), sem("logf"), sem("b")
        exponents, weights, weighted = sem("exponents"), sem("weights"), sem("weighted")
        scored, scored_s, picked, picked_s = sem("scored"), sem("scored_s"), sem("picked"), sem("picked_s")
        eb_done, tail_diff, tail_exp, qd_done, kd_done = sem("eb"), sem("tail_diff"), sem("tail_exp"), sem("qd"), sem("kd")
        turned, held, updates, updates_s, state_done = sem("turned"), sem("held"), sem("updates"), sem("updates_s"), sem("state")
        vx_done, s1_done, s_left = sem("vx"), sem("s1"), sem("s_left")
        o_done, sq_done, sum_done, ln_done, rs_done, on_done, mixed = (
            sem("o"), sem("sq"), sem("sum"), sem("ln"), sem("rs"), sem("on"), sem("mixed"))
        mix_left, state_left = sem("mix_left"), sem("state_left")
        block = ctx.enter_context(nc.Block())
        NCONST = 16 * 7

        def halves(t, l):
            m = P // 2 >> l
            n = T if 2 * m <= LS else TP
            return t[:, 0:n].rearrange("p (c two m) -> p c two m", two=2, m=m)

        def chunks(t):
            return t[:, 0:TP].rearrange("p (c n) -> p c n", n=P), t[:, TP:T].rearrange("p (c n) -> p c n", n=LS)

        @block.sync
        def _(sp):
            for dst, src in ((ident[:], consts["ident"]), (ones[:], consts["ones"]), (level_mask[:], consts["level_mask"]),
                             (own[:], consts["own"]), (reset[:], consts["reset"])):
                sp.dma_start(dst, src).then_inc(const_in, 16)
            sp.dma_start(ab[:], bounds.rearrange("e (h k) -> k e h", k=P), allow_slow_non_contiguous=True).then_inc(const_in, 16)
            sp.dma_start(gain[:], out_gain.rearrange("(k a) -> k a", a=1), allow_slow_non_contiguous=True).then_inc(const_in, 16)
            with sp.Fori(0, HB // 2) as pair:
                for s in range(2):
                    h = 2 * pair + s
                    rows = bass.ds(h * P, P)
                    sp.wait_ge(mixed, 3 * h + 1)
                    sp.wait_ge(s1_done, 2 * h + 1)
                    sp.dma_start(f[s][:], f_fm[rows, :]).then_inc(f_in[s], 16)
                    sp.dma_start(q[s][:], q_fm[rows, :]).then_inc(q_in[s], 16)
                    sp.dma_start(v[s][:, 0:NT - 1, :], v_tm[0:TP, rows].rearrange("(c p) n -> p c n", p=P)).then_inc(v_in[s], 16)
                    sp.dma_start(v[s][0:TS, NT - 1, :], v_tm[TP:T, rows]).then_inc(v_in[s], 16)
                    sp.dma_start(s0[s][:], state_in[:, bass.ds(h, 1)].rearrange("b a k v -> k (a b) v")).then_inc(s0_in[s], 16)
                    sp.dma_start(gate[s][:], gate_fm[rows, :]).then_inc(gate_in[s], 16)

        @block.gpsimd
        def _(pool):
            with pool.Fori(0, HB // 2) as pair:
                for s in range(2):
                    h = 2 * pair + s
                    pool.wait_ge(b_done, h + 1)
                    for l in range(NL):
                        bb, xx = halves(b, l), halves(x[l % 2], l)
                        shape = [P, bb.shape[1], bb.shape[3]]
                        r = bb[:, :, 0, bb.shape[3] - 1:].to_broadcast(shape)
                        pool.wait_ge(scored, (NL + 1) * h + (l + 1))
                        pool.sem_inc(pool_go, 1)
                        nc.gpsimd.tensor_tensor(xx[:, :, 0, :], r, bb[:, :, 0, :], ALU.subtract)
                        nc.gpsimd.tensor_tensor(xx[:, :, 1, :], bb[:, :, 1, :], r, ALU.subtract).then_inc(exponents, 1)

        @block.scalar
        def _(act):
            act.wait_ge(prep, 2)
            nc.scalar.activation(lb[:], diff[:], ACT.Sigmoid).then_inc(prep, 1)
            nc.scalar.activation(om[:], diff[:], ACT.Sigmoid, scale=-1.0).then_inc(prep, 1)
            act.wait_ge(prep, 4)
            with act.Fori(0, HB // 2) as pair:
                for s in range(2):
                    h = 2 * pair + s
                    act.wait_ge(f_in[s], 16 * pair + 16)
                    act.wait_ge(k_done, h)
                    nc.scalar.activation(nf[:], f[s][:], ACT.Sigmoid, scale=-1.0).then_inc(sig_done, 1)
                    nc.scalar.activation(sf[:], f[s][:], ACT.Sigmoid).then_inc(sig_done, 1)
                    load_exp_ln(nc)
                    act.wait_ge(sig_done, 2 * h + 2)
                    act.wait_ge(b_done, h)
                    nc.scalar.activation(logf[:], sf[:], ACT.Ln, scale=om[:, bass.ds(h, 1)], bias=lb[:, bass.ds(h, 1)]).then_inc(logf_done, 1)
                    for l in range(NL):
                        n = T if P >> l <= LS else TP
                        act.wait_ge(exponents, NL * h + l + 1)
                        nc.scalar.activation(x[l % 2][:, 0:n], x[l % 2][:, 0:n], ACT.Exp).then_inc(weights, 1)
                    act.wait_ge(b_done, h + 1)
                    act.wait_ge(s1_done, 2 * h + 2)
                    nc.scalar.activation(eb[:], b[:], ACT.Exp).then_inc(eb_done, 1)
                    act.wait_ge(tail_diff, h + 1)
                    nc.scalar.activation(tail[:], tail[:], ACT.Exp).then_inc(tail_exp, 1)
                    for g in range(NG + 1):
                        act.wait_ge(turned, 3 * h + g + 1)
                        if g == 0:
                            act.wait_ge(updates_s, h)
                        if g < NG:
                            nc.scalar.copy(kd_tm[:, 4 * g:4 * g + 4, :], ku[:]).then_inc(held, 1)
                        else:
                            nc.scalar.copy(kd_tm[0:TS, NT - 1, :], ku[0:TS, 0, :]).then_inc(held, 1)
                    for g in range(NG + 1):
                        src, n = (o[g][:].rearrange("p c n -> p (c n)"), 4 * P) if g < NG else (sx[:], TS)
                        ss = ku[:].rearrange("p c n -> p (c n)")[:, 0:n]
                        act.wait_ge(o_done, 3 * h + g + 1)
                        act.wait_ge(sum_done, 3 * h + g)
                        nc.scalar.activation(sq[:, 0:n], src, ACT.Square).then_inc(sq_done, 1)
                        act.wait_ge(sum_done, 3 * h + g + 1)
                        act.wait_ge(on_done, 3 * h + g)
                        nc.scalar.activation(rs[:, 0:n], ss, ACT.Ln, scale=1.0 / DB, bias=eps[:]).then_inc(ln_done, 1)
                        act.wait_ge(ln_done, 3 * h + g + 1)
                        nc.scalar.activation(rs[:, 0:n], rs[:, 0:n], ACT.Exp, scale=-0.5).then_inc(rs_done, 1)
                    act.wait_ge(mixed, 3 * h + 4)
                    act.dma_start(mix_fm[bass.ds(WA + h * P, P), :], mix[:]).then_inc(mix_left, 16)
                    act.wait_ge(state_done, NCH * h + NCH)
                    act.dma_start(state_prompt[bass.ds(h, 1)].rearrange("a k v -> (a k) v"), state[:, NCH, :]).then_inc(state_left, 16)
                    act.wait_ge(s1_done, 2 * h + 4)
                    act.dma_start(state_samples[:, bass.ds(h, 1)].rearrange("b a k v -> k (a b) v"), s1[:]).then_inc(s_left, 16)
            act.wait_ge(mix_left, 16 * HB)
            act.wait_ge(state_left, 16 * HB)
            act.wait_ge(s_left, 16 * HB)

        @block.vector
        def _(dve):
            dve.sem_inc(mixed, 1)
            dve.sem_inc(s1_done, 2)
            dve.wait_ge(const_in, NCONST)
            dve.tensor_tensor(diff[:], ab[:, 0, :], ab[:, 1, :], ALU.subtract).then_inc(prep, 1)
            nc.vector.memset(eps[:], EPS).then_inc(prep, 1)
            nc.vector.memset(scores[:], 0.0).then_inc(picked, 1)
            nc.vector.memset(scores_s[:], 0.0).then_inc(picked_s, 1)
            dve.wait_ge(prep, 4)
            dve.wait_ge(picked, 1)
            dve.wait_ge(picked_s, 1)
            with dve.Fori(0, HB // 2) as pair:
                for s in range(2):
                    h = 2 * pair + s
                    dve.wait_ge(sig_done, 2 * h + 1)
                    dve.wait_ge(kd_done, h)
                    dve.tensor_scalar(k[:], nf[:], om[:, bass.ds(h, 1)], None, ALU.mult).then_inc(k_done, 1)
                    dve.wait_ge(logf_done, h + 1)
                    dve.wait_ge(tail_exp, h)
                    dve.tensor_tensor_scan(b[:], reset[:], logf[:], 0.0, ALU.mult, ALU.add).then_inc(b_done, 1)
                    dve.wait_ge(q_in[s], 16 * pair + 16)
                    dve.wait_ge(k_done, h + 1)

                    def pick(l):
                        mask = level_mask[:, l, :].unsqueeze(1).to_broadcast([P, 4, P])
                        dve.wait_ge(scored, (NL + 1) * h + l + 1 + 2)
                        dve.wait_ge(picked, (NL + 1) * h + l + 1)
                        dve.sem_inc(dve_go, 1)
                        for g in range(NG):
                            ins = dve.copy_predicated(scores[:, 4 * g:4 * g + 4, :], mask, sc[2 * (l % 2) + g][:])
                        ins.then_inc(picked, 1)
                        if l >= 4:
                            dve.wait_ge(scored_s, 4 * h + l - 3)
                            dve.wait_ge(picked_s, 4 * h + l - 3)
                            dve.sem_inc(dve_go, 1)
                            dve.copy_predicated(scores_s[:], level_mask[0:TS, l, 0:TS], sx[0:TS, :]).then_inc(picked_s, 1)

                    for l in range(NL):
                        xx = halves(x[l % 2], l)
                        dve.wait_ge(weights, NL * h + l + 1)
                        dve.tensor_tensor(xx[:, :, 0, :], xx[:, :, 0, :], halves(k, l)[:, :, 0, :], ALU.mult)
                        dve.tensor_tensor(xx[:, :, 1, :], xx[:, :, 1, :], halves(q[s], l)[:, :, 1, :], ALU.mult).then_inc(weighted, 1)
                        if l == 0:
                            dve.wait_ge(o_done, 3 * h)
                        if l >= 1:
                            pick(l - 1)
                    pick(NL - 1)
                    dve.wait_ge(b_done, h + 1)
                    dve.wait_ge(kd_done, h)
                    for bb, tt, n in zip(chunks(b), chunks(tail), (P, LS)):
                        ins = dve.tensor_tensor(tt, bb[:, :, n - 1:].to_broadcast([P, bb.shape[1], n]), bb, ALU.subtract)
                    ins.then_inc(tail_diff, 1)
                    pick(NL)
                    dve.wait_ge(eb_done, h + 1)
                    dve.tensor_tensor(qd[:], q[s][:], eb[:], ALU.mult).then_inc(qd_done, 1)
                    dve.wait_ge(tail_exp, h + 1)
                    dve.wait_ge(turned, 3 * h)
                    dve.tensor_tensor(kd[:], k[:], tail[:], ALU.mult).then_inc(kd_done, 1)
                    dve.wait_ge(state_left, 16 * h)
                    for c in range(NCH):
                        u = sc[c // 4][:, c % 4, :]
                        if c % 4 == 0:
                            dve.wait_ge(updates, 2 * h + c // 4 + 1)
                        if c == 0:
                            dve.tensor_copy(state[:, 1, :], u).then_inc(state_done, 1)
                        else:
                            dve.wait_ge(state_done, NCH * h + c)
                            dve.scalar_tensor_tensor(state[:, c + 1, :], state[:, c, :], eb[:, c * P + P - 1:c * P + P], u,
                                                     ALU.mult, ALU.add).then_inc(state_done, 1)
                    dve.wait_ge(v_in[s], 32 * pair + 32)
                    dve.wait_ge(updates_s, h)
                    dve.tensor_tensor(vx[:], v[s][0:TS, NT - 1, :].unsqueeze(1).to_broadcast([TS, NS, P]),
                                      own[:].unsqueeze(2).to_broadcast([TS, NS, P]), ALU.mult).then_inc(vx_done, 1)
                    dve.wait_ge(s0_in[s], 16 * pair + 16)
                    ends = chunks(eb)[1][:, :, LS - 1:].to_broadcast([P, NS, P])
                    dve.wait_ge(s_left, 16 * h)
                    dve.tensor_tensor(s_dec[:], s0[s][:], ends, ALU.mult).then_inc(s1_done, 1)
                    dve.wait_ge(s1_done, 2 * h + 3)
                    dve.wait_ge(updates_s, h + 1)
                    for g in range(NG):
                        ins = dve.tensor_tensor(s1[:, 4 * g:4 * g + 4, :], s_dec[:, 4 * g:4 * g + 4, :], sc[2 + g][:], ALU.add)
                    ins.then_inc(s1_done, 1)
                    dve.wait_ge(gate_in[s], 16 * pair + 16)
                    dve.wait_ge(mix_left, 16 * h)
                    for g in range(NG + 1):
                        src, n = (o[g][:].rearrange("p c n -> p (c n)"), 4 * P) if g < NG else (sx[:], TS)
                        at = slice(4 * P * g, 4 * P * g + n)
                        dve.wait_ge(rs_done, 3 * h + g + 1)
                        dve.wait_ge(mixed, 3 * h + g + 1)
                        dve.tensor_tensor(on[:, 0:n], src, rs[:, 0:n], ALU.mult).then_inc(on_done, 1)
                        dve.wait_ge(on_done, 3 * h + g + 1)
                        dve.scalar_tensor_tensor(mix[:, at], on[:, 0:n], gain[:, 0:1], gate[s][:, at], ALU.mult, ALU.mult).then_inc(mixed, 1)

        @block.tensor
        def _(pe):
            pe.sem_inc(scored, 2)
            pe.wait_ge(const_in, NCONST)
            with pe.Fori(0, HB // 2) as pair:
                for s in range(2):
                    h = 2 * pair + s
                    pe.wait_ge(mixed, 3 * h + 1)
                    pe.wait_ge(s1_done, 2 * h + 2)
                    for l in range(NL + 1):
                        if l < NL:
                            pe.wait_ge(weighted, NL * h + l + 1)
                        pe.wait_ge(picked, (NL + 1) * h + max(1, l))
                        xl = x[l % 2]
                        for c in range(NCH + (l >= 4)):
                            tok = slice(c * P, c * P + (P if c < NCH else TS))
                            lhs, rhs = (xl, xl) if l < NL else (k, q[s])
                            if c < NCH:
                                mm = pe.matmul(sc[2 * (l % 2) + c // 4][:, c % 4, :], lhs[:, tok], rhs[:, tok], start=True, stop=True)
                                if c == NCH - 1:
                                    mm.then_inc(scored, 1) if l < 4 else None
                            else:
                                pe.wait_ge(picked_s, 4 * h + l - 3)
                                pe.matmul(sx[0:TS, :], lhs[:, tok], rhs[:, tok], start=True, stop=True).then_inc(scored_s, 1)
                        if l >= 4:
                            pe.wait_ge(scored_s, 4 * h + l - 3)
                            pe.sem_inc(scored, 1)
                    pe.wait_ge(kd_done, h + 1)
                    for g in range(NG + 1):
                        if g:
                            pe.wait_ge(held, 3 * h + g)
                            pe.sem_inc(pe_go, 1)
                        for c in range(4 if g < NG else 1):
                            n = P if g < NG else TS
                            at = 4 * g * P + c * P
                            mm = pe.transpose(ku[0:n, c, :], kd[:, at:at + n], ident[:])
                        mm.then_inc(turned, 1)
                    pe.wait_ge(v_in[s], 32 * pair + 32)
                    pe.wait_ge(picked, (NL + 1) * h + NL + 2)
                    for g in range(NG):
                        pe.wait_ge(held, 3 * h + g + 1)
                        for c in range(4):
                            mm = pe.matmul(sc[g][:, c, :], kd_tm[:, 4 * g + c, :], v[s][:, 4 * g + c, :], start=True, stop=True)
                        mm.then_inc(updates, 1)
                    pe.wait_ge(held, 3 * h + 3)
                    pe.wait_ge(vx_done, h + 1)
                    for g in range(NG):
                        mm = pe.matmul(sc[2 + g][:], kd_tm[0:TS, NT - 1, :], vx[:, 4 * g:4 * g + 4, :], start=True, stop=True)
                    mm.then_inc(updates_s, 1)
                    pe.wait_ge(qd_done, h + 1)
                    pe.wait_ge(s0_in[s], 16 * pair + 16)
                    for c in range(NCH):
                        tok = slice(c * P, c * P + P)
                        mm = pe.matmul(o[c // 4][:, c % 4, :], v[s][:, c, :], scores[:, c, :], start=True, stop=True)
                        if c:
                            pe.wait_ge(state_done, NCH * h + c)
                            mm = pe.matmul(o[c // 4][:, c % 4, :], state[:, c, :], qd[:, tok], start=False, stop=True, skip_group_check=True)
                        if c % 4 == 3:
                            mm.then_inc(o_done, 1)
                    pe.wait_ge(picked_s, 4 * h + 5)
                    pe.matmul(sx[:], v[s][0:TS, NT - 1, :], scores_s[:], start=True, stop=True)
                    for c in range(NS):
                        mm = pe.matmul(sx[:, c * LS:c * LS + LS], s0[s][:, c, :], qd[:, TP + c * LS:TP + c * LS + LS],
                                       start=False, stop=True, skip_group_check=True)
                    mm.then_inc(o_done, 1)
                    for g in range(NG + 1):
                        n = 4 * P if g < NG else TS
                        pe.wait_ge(sq_done, 3 * h + g + 1)
                        if g:
                            pe.wait_ge(ln_done, 3 * h + g)
                        pe.matmul(ku[:].rearrange("p c n -> p (c n)")[:, 0:n], ones[:], sq[:, 0:n], start=True, stop=True).then_inc(sum_done, 1)



def project_out(nc, tag, mix_fm, weight, x_of, y_of, consts):
    with nc.cleanup_on_exit(), ExitStack() as ctx:
        sb = lambda n, s, d=F32: ctx.enter_context(nc.sbuf_tensor(f"{tag}_{n}", s, d))
        sem = lambda n: nc.alloc_semaphore(f"{tag}_{n}")
        K, NH = weight.shape[0] // P, D // 512
        bank = [[ctx.enter_context(nc.psum_tensor(f"{tag}_bank{s}{n}", [P, 512], F32)) for n in range(NH)] for s in range(2)]
        raw = sb("raw", [P, 2, D])
        w_hi, w_lo = sb("w_hi", [P, K, D], F32R), sb("w_lo", [P, K, D], F32R)
        mix = sb("mix", [P, 2, K, P])
        m_hi, m_lo = sb("m_hi", [P, 2, K, P], F32R), sb("m_lo", [P, 2, K, P], F32R)
        x, y = sb("x", [P, 2, D]), sb("y", [P, 2, D])
        raw_in, mix_in, x_in = ([sem(f"{n}{i}") for i in range(2)] for n in ("raw", "mix", "x"))
        w_hi_done, w_split, m_hi_done, m_split = sem("w_hi"), sem("w_split"), sem("m_hi"), sem("m_split")
        full, added, y_left = sem("full"), sem("added"), sem("y_left")
        block = ctx.enter_context(nc.Block())
        w_rows = weight.rearrange("(c p) n -> p c n", p=P)
        mix_cols = mix_fm.rearrange("(c p) t -> p c t", p=P)

        def tiles(engine, step):
            with engine.Fori(0, (NT - 1) // 2) as it:
                for slot in range(2):
                    step(2 * it + slot, slot, P, it)
            step(NT - 1, 0, TS, (NT - 1) // 2)

        @block.sync
        def _(sp):
            def load(t, slot, r, turn):
                sp.wait_ge(m_split, t + 1)
                sp.dma_start(mix[:, slot, :, 0:r], mix_cols[:, :, bass.ds(t * P, r)]).then_inc(mix_in[slot], 16)
                sp.wait_ge(added, t + 1)
                sp.dma_start(x[0:r, slot, :], x_of(t)).then_inc(x_in[slot], 16)
            tiles(sp, load)

        @block.gpsimd
        def _(pool):
            for c in range(K + 1):
                if c < K:
                    if c >= 2:
                        pool.wait_ge(w_split, c - 1)
                    pool.dma_start(raw[:, c % 2, :], w_rows[:, c, :]).then_inc(raw_in[c % 2], 16)
                if c >= 1:
                    r, hi = raw[:, (c - 1) % 2, :], w_hi[:, c - 1, :]
                    pool.wait_ge(raw_in[(c - 1) % 2], 16 * ((c - 1) // 2) + 16)
                    nc.gpsimd.tensor_copy(hi, r).then_inc(w_hi_done, 1)
                    pool.wait_ge(w_hi_done, c)
                    nc.gpsimd.tensor_tensor(w_lo[:, c - 1, :], r, hi.bitcast(F32), ALU.subtract).then_inc(w_split, 1)

        @block.tensor
        def _(pe):
            def product(t, slot, r, turn):
                pe.wait_ge(m_split, t + 3)
                pe.wait_ge(added, t + 1)
                for c in range(K):
                    pe.wait_ge(w_split, c + 1)
                    hi, lo = m_hi[:, slot, c, 0:r], m_lo[:, slot, c, 0:r]
                    for j, (m, w) in enumerate(((hi, w_hi), (hi, w_lo), (lo, w_hi))):
                        for n in range(NH):
                            mm = pe.matmul(bank[slot][n][0:r, :], m, w[:, c, n * 512:n * 512 + 512],
                                           start=(c == 0 and j == 0), stop=(c == K - 1 and j == 2))
                mm.then_inc(full, 1)
            tiles(pe, product)

        @block.scalar
        def _(act):
            def split_hi(t, slot, r, turn):
                act.wait_ge(mix_in[slot], 16 * turn + 16)
                act.wait_ge(full, t + 1)
                nc.scalar.copy(m_hi[:, slot, :, 0:r], mix[:, slot, :, 0:r]).then_inc(m_hi_done, 1)

            def store(t, slot, r, turn):
                act.wait_ge(added, t + 3)
                act.dma_start(y_of(t), y[0:r, slot, :]).then_inc(y_left, 16)

            act.sem_inc(full, 2)
            split_hi(0, 0, P, 0)
            split_hi(1, 1, P, 0)
            with act.Fori(0, (NT - 1) // 2 - 1) as it:
                for slot in range(2):
                    split_hi(2 * it + slot + 2, slot, P, it + 1)
                    store(2 * it + slot, slot, P, it)
            split_hi(NT - 1, 0, TS, (NT - 1) // 2)
            store(NT - 3, 0, P, (NT - 3) // 2)
            store(NT - 2, 1, P, (NT - 3) // 2)
            store(NT - 1, 0, TS, (NT - 1) // 2)
            act.wait_ge(y_left, 16 * NT)

        @block.vector
        def _(dve):
            def split_lo(t, slot, r):
                hi = m_hi[:, slot, :, 0:r]
                dve.wait_ge(m_hi_done, t + 1)
                dve.tensor_tensor(m_lo[:, slot, :, 0:r], mix[:, slot, :, 0:r], hi.bitcast(F32), ALU.subtract).then_inc(m_split, 1)

            def add(t, slot, r, turn):
                dve.wait_ge(full, t + 3)
                dve.wait_ge(x_in[slot], 16 * turn + 16)
                for n in range(NH):
                    cols = slice(n * 512, n * 512 + 512)
                    ins = dve.tensor_tensor(y[0:r, slot, cols], bank[slot][n][0:r, :], x[0:r, slot, cols], ALU.add)
                ins.then_inc(added, 1)

            dve.sem_inc(m_split, 2)
            dve.sem_inc(added, 2)
            split_lo(0, 0, P)
            split_lo(1, 1, P)
            with dve.Fori(0, (NT - 1) // 2 - 1) as it:
                for slot in range(2):
                    split_lo(2 * it + slot + 2, slot, P)
                    dve.wait_ge(y_left, 32 * it)
                    add(2 * it + slot, slot, P, it)
            split_lo(NT - 1, 0, TS)
            last = (NT - 3) // 2
            dve.wait_ge(y_left, 32 * last)
            add(NT - 3, 0, P, last)
            add(NT - 2, 1, P, last)
            dve.wait_ge(y_left, 32 * last + 32)
            add(NT - 1, 0, TS, last + 1)



def retention(nc, q_fm, k_fm, v_tm, g_tm, state_in, state_prompt, state_samples, mix_fm, consts):
    with nc.cleanup_on_exit(), ExitStack() as ctx:
        sb = lambda n, s, d=F32: ctx.enter_context(nc.sbuf_tensor(f"rt_{n}", s, d))
        sem = lambda n: nc.alloc_semaphore(f"rt_{n}")
        ps = lambda n, s: ctx.enter_context(nc.psum_tensor(f"rt_{n}", s, F32))
        NCH, J = TP // P, DK // P
        gamma = [1.0 - 2.0 ** (-5 - h) for h in range(HC)]
        sc, kt = ps("sc", [P, P]), ps("kt", [P, J, P])
        o = [ps("o0", [P, DV]), ps("o1", [P, DV])]
        u = [ps("u0", [P, DV]), ps("u1", [P, DV])]
        os_, tr = ps("os", [TS, DV]), ps("tr", [P, DV // P, P])

        ident = sb("ident", [P, P])
        decay, decay_s = sb("decay", [P, HC, P]), sb("decay_s", [TS, HC, TS])
        q_dec, q_dec_s = sb("q_dec", [P, HC, P]), sb("q_dec_s", [P, HC, TS])
        k_dec, k_dec_s = sb("k_dec", [P, HC]), sb("k_dec_s", [TS, HC])
        of_seq, own = sb("of_seq", [P, NS, TS]), sb("own", [TS, NS])
        eps = sb("eps", [P, 1])
        q, k = sb("q", [P, 2, HC, J, P]), sb("k", [P, 2, HC, J, P])
        v, g = sb("v", [P, 2, HC, DV]), sb("g", [P, 2, HC, DV])
        q_s, k_s = sb("q_s", [P, HC, J, TS]), sb("k_s", [P, HC, J, TS])
        v_s, g_s = sb("v_s", [TS, HC, DV]), sb("g_s", [TS, HC, DV])
        qd_s, kd_s = sb("qd_s", [P, HC, J, TS]), sb("kd_s", [TS, HC, J, P])
        scm_s, acc = sb("scm_s", [TS, 2, TS]), sb("acc", [TS, HC, DV])
        scm, kd, qd = sb("scm", [P, 2, P]), sb("kd", [P, 2, J, P]), sb("qd", [P, 2, J, P])
        qx, kx = sb("qx", [P, 2, J, TS]), sb("kx", [TS, 2, J, P])
        state = sb("state", [P, HC, J, DV])
        s0 = [sb(f"s0{h}", [P, J, DV]) for h in range(HC)]
        s1 = [sb(f"s1{i}", [P, J, DV]) for i in range(2)]
        square, ss, rs = sb("square", [P, DV]), sb("ss", [P, 2]), sb("rs", [P, 2])
        og = sb("og", [P, 2, DV])
        mix = sb("mix", [P, 2, DV // P, P])

        const_in, smp_in, zeroed = sem("const_in"), sem("smp_in"), sem("zeroed")
        chunk_in = [sem("chunk_in0"), sem("chunk_in1")]
        s0_in = [sem(f"s0_in{h}") for h in range(HC)]
        first_sc, first_scm, first_kt, first_kd, first_os, first_acc, first_qd = (
            sem(f"first_{n}") for n in ("sc", "scm", "kt", "kd", "os", "acc", "qd"))
        sc_done, scm_done, kt_done, kd_done, qd_done, qx_done, kx_done = (
            sem(n) for n in ("sc", "scm", "kt", "kd", "qd", "qx", "kx"))
        o_done, u_done, os_done, us_done = sem("o"), sem("u"), sem("os"), sem("us")
        sq_done, ln_done, rs_done, gated, state_done, acc_done, s1_done = (
            sem(n) for n in ("sq", "ln", "rs", "gated", "state", "acc", "s1"))
        tr_done, tr_read, state_left = (sem(n) for n in ("tr", "tr_read", "state_left"))
        mix_left, s1_left = ([sem(f"{n}{i}") for i in range(2)] for n in ("mix_left", "s1_left"))
        pool_go, pe_go = sem("pool_go"), sem("pe_go")
        block = ctx.enter_context(nc.Block())
        NB = 2 * HC
        NTURN = NCH // 2
        NSTEP = NB * NTURN
        q_cols, k_cols = (t.rearrange("(h j p) t -> p h j t", j=J, p=P) for t in (q_fm, k_fm))
        v_rows, g_rows = (t.rearrange("t (h n) -> t h n", n=DV) for t in (v_tm, g_tm))
        mix_cols = mix_fm.rearrange("(h r p) t -> p h r t", r=DV // P, p=P)
        tables = ((ident, "ident"), (decay, "ret_decay"), (decay_s, "ret_decay_s"), (q_dec, "ret_q"), (q_dec_s, "ret_q_s"),
                  (k_dec, "ret_k"), (k_dec_s, "ret_k_s"), (of_seq, "of_seq"), (own, "own"))
        NCONST = 16 * len(tables)

        @block.sync
        def _(sp):
            for dst, name in tables:
                sp.dma_start(dst[:], consts[name]).then_inc(const_in, 16)
            for h in range(HC):
                sp.dma_start(q_s[:, h], q_cols[:, h, :, TP:T]).then_inc(smp_in, 16)
                sp.dma_start(k_s[:, h], k_cols[:, h, :, TP:T]).then_inc(smp_in, 16)
            sp.dma_start(v_s[:], v_rows[TP:T]).then_inc(smp_in, 16)
            sp.dma_start(g_s[:], g_rows[TP:T]).then_inc(smp_in, 16)
            with sp.Fori(0, NTURN) as it:
                for slot in range(2):
                    chunk = 2 * it + slot
                    sp.wait_ge(state_done, HC * chunk + 1)
                    cols = bass.ds(chunk * P, P)
                    for h in range(HC):
                        sp.dma_start(q[:, slot, h], q_cols[:, h, :, cols]).then_inc(chunk_in[slot], 16)
                        sp.dma_start(k[:, slot, h], k_cols[:, h, :, cols]).then_inc(chunk_in[slot], 16)
                    sp.dma_start(v[:, slot], v_rows[cols]).then_inc(chunk_in[slot], 16)
                    sp.dma_start(g[:, slot], g_rows[cols]).then_inc(chunk_in[slot], 16)
                    for h in range(HC):
                        sp.wait_ge(s1_done, HC * chunk + h + 1)
                        sp.dma_start(s0[h][:], state_in[bass.ds(chunk, 1), h].rearrange("a (j k) v -> k (a j) v", k=P)).then_inc(s0_in[h], 16)
            sp.wait_ge(state_done, NSTEP + HC + 1)
            sp.dma_start(state_prompt.rearrange("h (j k) v -> k h j v", k=P), state[:]).then_inc(state_left, 16)
            sp.wait_ge(state_left, 16)
            for i in range(2):
                sp.wait_ge(s1_left[i], 16 * NSTEP // 2)

        @block.gpsimd
        def _(pool):
            nc.gpsimd.memset(state[:], 0.0).then_inc(zeroed, 1)
            pool.wait_ge(const_in, NCONST)
            pool.wait_ge(smp_in, 160)
            nc.gpsimd.tensor_tensor(qd_s[:], q_s[:], q_dec_s[:].unsqueeze(2).to_broadcast([P, HC, J, TS]), ALU.mult).then_inc(first_qd, 1)
            pool.wait_ge(first_qd, 1)
            pool.wait_ge(first_kd, HC)
            with pool.Fori(0, NTURN) as it:
                for i in range(NB + 1):
                    if i < NB:
                        h, slot, n = i % HC, i // HC, NB * it + i
                        if h == 0:
                            pool.wait_ge(chunk_in[slot], 160 * it + 160)
                        pool.wait_ge(us_done, n + 1)
                        pool.sem_inc(pool_go, 1)
                        nc.gpsimd.tensor_tensor(qd[:, i % 2], q[:, slot, h], q_dec[:, h].unsqueeze(1).to_broadcast([P, J, P]),
                                                ALU.mult).then_inc(qd_done, 1)
                        seq = bass.ds(2 * it + slot, 1)
                        nc.gpsimd.tensor_tensor(qx[:, i % 2], qd_s[:, h], of_seq[:, seq].to_broadcast([P, J, TS]),
                                                ALU.mult).then_inc(qx_done, 1)
                        nc.gpsimd.tensor_tensor(kx[:, i % 2], kd_s[:, h],
                                                own[:, seq].unsqueeze(2).to_broadcast([TS, J, P]), ALU.mult).then_inc(kx_done, 1)
                    if i >= 1:
                        h, slot, n = (i - 1) % HC, (i - 1) // HC, NB * it + i - 1
                        pool.wait_ge(s1_done, n + HC + 1)
                        pool.dma_start(state_samples[bass.ds(2 * it + slot, 1), h].rearrange("a (j k) v -> k (a j) v", k=P),
                                       s1[(i - 1) % 2][:]).then_inc(s1_left[(i - 1) % 2], 16)

        @block.tensor
        def _(pe):
            pe.wait_ge(const_in, NCONST)
            pe.wait_ge(smp_in, 160)
            for h in range(HC):
                if h:
                    pe.wait_ge(first_scm, h)
                for j in range(J):
                    mm = pe.matmul(sc[0:TS, 0:TS], k_s[:, h, j], q_s[:, h, j], start=(j == 0), stop=(j == J - 1))
                mm.then_inc(first_sc, 1)
                if h:
                    pe.wait_ge(first_kd, h)
                for j in range(J):
                    mm = pe.transpose(kt[0:TS, j], k_s[:, h, j], ident[:])
                mm.then_inc(first_kt, 1)
                pe.wait_ge(first_scm, h + 1)
                if h:
                    pe.wait_ge(first_acc, h)
                pe.matmul(os_[:], scm_s[:, h % 2], v_s[:, h], start=True, stop=True).then_inc(first_os, 1)
            pe.wait_ge(first_kd, HC)
            pe.wait_ge(first_acc, HC)
            pe.wait_ge(zeroed, 1)

            def turn_out(n, slot, r):
                pe.wait_ge(gated, n + 1)
                pe.wait_ge(tr_read, n)
                pe.sem_inc(pe_go, 1)
                for c in range(DV // P):
                    mm = pe.transpose(tr[:, c, 0:r], og[0:r, slot, c * P:c * P + P], ident[0:r, 0:r])
                mm.then_inc(tr_done, 1)

            with pe.Fori(0, NTURN) as it:
                for i in range(NB + 2):
                    if i < NB:
                        h, slot, n = i % HC, i // HC, NB * it + i
                        if h == 0:
                            pe.wait_ge(chunk_in[slot], 160 * it + 160)
                        pe.wait_ge(scm_done, n)
                        for j in range(J):
                            mm = pe.matmul(sc[:], k[:, slot, h, j], q[:, slot, h, j], start=(j == 0), stop=(j == J - 1))
                        mm.then_inc(sc_done, 1)
                        pe.wait_ge(kd_done, n)
                        pe.sem_inc(pe_go, 1)
                        for j in range(J):
                            mm = pe.transpose(kt[:, j], k[:, slot, h, j], ident[:])
                        mm.then_inc(kt_done, 1)
                    if i >= 2:
                        turn_out(NB * it + i - 2, i % 2, P)
                    if 1 <= i <= NB:
                        h, slot, n, m = (i - 1) % HC, (i - 1) // HC, NB * it + i - 1, (i - 1) % 2
                        pe.wait_ge(scm_done, n + 1)
                        pe.wait_ge(qd_done, n + 1)
                        if i >= 2:
                            pe.wait_ge(gated, n - 1)
                        pe.matmul(o[m][:], scm[:, m], v[:, slot, h], start=True, stop=False)
                        for j in range(J):
                            mm = pe.matmul(o[m][:], qd[:, m, j], state[:, h, j], start=False, stop=(j == J - 1))
                        mm.then_inc(o_done, 1)
                        pe.wait_ge(kd_done, n + 1)
                        pe.wait_ge(s1_done, n + HC)
                        for j in range(J):
                            mm = pe.matmul(u[j][:], kd[:, m, j], v[:, slot, h], start=True, stop=True)
                        mm.then_inc(u_done, 1)
                        pe.wait_ge(s0_in[h], 32 * it + 16 * slot + 16)
                        pe.wait_ge(qx_done, n + 1)
                        pe.wait_ge(acc_done, n)
                        for j in range(J):
                            mm = pe.matmul(os_[:], qx[:, m, j], s0[h][:, j], start=(j == 0), stop=(j == J - 1))
                        mm.then_inc(os_done, 1)
                        pe.wait_ge(kx_done, n + 1)
                        pe.wait_ge(state_done, n + HC + 2)
                        for j in range(J):
                            mm = pe.matmul(u[j][:], kx[:, m, j], v_s[:, h], start=True, stop=True)
                        mm.then_inc(us_done, 1)
            for h in range(HC):
                turn_out(NSTEP + h, h % 2, TS)

        @block.scalar
        def _(act):
            load_exp_ln(nc)
            act.wait_ge(const_in, NCONST)
            for h in range(HC):
                act.wait_ge(first_kt, h + 1)
                nc.scalar.activation(kd_s[:, h], kt[0:TS], ACT.Copy, scale=k_dec_s[:, h:h + 1]).then_inc(first_kd, 1)
            act.wait_ge(zeroed, 2)

            def norm(n, slot, r, src):
                nc.scalar.activation(square[0:r, :], src, ACT.Square, accum_out=ss[0:r, slot:slot + 1]).then_inc(sq_done, 1)
                act.wait_ge(sq_done, n + 1)
                nc.scalar.activation(ss[0:r, slot:slot + 1], ss[0:r, slot:slot + 1], ACT.Ln, scale=1.0 / DV, bias=eps[0:r, :]).then_inc(ln_done, 1)
                act.wait_ge(ln_done, n + 1)
                nc.scalar.activation(rs[0:r, slot:slot + 1], ss[0:r, slot:slot + 1], ACT.Exp, scale=-0.5).then_inc(rs_done, 1)

            def store(n, nth, slot, r, dst):
                act.wait_ge(tr_done, n + 1)
                act.wait_ge(mix_left[slot], 16 * nth)
                nc.scalar.copy(mix[:, slot, :, 0:r], tr[:, :, 0:r]).then_inc(tr_read, 1)
                act.wait_ge(tr_read, n + 1)
                act.dma_start(dst, mix[:, slot, :, 0:r]).then_inc(mix_left[slot], 16)

            with act.Fori(0, NTURN) as it:
                for i in range(NB + 2):
                    if i < NB:
                        h, n = i % HC, NB * it + i
                        act.wait_ge(kt_done, n + 1)
                        act.wait_ge(us_done, n + 1)
                        nc.scalar.activation(kd[:, i % 2], kt[:], ACT.Copy, scale=k_dec[:, h:h + 1]).then_inc(kd_done, 1)
                    if 1 <= i <= NB:
                        n, m = NB * it + i - 1, (i - 1) % 2
                        act.wait_ge(o_done, n + 1)
                        act.wait_ge(sq_done, n)
                        if i >= 2:
                            act.wait_ge(gated, n - 1)
                        norm(n, m, P, o[m][:])
                    if i >= 2:
                        h, slot, n = (i - 2) % HC, (i - 2) // HC, NB * it + i - 2
                        store(n, NB // 2 * it + (i - 2) // 2, i % 2, P, mix_cols[:, h, :, bass.ds((2 * it + slot) * P, P)])
            act.wait_ge(acc_done, NSTEP)
            for h in range(HC):
                act.wait_ge(sq_done, NSTEP + h)
                act.wait_ge(gated, NSTEP + h - 1)
                norm(NSTEP + h, h % 2, TS, acc[:, h])
                if h:
                    store(NSTEP + h - 1, (NSTEP + h - 1) // 2, (h - 1) % 2, TS, mix_cols[:, h - 1, :, TP:T])
            store(NSTEP + HC - 1, (NSTEP + HC - 1) // 2, (HC - 1) % 2, TS, mix_cols[:, HC - 1, :, TP:T])
            for i in range(2):
                act.wait_ge(mix_left[i], 16 * (NSTEP + HC) // 2)

        @block.vector
        def _(dve):
            nc.vector.memset(eps[:], EPS).then_inc(zeroed, 1)
            dve.sem_inc(us_done, 2)
            dve.sem_inc(state_done, HC + 1)
            dve.sem_inc(s1_done, HC)
            dve.wait_ge(const_in, NCONST)
            dve.wait_ge(smp_in, 160)
            dve.wait_ge(zeroed, 2)
            for h in range(HC):
                dve.wait_ge(first_sc, h + 1)
                dve.tensor_tensor(scm_s[:, h % 2], sc[0:TS, 0:TS], decay_s[:, h], ALU.mult).then_inc(first_scm, 1)
                dve.wait_ge(first_os, h + 1)
                dve.tensor_copy(acc[:, h], os_[:]).then_inc(first_acc, 1)
            dve.wait_ge(first_acc, HC)

            def gate(n, slot, r, src, silu):
                dve.wait_ge(rs_done, n + 1)
                dve.scalar_tensor_tensor(og[0:r, slot, :], src, rs[0:r, slot:slot + 1], silu, ALU.mult, ALU.mult).then_inc(gated, 1)

            with dve.Fori(0, NTURN) as it:
                for i in range(NB + 1):
                    if i < NB:
                        h, n = i % HC, NB * it + i
                        dve.wait_ge(sc_done, n + 1)
                        dve.wait_ge(us_done, n + 1)
                        dve.tensor_tensor(scm[:, i % 2], sc[:], decay[:, h], ALU.mult).then_inc(scm_done, 1)
                    if i >= 1:
                        h, slot, n, m = (i - 1) % HC, (i - 1) // HC, NB * it + i - 1, (i - 1) % 2
                        if i >= 3:
                            dve.wait_ge(tr_done, n - 1)
                        else:
                            dve.wait_ge(tr_done, NB * it)
                        gate(n, m, P, o[m][:], g[:, slot, h])
                        dve.wait_ge(u_done, n + 1)
                        dve.wait_ge(state_done, n + HC + 1)
                        for j in range(J):
                            ins = dve.scalar_tensor_tensor(state[:, h, j], state[:, h, j], gamma[h] ** P, u[j][:], ALU.mult, ALU.add)
                        ins.then_inc(state_done, 1)
                        dve.wait_ge(os_done, n + 1)
                        dve.wait_ge(acc_done, n)
                        dve.tensor_tensor(acc[:, h], acc[:, h], os_[:], ALU.add).then_inc(acc_done, 1)
                        dve.wait_ge(us_done, n + 3)
                        dve.wait_ge(s1_left[m], 16 * (NB // 2 * it + (i - 1) // 2))
                        for j in range(J):
                            ins = dve.scalar_tensor_tensor(s1[m][:, j], s0[h][:, j], gamma[h] ** LS, u[j][:], ALU.mult, ALU.add)
                        ins.then_inc(s1_done, 1)
            dve.wait_ge(acc_done, NSTEP)
            for h in range(HC):
                dve.wait_ge(tr_done, NSTEP + h - 1)
                gate(NSTEP + h, h % 2, TS, acc[:, h], g_s[:, h])



INPUTS = ["x_prompt", "x_sample", "cache_k", "cache_v", "page_table", "state_hgrn", "state_ret", "norm_g",
          "w_in_even", "w_out_even", "q_norm_g", "k_norm_g", "sb_logit_bias", "hgrn_lower_bounds",
          "hgrn_out_norm_g", "w_in_odd", "w_out_odd"]
OUTPUTS = {
    "y_prompt": (1, TP, D), "y_sample": (NS, LS, D),
    "k_prompt": (1, 1, TP, HA, DA), "v_prompt": (1, 1, TP, HA, DA),
    "k_sample": (1, NS, LS, HA, DA), "v_sample": (1, NS, LS, HA, DA),
    "hgrn_prompt": (1, 1, HB, DB, DB), "hgrn_sample": (1, NS, HB, DB, DB),
    "ret_prompt": (1, 1, HC, DK, DV), "ret_sample": (1, NS, HC, DK, DV),
}


def shape_tables():
    f = np.float32
    out = {"ident": np.eye(P, dtype=f)}
    pos = np.concatenate([np.arange(TP), np.tile(PAGE * NPAGE + np.arange(LS), NS)]).astype(f)
    inv = (1.0 / (f(10000.0) ** np.linspace(0.0, 1.0, DK // 2, dtype=f))).astype(f)
    angle = (inv[:, None] * pos[None, :]).astype(f).astype(np.float64)
    key, other = np.arange(P)[:, None], np.arange(P)[None, :]
    out["tri"] = (key >= other).astype(f)
    out["ones"] = np.ones((P, P), f)
    out["mask"] = np.where(key < other, f(0), f(MASKED)).astype(f)
    sk, sq = np.arange(TS)[:, None], np.arange(TS)[None, :]
    seen = (sk // LS == sq // LS) & (sk < sq)
    out["mask_s"] = np.where(seen, f(0), f(MASKED)).astype(f)
    level = np.zeros((P, 8, P), np.int32)
    for l in range(7):
        m = P // 2 >> l
        level[:, l] = (key // (2 * m) == other // (2 * m)) & (key // m % 2 == 0) & (other // m % 2 == 1)
    level[:, 7] = key == other
    out["level_mask"] = level
    out["own"] = (np.arange(TS)[:, None] // LS == np.arange(NS)[None, :]).astype(f)
    t = np.arange(T)
    out["reset"] = np.tile(np.where(t < TP, t % P != 0, (t - TP) % LS != 0).astype(f), (P, 1))
    lg = np.log1p(-np.exp2(-5.0 - np.arange(HC)))
    rel, rel_s = other - key, sq - sk
    out["ret_decay"] = np.stack([np.where(rel >= 0, np.exp(np.maximum(rel, 0) * g), 0) for g in lg], 1).astype(f)
    seen = (sk // LS == sq // LS) & (rel_s >= 0)
    out["ret_decay_s"] = np.stack([np.where(seen, np.exp(np.where(seen, rel_s, 0) * g), 0) for g in lg], 1).astype(f)
    i, i_s = np.arange(P), np.arange(TS) % LS
    out["ret_q"] = np.tile(np.exp((i + 1) * lg[:, None])[None], (P, 1, 1)).astype(f)
    out["ret_q_s"] = np.tile(np.exp((i_s + 1) * lg[:, None])[None], (P, 1, 1)).astype(f)
    out["ret_k"] = np.exp((P - 1 - i)[:, None] * lg[None]).astype(f)
    out["ret_k_s"] = np.exp((LS - 1 - i_s)[:, None] * lg[None]).astype(f)
    out["of_seq"] = np.tile(out["own"].T[None], (P, 1, 1)).astype(f)
    out["cos"], out["sin"] = np.cos(angle).astype(f), np.sin(angle).astype(f)
    return out


def build(nc, a, o, consts):
    dram = lambda n, s: nc.dram_tensor(n, s, F32).ap()
    q_tm = dram("q_tm", (T, WA))
    qb_fm, fb_fm, ga_fm, gb_fm = (dram(n, (WB, T)) for n in ("qb_fm", "fb_fm", "ga_fm", "gb_fm"))
    ib_tm = dram("ib_tm", (T, WB))
    tm2 = lambda t: t.rearrange("a b t h d -> (a b t) (h d)")
    k_p, v_p, k_s, v_s = (tm2(o[n]) for n in ("k_prompt", "v_prompt", "k_sample", "v_sample"))
    x_p, x_s = (a[n].rearrange("b t d -> (b t) d") for n in ("x_prompt", "x_sample"))

    def split_tm(prompt, sample):
        return lambda t, col: (prompt[t * P:t * P + P, bass.ds(col, WBLK)] if t < NT - 1
                               else sample[:, bass.ds(col, WBLK)])

    def whole_tm(x):
        return lambda t, col: x[t * P:t * P + rows_of(t), bass.ds(col, WBLK)]

    def rows_fm(x):
        tiles = x.rearrange("(r p) t -> r p t", p=P)
        return lambda row: tiles[row] if isinstance(row, int) else tiles[bass.ds(row, 1)].rearrange("a p t -> (a p) t")

    x_of = lambda t: x_p[t * P:t * P + P] if t < NT - 1 else x_s
    project_in(nc, "even", x_of, a["norm_g"][0].rearrange("(c p) -> p c", p=P), a["w_in_even"][0], [
        ("norm", 1, whole_tm(q_tm)), ("norm", 1, split_tm(k_p, k_s)), ("copy", 1, split_tm(v_p, v_s)),
        ("silu", 1, rows_fm(ga_fm)), ("silu", 1, rows_fm(qb_fm)), ("plain", 1, rows_fm(fb_fm)),
        ("copy", 1, whole_tm(ib_tm)), ("silu", 1, rows_fm(gb_fm))], consts, (a["q_norm_g"], a["k_norm_g"]))
    mix0 = dram("mix0", (WA + WB, T))
    attend_prompt(nc, q_tm, k_p, v_p, ga_fm, a["sb_logit_bias"], mix0, consts)
    attend_samples(nc, q_tm, k_s, v_s, ga_fm, a["sb_logit_bias"], a["cache_k"][0], a["cache_v"][0], a["page_table"],
                   mix0, consts)
    hgrn(nc, qb_fm, fb_fm, ib_tm, gb_fm, a["hgrn_lower_bounds"], a["hgrn_out_norm_g"][0], a["state_hgrn"][0],
         o["hgrn_prompt"][0, 0], o["hgrn_sample"][0], mix0, consts)
    tile = lambda prompt, sample: lambda t: sample if isinstance(t, int) and t == NT - 1 else prompt[bass.ds(t * P, P)]
    y1 = dram("y1", (T, D))
    project_out(nc, "out0", mix0, a["w_out_even"][0], tile(x_p, x_s), tile(y1, y1[TP:T]), consts)

    q1_fm, k1_fm = dram("q1_fm", (HC * DK, T)), dram("k1_fm", (HC * DK, T))
    v1_tm, g1_tm = dram("v1_tm", (T, WC)), dram("g1_tm", (T, WC))

    def head_fm(x):
        return lambda row: x.rearrange("(h r) t -> h r t", r=DK)[bass.ds(row, 1)].rearrange("a (j p) t -> p (a j) t", p=P)

    npair = HC * DK // (2 * WBLK)
    project_in(nc, "odd", lambda t: y1[t * P:t * P + rows_of(t)], a["norm_g"][1].rearrange("(c p) -> p c", p=P),
               a["w_in_odd"][0], [("rotary", npair, head_fm(q1_fm)), ("rotary", npair, head_fm(k1_fm)),
                                  ("copy", WC // (2 * WBLK), whole_tm(v1_tm)), ("silu_tm", WC // (2 * WBLK), whole_tm(g1_tm))], consts)
    mix1 = dram("mix1", (WC, T))
    retention(nc, q1_fm, k1_fm, v1_tm, g1_tm, a["state_ret"][0], o["ret_prompt"][0, 0], o["ret_sample"][0], mix1, consts)
    y_p, y_s = (o[n].rearrange("b t d -> (b t) d") for n in ("y_prompt", "y_sample"))
    project_out(nc, "out1", mix1, a["w_out_odd"][0], tile(y1, y1[TP:T]), tile(y_p, y_s), consts)


def make(nc, arrays):
    a = {n: nc.dram_tensor(f"in_{n}", arrays[f"in_{n}"].shape, mybir.dt.from_np(arrays[f"in_{n}"].dtype),
                           kind="ExternalInput").ap() for n in INPUTS}
    consts = {n[6:]: nc.dram_tensor(n, v.shape, mybir.dt.from_np(v.dtype), kind="ExternalInput").ap()
              for n, v in arrays.items() if n.startswith("table_")}
    o = {n: nc.dram_tensor(f"out_{n}", s, F32, kind="ExternalOutput").ap() for n, s in OUTPUTS.items()}
    build(nc, a, o, consts)


def layout(inputs):
    arrays = {f"in_{n}": np.ascontiguousarray(inputs[n]) for n in INPUTS}
    arrays |= {f"table_{n}": v for n, v in shape_tables().items()}
    return arrays


def kernel(**inputs):
    import concourse.bacc as bacc
    from concourse.bass_utils import run_bass_kernel_spmd

    nc = bacc.Bacc("TRN2", target_bir_lowering=False, num_devices=1)
    arrays = layout(inputs)
    make(nc, arrays)
    got = run_bass_kernel_spmd(nc, [arrays], core_ids=[0]).results[0]
    return tuple(got[f"out_{n}"] for n in OUTPUTS)
```

```python
from contextlib import ExitStack, contextmanager

import numpy as np

import concourse.bass as bass
from concourse import mybir

F32 = mybir.dt.float32
F32R = mybir.dt.float32r
I32 = mybir.dt.int32
ACT = mybir.ActivationFunctionType
ALU = mybir.AluOpType
AX_X = mybir.AxisListType.X

P = 128
D = 1024
KD = D // P
TP = 1024
NS, LS = 8, 8
TS = NS * LS
T = TP + TS
NT = TP // P + 1
HA, DA = 8, 64
WA = HA * DA
HB, DB = 4, 128
WB = HB * DB
HC, DK, DV = 4, 256, 512
WC = HC * DV
PAGE = 128
NPAGE = 8
W_EVEN = 4 * WA + 4 * WB
W_ODD = 2 * HC * DK + 2 * WC
EPS = 1e-6
MASKED = -1e30

WBLK = 256
GROUPS = [(0, 364), (364, 362), (726, 362)]


@contextmanager
def repeat(engine, n):
    if n == 1:
        yield 0
    else:
        with engine.Fori(0, n) as i:
            yield i


def load_exp_ln(nc):
    nc.scalar.add_instruction(mybir.InstLoadActFuncSet(
        name=nc.get_next_instruction_name(), engine=mybir.EngineType.Activation, ins=[], outs=[], act_func_set_id=6))


def rows_of(t):
    return P if t < NT - 1 else TS



UNITS = {"norm": 2 * NT, "copy": 2 * NT, "silu_tm": 2 * NT, "silu": 12, "plain": 12, "rotary": 12}
BY_VECTOR = ("norm", "copy", "rotary")
NBANK = 6
NSTAGE = 3


def project_in(nc, tag, x_of, gain_dram, weight, segments, consts, qk_gain_dram=None):
    with nc.cleanup_on_exit(), ExitStack() as ctx:
        sb = lambda n, s, d=F32: ctx.enter_context(nc.sbuf_tensor(f"{tag}_{n}", s, d))
        sem = lambda n: nc.alloc_semaphore(f"{tag}_{n}")
        even = tag == "even"
        bank = [ctx.enter_context(nc.psum_tensor(f"{tag}_bank{i}", [P, 512], F32)) for i in range(NBANK)]
        turn = [ctx.enter_context(nc.psum_tensor(f"{tag}_turn{i}", [P, 4, P], F32)) for i in range(2)]

        h_hi = sb("h_hi", [P, KD, T], F32R)
        h_lo = sb("h_lo", [P, KD, T], F32R)
        x_in = sb("x_in", [P, 2, D])
        x_n = sb("x_n", [P, 2, D])
        square = sb("square", [P, D])
        ssum = sb("ssum", [P, NT])
        std = sb("std", [P, NT])
        rstd = sb("rstd", [P, NT])
        gain = sb("gain", [P, KD])
        h_f = sb("h_f", [P, 2, 4, P])
        ident = sb("ident", [P, P])
        eps = sb("eps", [P, 1])
        raw = sb("raw", [P, 2, KD // 2, WBLK])
        w_hi = sb("w_hi", [P, 2, KD, WBLK], F32R)
        w_lo = sb("w_lo", [P, 2, KD, WBLK], F32R)
        stage_tm = sb("stage_tm", [P, NSTAGE, WBLK])
        if even:
            stage_fm = sb("stage_fm", [P, 2, T])
            qk_gain = sb("qk_gain", [P, 2, DA])
            head_sq = sb("head_sq", [P, 2, WBLK])
            head_ss = sb("head_ss", [P, 2, 4])
            head_std = sb("head_std", [P, 2, 4])
            head_rstd = sb("head_rstd", [P, 2, 4])
            head_n = sb("head_n", [P, 2, WBLK])
        else:
            stage_rot = sb("stage_rot", [P, 2, 2, T])
            cos = sb("cos", [P, T])
            sin = sb("sin", [P, T])
            rot = sb("rot", [P, 4, 364])

        const_in = sem("const_in")
        x_load = [sem("x_load0"), sem("x_load1")]
        sumsq_done, std_done, rstd_done, xn_done = sem("sumsq"), sem("std"), sem("rstd"), sem("xn")
        turned, gained, hi_done, lo_done = sem("turned"), sem("gained"), sem("hi"), sem("lo")
        raw_in = [sem("raw0"), sem("raw1")]
        w_hi_done, w_split, w_used = sem("w_hi"), sem("w_split"), sem("w_used")
        w_at_hand = sem("w_at_hand")
        full = sem("full")
        free = sem("free")
        staged = sem("staged")
        left_tm = [sem(f"left_tm{i}") for i in range(NSTAGE)]
        left_fm = [sem("left_fm0"), sem("left_fm1")]
        eps_set = sem("eps_set")
        head_sq_done, head_ss_done, head_std_done, head_rstd_done, head_n_done = (
            sem("hsq"), sem("hss"), sem("hstd"), sem("hrstd"), sem("hn"))

        NBLK = 2 * sum(n for _, n, _ in segments)
        NCONST = 16 * 4
        w_rows = weight.rearrange("(c p) n -> p c n", p=P)
        block = ctx.enter_context(nc.Block())

        def starts():
            at = dict(unit=0, tm=0, fm=0, norm=0, staged=0)
            for kind, n, place in segments:
                yield kind, n, place, dict(at)
                at["unit"] += n * UNITS[kind]
                at["tm"] += n * UNITS[kind] * (kind in ("norm", "copy", "silu_tm"))
                at["fm"] += {"silu": 4, "plain": 4, "rotary": 2}.get(kind, 0) * n
                at["norm"] += n * UNITS[kind] * (kind == "norm")
                at["staged"] += {"norm": UNITS[kind], "rotary": 12}.get(kind, 0) * n

        @block.sync
        def _(sp):
            sp.dma_start(ident[:], consts["ident"]).then_inc(const_in, 16)
            sp.dma_start(gain[:], gain_dram, allow_slow_non_contiguous=True).then_inc(const_in, 16)
            if even:
                for i in range(2):
                    sp.dma_start(qk_gain[:, i, :], qk_gain_dram[i].to_broadcast([P, DA])).then_inc(const_in, 16)
            else:
                sp.dma_start(cos[:], consts["cos"]).then_inc(const_in, 16)
                sp.dma_start(sin[:], consts["sin"]).then_inc(const_in, 16)
            for t in range(NT):
                if t >= 2:
                    sp.wait_ge(xn_done, t - 1)
                sp.dma_start(x_in[0:rows_of(t), t % 2, :], x_of(t)).then_inc(x_load[t % 2], 16)
                if t in (1, 2):
                    sp.dma_start(raw[:, t - 1, :, :], w_rows[:, 4 * (t - 1):4 * t, 0:WBLK]).then_inc(raw_in[t - 1], 16)
            with sp.Fori(1, NBLK) as b:
                for half in range(2):
                    sp.wait_ge(w_split, 2 * b + half - 1)
                    sp.dma_start(raw[:, half, :, :],
                                 w_rows[:, half * 4:half * 4 + 4, bass.ds(b * WBLK, WBLK)]).then_inc(raw_in[half], 16)

        @block.gpsimd
        def _(pool):
            pool.sem_inc(w_used, 1)
            with pool.Fori(0, NBLK // 2) as pair:
                for slot in range(2):
                    pool.wait_ge(w_used, 2 * pair + slot + 1)
                    for half in range(2):
                        r = raw[:, half, :, :]
                        hi = w_hi[:, slot, half * 4:half * 4 + 4, :]
                        lo = w_lo[:, slot, half * 4:half * 4 + 4, :]
                        pool.wait_ge(raw_in[half], 32 * pair + 16 * slot + 16)
                        pool.sem_inc(w_at_hand, 1)
                        nc.gpsimd.tensor_copy(hi, r).then_inc(w_hi_done, 1)
                        pool.wait_ge(w_hi_done, 4 * pair + 2 * slot + half + 1)
                        nc.gpsimd.tensor_tensor(lo, r, hi.bitcast(F32), ALU.subtract).then_inc(w_split, 1)

        @block.tensor
        def _(pe):
            pe.sem_inc(free, NBANK)
            pe.wait_ge(const_in, NCONST)
            for t in range(NT):
                r = rows_of(t)
                pe.wait_ge(xn_done, t + 1)
                for k in range(2):
                    if t >= 1:
                        pe.wait_ge(gained, 2 * t + k - 1)
                    for c in range(4):
                        mm = pe.transpose(turn[k][:, c, 0:r], x_n[0:r, t % 2, (4 * k + c) * P:(4 * k + c + 1) * P],
                                          ident[0:r, 0:r])
                    mm.then_inc(turned, 1)
            pe.wait_ge(lo_done, 2 * NT)

            def product(out, pairs, opens_block):
                for j, (stationary, moving) in enumerate(pairs):
                    mm = pe.matmul(out, stationary, moving, start=(j == 0), stop=(j == len(pairs) - 1))
                    if j == 0 and opens_block:
                        mm.then_inc(w_used, 1)
                return mm.then_inc(full, 1)

            def parts(h, w):
                return ((h[0], w[0]), (h[0], w[1]), (h[1], w[0]))

            pairs_before, was_by_vector = 0, True
            for kind, n, _, at in starts():
                if (kind in BY_VECTOR) != was_by_vector:
                    pe.wait_ge(free, at["unit"] + NBANK)
                was_by_vector = kind in BY_VECTOR
                with repeat(pe, n) as it:
                    for s in range(2):
                        pe.wait_ge(w_split, 4 * it + 4 * pairs_before + 2 * s + 2)
                        for j in range(UNITS[kind] // 2):
                            u = s * (UNITS[kind] // 2) + j
                            pe.wait_ge(free, it * UNITS[kind] + (at["unit"] + u + 1))
                            if kind in ("norm", "copy", "silu_tm"):
                                tok = slice(j * P, j * P + rows_of(j))
                                out = bank[u % NBANK][0:rows_of(j), 0:WBLK]
                                ops = [(h, w) for c in range(KD)
                                       for h, w in parts((h_hi[:, c, tok], h_lo[:, c, tok]), (w_hi[:, s, c, :], w_lo[:, s, c, :]))]
                            else:
                                g, f = (j // 2, j % 2) if kind == "rotary" else (j % 3, j // 3)
                                g0, gn = GROUPS[g]
                                out = bank[u % NBANK][:, 0:gn]
                                cols = slice(f * P, f * P + P)
                                ops = [(w, h) for c in range(KD)
                                       for h, w in parts((h_hi[:, c, g0:g0 + gn], h_lo[:, c, g0:g0 + gn]),
                                                         (w_hi[:, s, c, cols], w_lo[:, s, c, cols]))]
                            product(out, ops, j == 0)
                pairs_before += n

        @block.scalar
        def _(act):
            for i in range(NSTAGE):
                act.sem_inc(left_tm[i], 16)
            for i in range(2):
                act.sem_inc(left_fm[i], 16)

            def cast_hi(t, k):
                r = rows_of(t)
                act.wait_ge(gained, 2 * t + k + 1)
                nc.scalar.copy(h_hi[:, 4 * k:4 * k + 4, t * P:t * P + r], h_f[:, k, :, 0:r]).then_inc(hi_done, 1)

            act.wait_ge(eps_set, 1)
            for t in range(NT):
                r = rows_of(t)
                act.wait_ge(x_load[t % 2], 16 * (t // 2 + 1))
                nc.scalar.activation(square[0:r, :], x_in[0:r, t % 2, :], ACT.Square,
                                     accum_out=ssum[0:r, t:t + 1]).then_inc(sumsq_done, 1)
                act.wait_ge(sumsq_done, t + 1)
                nc.scalar.activation(std[0:r, t:t + 1], ssum[0:r, t:t + 1], ACT.Sqrt,
                                     bias=eps[0:r, :], scale=1.0 / D).then_inc(std_done, 1)
                if t >= 1:
                    cast_hi(t - 1, 0)
                    cast_hi(t - 1, 1)
            cast_hi(NT - 1, 0)
            cast_hi(NT - 1, 1)

            for kind, n, place, at in starts():
                with repeat(act, n) as it:
                    for u in range(UNITS[kind]):
                        s, j = divmod(u, UNITS[kind] // 2)
                        r = rows_of(j) if kind in ("norm", "copy", "silu_tm") else P
                        src = bank[u % NBANK]
                        this = it * UNITS[kind] + (at["unit"] + u + 1)
                        slot = u % NSTAGE
                        if kind == "norm":
                            nth = it * UNITS[kind] + (at["norm"] + u + 1)
                            act.wait_ge(full, this)
                            act.wait_ge(head_ss_done, nth)
                            nc.scalar.activation(head_sq[0:r, u % 2, :], src[0:r, 0:WBLK], ACT.Square).then_inc(head_sq_done, 1)
                            act.wait_ge(head_ss_done, nth + 2)
                            nc.scalar.activation(head_std[0:r, u % 2, :], head_ss[0:r, u % 2, :], ACT.Sqrt,
                                                 bias=eps[0:r, :], scale=1.0 / DA).then_inc(head_std_done, 1)
                            act.wait_ge(staged, it * UNITS[kind] + (at["staged"] + u + 1))
                        elif kind == "copy":
                            act.wait_ge(free, this + NBANK)
                        elif kind == "silu_tm":
                            act.wait_ge(full, this)
                            act.wait_ge(left_tm[slot], it * (16 * UNITS[kind] // NSTAGE) + 16 * ((at["tm"] + u) // NSTAGE) + 16)
                            nc.scalar.activation(stage_tm[0:r, slot, :], src[0:r, 0:WBLK], ACT.Silu).then_inc(free, 1)
                            act.wait_ge(free, this + NBANK)
                        if kind in ("norm", "copy", "silu_tm"):
                            act.dma_start(place(j, it * 2 * WBLK + s * WBLK), stage_tm[0:r, slot, :]).then_inc(left_tm[slot], 16)
                        if kind in ("silu", "plain"):
                            f, g = j // 3, j % 3
                            row = 2 * s + f
                            slot = row % 2
                            g0, gn = GROUPS[g]
                            act.wait_ge(full, this)
                            if g == 0:
                                act.wait_ge(left_fm[slot], it * 32 + 16 * ((at["fm"] + row) // 2) + 16)
                            nc.scalar.activation(stage_fm[:, slot, g0:g0 + gn], src[:, 0:gn],
                                                 ACT.Silu if kind == "silu" else ACT.Copy).then_inc(free, 1)
                            if g == 2:
                                act.wait_ge(free, this + NBANK)
                                act.dma_start(place(it * 4 + row), stage_fm[:, slot, :]).then_inc(left_fm[slot], 16)
                        if kind == "rotary" and j == 5:
                            act.wait_ge(staged, it * 12 + (at["staged"] + 6 * s + 6))
                            act.dma_start(place(it * 2 + s), stage_rot[:, s, :, :]).then_inc(left_fm[s], 16)
            tm = sum(n * UNITS[k] for k, n, _ in segments if k in ("norm", "copy", "silu_tm"))
            fm = sum(n * {"silu": 4, "plain": 4, "rotary": 2}.get(k, 0) for k, n, _ in segments)
            for i in range(NSTAGE):
                act.wait_ge(left_tm[i], 16 * (tm // NSTAGE) + 16)
            for i in range(2):
                act.wait_ge(left_fm[i], 16 * (fm // 2) + 16)

        @block.vector
        def _(dve):
            nc.vector.memset(eps[:], EPS).then_inc(eps_set, 1)
            dve.sem_inc(head_ss_done, 2)

            def gain_and_split(t):
                r = rows_of(t)
                for k in range(2):
                    dve.wait_ge(turned, 2 * t + k + 1)
                    if t >= 1:
                        dve.wait_ge(lo_done, 2 * t + k - 1)
                        dve.wait_ge(hi_done, 2 * t + k - 1)
                    dve.tensor_tensor(h_f[:, k, :, 0:r], turn[k][:, :, 0:r],
                                      gain[:, 4 * k:4 * k + 4].unsqueeze(2).to_broadcast([P, 4, r]), ALU.mult).then_inc(gained, 1)
                for k in range(2):
                    hi = h_hi[:, 4 * k:4 * k + 4, t * P:t * P + r]
                    dve.wait_ge(hi_done, 2 * t + k + 1)
                    dve.tensor_tensor(h_lo[:, 4 * k:4 * k + 4, t * P:t * P + r], h_f[:, k, :, 0:r],
                                      hi.bitcast(F32), ALU.subtract).then_inc(lo_done, 1)

            dve.wait_ge(const_in, NCONST)
            for t in range(NT):
                r = rows_of(t)
                dve.wait_ge(std_done, t + 1)
                dve.reciprocal(rstd[0:r, t:t + 1], std[0:r, t:t + 1]).then_inc(rstd_done, 1)
                dve.wait_ge(rstd_done, t + 1)
                if t >= 2:
                    dve.wait_ge(turned, 2 * t - 2)
                dve.tensor_scalar(x_n[0:r, t % 2, :], x_in[0:r, t % 2, :], rstd[0:r, t:t + 1], None,
                                  ALU.mult).then_inc(xn_done, 1)
                if t >= 1:
                    gain_and_split(t - 1)
            gain_and_split(NT - 1)

            norm_segments = 0
            for kind, n, _, at in starts():
                if kind in ("silu", "silu_tm", "plain"):
                    continue
                with repeat(dve, n) as it:
                    for u in range(UNITS[kind]):
                        s, j = divmod(u, UNITS[kind] // 2)
                        r = rows_of(j) if kind != "rotary" else P
                        src = bank[u % NBANK]
                        this = it * UNITS[kind] + (at["unit"] + u + 1)
                        slot = u % NSTAGE
                        slot_left = it * (16 * UNITS[kind] // NSTAGE) + 16 * ((at["tm"] + u) // NSTAGE) + 16
                        if kind == "norm":
                            nth = it * UNITS[kind] + (at["norm"] + u + 1)
                            heads = lambda x: x.rearrange("p (h d) -> p h d", d=DA)
                            dve.wait_ge(head_sq_done, nth)
                            dve.tensor_reduce(head_ss[0:r, u % 2, :], heads(head_sq[0:r, u % 2, :]), AX_X, ALU.add).then_inc(head_ss_done, 1)
                            dve.wait_ge(head_std_done, nth)
                            dve.reciprocal(head_rstd[0:r, u % 2, :], head_std[0:r, u % 2, :]).then_inc(head_rstd_done, 1)
                            dve.wait_ge(head_rstd_done, nth)
                            dve.tensor_tensor(heads(head_n[0:r, u % 2, :]), heads(src[0:r, 0:WBLK]),
                                              head_rstd[0:r, u % 2, :].unsqueeze(2).to_broadcast([r, 4, DA]), ALU.mult).then_inc(free, 1)
                            dve.wait_ge(free, this + NBANK)
                            dve.wait_ge(left_tm[slot], slot_left)
                            dve.tensor_tensor(heads(stage_tm[0:r, slot, :]), heads(head_n[0:r, u % 2, :]),
                                              qk_gain[0:r, norm_segments, :].unsqueeze(1).to_broadcast([r, 4, DA]), ALU.mult).then_inc(staged, 1)
                        elif kind == "copy":
                            dve.wait_ge(full, this)
                            dve.wait_ge(left_tm[slot], slot_left)
                            dve.tensor_copy(stage_tm[0:r, slot, :], src[0:r, 0:WBLK]).then_inc(free, 1)
                        elif j % 2 == 1:
                            g0, gn = GROUPS[j // 2]
                            scale = 1.0 if at["unit"] == 0 else DK ** -0.5
                            c, sn = cos[:, g0:g0 + gn], sin[:, g0:g0 + gn]
                            x1, x2 = bank[(u - 1) % NBANK][:, 0:gn], src[:, 0:gn]
                            before = it * 12 + (at["staged"] + 6 * s + (j // 2) * 2)
                            dve.wait_ge(full, this)
                            dve.wait_ge(staged, before)
                            dve.scalar_tensor_tensor(rot[:, 0, 0:gn], x1, scale, c, ALU.mult, ALU.mult)
                            dve.scalar_tensor_tensor(rot[:, 1, 0:gn], x1, scale, sn, ALU.mult, ALU.mult).then_inc(free, 1)
                            dve.scalar_tensor_tensor(rot[:, 2, 0:gn], x2, scale, sn, ALU.mult, ALU.mult)
                            dve.scalar_tensor_tensor(rot[:, 3, 0:gn], x2, scale, c, ALU.mult, ALU.mult).then_inc(free, 1)
                            dve.wait_ge(free, this + NBANK)
                            if j == 1:
                                dve.wait_ge(left_fm[s], it * 16 + 16 * (at["fm"] // 2) + 16)
                            dve.tensor_tensor(stage_rot[:, s, 0, g0:g0 + gn], rot[:, 0, 0:gn], rot[:, 2, 0:gn], ALU.subtract).then_inc(staged, 1)
                            dve.tensor_tensor(stage_rot[:, s, 1, g0:g0 + gn], rot[:, 3, 0:gn], rot[:, 1, 0:gn], ALU.add).then_inc(staged, 1)
                if kind == "norm":
                    norm_segments += 1



def attend_prompt(nc, q_tm, k_tm, v_tm, gate_fm, bias_dram, mix_fm, consts):
    with nc.cleanup_on_exit(), ExitStack() as ctx:
        sb = lambda n, s, d=F32: ctx.enter_context(nc.sbuf_tensor(f"ap_{n}", s, d))
        sem = lambda n: nc.alloc_semaphore(f"ap_{n}")
        NQ = 512
        z = [ctx.enter_context(nc.psum_tensor(f"ap_z{i}", [P, NQ], F32)) for i in range(4)]
        o = [ctx.enter_context(nc.psum_tensor(f"ap_o{i}", [P, NQ], F32)) for i in range(2)]
        turn = [ctx.enter_context(nc.psum_tensor(f"ap_turn{i}", [P, 4, P], F32)) for i in range(2)]
        ident, tri, ones, mask = sb("ident", [P, P]), sb("tri", [P, P]), sb("ones", [P, P]), sb("mask", [P, P])
        qk_in = sb("qk_in", [P, 2, 8, P])
        v_in, v = sb("v_in", [P, 8, P]), sb("v", [P, 8, P])
        gate = sb("gate", [P, TP])
        qk = sb("qk", [P, 2, TP])
        biases = sb("biases", [P, HA])
        bias = sb("bias", [P, 2])
        soft = sb("soft", [P, 2, NQ])
        relu = sb("relu", [P, 2, NQ])
        keep = sb("keep", [P, 3, NQ])
        carry = sb("carry", [P, 3, NQ])
        w = sb("w", [P, 2, NQ])
        mix = sb("mix", [P, TP])

        head_steps = [(1, kb, max(0, kb - 4) * P) for kb in range(7, -1, -1)] + [(0, kb, kb * P) for kb in range(3, -1, -1)]
        steps = [(e, half, kb, lo) for e in range(2) for half, kb, lo in head_steps]
        NSTEP = len(steps)
        opens = [kb == (7 if half else 3) for _, half, kb, _ in steps]
        closes = [kb == 0 for _, _, kb, _ in steps]
        run = [2 * e + 1 - half for e, half, _, _ in steps]
        run_end = [i + 1 for i in range(NSTEP) if closes[i]]

        const_in = sem("const_in")
        qk_load, v_load, gate_load = sem("qk_load"), sem("v_load"), sem("gate_load")
        turned, turn_read = sem("turned"), sem("turn_read")
        v_held, bias_held = sem("v_held"), sem("bias_held")
        logits, abs_done, exp_done, soft_done = sem("logits"), sem("abs"), sem("exp"), sem("soft")
        relu_done, keep_done, carry_done = sem("relu"), sem("keep"), sem("carry")
        summed, w_done, pv_done = sem("summed"), sem("w"), sem("pv")
        mixed, mix_left = sem("mixed"), sem("mix_left")
        block = ctx.enter_context(nc.Block())
        NPAIR = HA // 2
        v_tiles = v_tm.rearrange("(t p) n -> p t n", p=P)
        q_tiles = q_tm[0:TP].rearrange("(t p) n -> p t n", p=P)
        k_tiles = k_tm.rearrange("(t p) n -> p t n", p=P)

        @block.sync
        def _(sp):
            for dst, name in ((ident, "ident"), (tri, "tri"), (ones, "ones"), (mask, "mask")):
                sp.dma_start(dst[:], consts[name]).then_inc(const_in, 16)
            sp.dma_start(biases[:], bias_dram.to_broadcast([P, HA])).then_inc(const_in, 16)
            with sp.Fori(0, NPAIR) as p:
                sp.wait_ge(turned, 4 * p)
                sp.dma_start(qk_in[:, 0, :, :], q_tiles[:, :, bass.ds(p * P, P)]).then_inc(qk_load, 16)
                sp.dma_start(qk_in[:, 1, :, :], k_tiles[:, :, bass.ds(p * P, P)]).then_inc(qk_load, 16)
                sp.wait_ge(v_held, p)
                sp.dma_start(v_in[:], v_tiles[:, :, bass.ds(p * P, P)]).then_inc(v_load, 16)
                sp.wait_ge(mixed, 4 * p + 2)
                sp.dma_start(gate[:], gate_fm[bass.ds(p * P, P), 0:TP]).then_inc(gate_load, 16)
            sp.wait_ge(mix_left, 16 * NPAIR + 16)

        @block.tensor
        def _(pe):
            pe.wait_ge(const_in, 80)
            with pe.Fori(0, NPAIR) as p:
                pe.wait_ge(qk_load, 32 * p + 32)
                for i in range(4):
                    pe.wait_ge(turn_read, 4 * p + i + 1)
                    for c in range(4):
                        mm = pe.transpose(turn[i % 2][:, c, :], qk_in[:, i // 2, 4 * (i % 2) + c, :], ident[:])
                    mm.then_inc(turned, 1)
                pe.wait_ge(turn_read, 4 * p + 6)
                pe.wait_ge(v_held, p + 1)
                for i in range(NSTEP + 3):
                    if i < NSTEP:
                        e, half, kb, lo = steps[i]
                        rows = slice(DA * e, DA * e + DA)
                        pe.wait_ge(w_done, NSTEP * p + i + 1)
                        diagonal = kb >= 4 * half
                        mm = pe.matmul(z[i % 4][:, lo:NQ], qk[rows, 1, kb * P:kb * P + P],
                                       qk[rows, 0, half * NQ + lo:(half + 1) * NQ], start=True, stop=True)
                        if diagonal:
                            mm = pe.matmul(z[i % 4][:, lo:lo + P], ident[:], mask[:], start=False, stop=True,
                                           skip_group_check=True)
                        mm.then_inc(logits, 1)
                    j = i - 2
                    if 0 <= j < NSTEP:
                        lo = steps[j][3]
                        pe.wait_ge(keep_done, NSTEP * p + j + 1)
                        mm = pe.matmul(z[j % 4][:, lo:NQ], tri[:], keep[:, j % 3, lo:NQ], start=False, stop=True,
                                       skip_group_check=True)
                        if not opens[j]:
                            before = steps[j - 1][3]
                            pe.wait_ge(carry_done, NSTEP * p + j)
                            mm = pe.matmul(z[j % 4][:, before:NQ], ones[:], carry[:, (j - 1) % 3, before:NQ],
                                           start=False, stop=True, skip_group_check=True)
                        mm.then_inc(summed, 1)
                    j = i - 3
                    if 0 <= j < NSTEP:
                        e, half, kb, lo = steps[j]
                        rows = slice(DA * e, DA * e + DA)
                        pe.wait_ge(w_done, NSTEP * p + (j + 1 + 4))
                        if opens[j]:
                            pe.wait_ge(mixed, 4 * p + run[j] + 1)
                        pe.matmul(o[run[j] % 2][rows, lo:NQ], v[:, kb, rows], w[:, j % 2, lo:NQ], start=opens[j],
                                  stop=closes[j], skip_group_check=True).then_inc(pv_done, 1)

        @block.scalar
        def _(act):
            load_exp_ln(nc)
            act.sem_inc(turn_read, 2)
            act.sem_inc(w_done, 4)
            with act.Fori(0, NPAIR) as p:
                for i in range(4):
                    act.wait_ge(turned, 4 * p + i + 1)
                    if i == 0:
                        act.wait_ge(pv_done, NSTEP * p)
                    nc.scalar.activation(qk[:, i // 2, 4 * (i % 2) * P:4 * (i % 2 + 1) * P].rearrange("p (c n) -> p c n", n=P),
                                         turn[i % 2][:], ACT.Copy, scale=DA ** -0.5 if i < 2 else 1.0).then_inc(turn_read, 1)
                act.wait_ge(bias_held, p + 1)
                for i in range(NSTEP + 2):
                    if i < NSTEP:
                        e, _, _, lo = steps[i]
                        at = soft[:, i % 2, lo:NQ]
                        act.wait_ge(logits, NSTEP * p + i + 1)
                        act.wait_ge(keep_done, NSTEP * p + i - 1) if i >= 2 else act.wait_ge(keep_done, NSTEP * p)
                        nc.scalar.activation(at, z[i % 4][:, lo:NQ], ACT.Abs, bias=bias[:, e:e + 1]).then_inc(abs_done, 1)
                        act.wait_ge(abs_done, NSTEP * p + i + 1)
                        nc.scalar.activation(at, at, ACT.Exp, scale=-1.0).then_inc(exp_done, 1)
                        act.wait_ge(exp_done, NSTEP * p + i + 1)
                        nc.scalar.activation(at, at, ACT.Ln, bias=1.0).then_inc(soft_done, 1)
                    j = i - 2
                    if j >= 0:
                        e, _, _, lo = steps[j]
                        act.wait_ge(summed, NSTEP * p + j + 1)
                        act.wait_ge(pv_done, NSTEP * p + max(0, j - 1))
                        nc.scalar.activation(w[:, j % 2, lo:NQ], z[j % 4][:, lo:NQ], ACT.Exp,
                                             bias=bias[:, e:e + 1]).then_inc(w_done, 1)
                act.wait_ge(mixed, 4 * p + 4 + 2)
                act.dma_start(mix_fm[bass.ds(p * P, P), 0:TP], mix[:]).then_inc(mix_left, 16)

        @block.vector
        def _(dve):
            dve.sem_inc(mixed, 2)
            dve.sem_inc(mix_left, 16)
            dve.wait_ge(const_in, 80)
            with dve.Fori(0, NPAIR) as p:
                dve.wait_ge(v_load, 16 * p + 16)
                dve.wait_ge(pv_done, NSTEP * p)
                dve.tensor_copy(v[:], v_in[:]).then_inc(v_held, 1)
                dve.wait_ge(w_done, NSTEP * p + 4)
                dve.tensor_copy(bias[:], biases[:, bass.ds(2 * p, 2)]).then_inc(bias_held, 1)
                dve.wait_ge(bias_held, p + 1)
                for i in range(NSTEP + 3):
                    if i < NSTEP:
                        e, half, kb, lo = steps[i]
                        dve.wait_ge(abs_done, NSTEP * p + i + 1)
                        dve.tensor_scalar(relu[:, i % 2, lo:NQ], z[i % 4][:, lo:NQ], bias[:, e:e + 1], 0.0,
                                          ALU.add, ALU.max).then_inc(relu_done, 1)
                        dve.wait_ge(relu_done, NSTEP * p + i + 1)
                        dve.wait_ge(soft_done, NSTEP * p + i + 1)
                        dve.wait_ge(summed, NSTEP * p + max(0, i - 2))
                        dve.scalar_tensor_tensor(keep[:, i % 3, lo:NQ], relu[:, i % 2, lo:NQ], -1.0, soft[:, i % 2, lo:NQ],
                                                 ALU.mult, ALU.subtract).then_inc(keep_done, 1)
                        dve.wait_ge(keep_done, NSTEP * p + i + 1)
                        dve.wait_ge(summed, NSTEP * p + max(0, i - 1))
                        if opens[i]:
                            dve.tensor_copy(carry[:, i % 3, lo:NQ], keep[:, i % 3, lo:NQ]).then_inc(carry_done, 1)
                        else:
                            before = steps[i - 1][3]
                            dve.wait_ge(carry_done, NSTEP * p + i)
                            if lo < before:
                                dve.tensor_copy(carry[:, i % 3, lo:before], keep[:, i % 3, lo:before])
                            dve.tensor_tensor(carry[:, i % 3, before:NQ], carry[:, (i - 1) % 3, before:NQ],
                                              keep[:, i % 3, before:NQ], ALU.add).then_inc(carry_done, 1)
                    j = i - 3
                    if j >= 0 and closes[j]:
                        e, half, _, _ = steps[j]
                        rows = slice(DA * e, DA * e + DA)
                        cols = slice(half * NQ, half * NQ + NQ)
                        dve.wait_ge(pv_done, NSTEP * p + j + 1)
                        if run[j] == 0:
                            dve.wait_ge(gate_load, 16 * p + 16)
                            dve.wait_ge(mix_left, 16 * p + 16)
                        dve.tensor_tensor(mix[rows, cols], o[run[j] % 2][rows, :], gate[rows, cols], ALU.mult).then_inc(mixed, 1)



def attend_samples(nc, q_tm, k_tm, v_tm, gate_fm, bias_dram, cache_k, cache_v, page_table, mix_fm, consts):
    with nc.cleanup_on_exit(), ExitStack() as ctx:
        sb = lambda n, s, d=F32: ctx.enter_context(nc.sbuf_tensor(f"as_{n}", s, d))
        sem = lambda n: nc.alloc_semaphore(f"as_{n}")
        ps = lambda n, s: ctx.enter_context(nc.psum_tensor(f"as_{n}", s, F32))
        HP = HA // 2
        ROWS, NU = HA * LS, 2 * NPAGE
        PAST = NPAGE * PAGE
        ALL = PAST + LS
        z = [[ps(f"z{i}{j}", [P, 512]) for j in range(2)] for i in range(2)]
        turn = [ps("turn0", [P, HP, P]), ps("turn1", [P, HP, P])]
        o = ps("o", [P, WA])
        small = ps("small", [P, 512])
        ident, ones = sb("ident", [P, P]), sb("ones", [P, P])
        mask, sel, own = sb("mask", [P, LS]), sb("sel", [P, 2 * LS]), sb("own", [P, WA])
        table = sb("table", [1, NS * NPAGE], I32)
        biases, bias_row, bias = sb("biases", [1, HA]), sb("bias_row", [1, 2, HA, LS]), sb("bias", [P, 1])
        qk_in = sb("qk_in", [TS, 2, WA])
        qT, kT_new = sb("qT", [P, HP, TS]), sb("kT_new", [P, HP, TS])
        q_now = [sb(f"q_now{i}", [P, HP * (2 * P + 2 * LS)]) for i in range(2)]
        gate, mix = sb("gate", [P, HP, TS]), sb("mix", [P, HP, TS])
        k_page = [sb(f"k_page{i}", [P, NU, WA]) for i in range(2)]
        v_page = [sb(f"v_page{i}", [P, NU, WA]) for i in range(2)]
        v_new = [sb(f"v_new{i}", [LS, 2, WA]) for i in range(2)]
        kT = sb("kT", [P, 4, HP, P])
        soft = [sb(f"soft{i}", [P, ALL]) for i in range(2)]
        keep = [sb(f"keep{i}", [P, ALL]) for i in range(2)]
        w = sb("w", [P, ALL])
        zm = [sb(f"zm{i}", [P, LS]) for i in range(2)]
        wT, wT_new = sb("wT", [P, NPAGE, P]), sb("wT_new", [LS, P])
        mine = sb("mine", [P, WA])

        const_in, table_in, prep = sem("const_in"), sem("table_in"), sem("prep")
        new_turned, new_held = sem("new_turned"), sem("new_held")
        k_in = [[sem(f"k_in{i}{g}") for g in range(NPAGE)] for i in range(2)]
        v_in = [sem("v_in0"), sem("v_in1")]
        cleared, q_set = sem("cleared"), sem("q_set")
        turned = sem("turned")
        held_a, held_d = sem("held_a"), sem("held_d")
        page_logits = sem("page_logits")
        new_logits = sem("new_logits")
        small_read = sem("small_read")
        soft_step, keep_step = sem("soft_step"), sem("keep_step")
        outputs, mined, mix_left = sem("outputs"), sem("mined"), sem("mix_left")
        block = ctx.enter_context(nc.Block())
        NCONST = 16 * 9
        NTURN = NS // 4
        caches = {"k": cache_k.rearrange("g t h d -> g t (h d)"), "v": cache_v.rearrange("g t h d -> g t (h d)")}
        n_pool = cache_k.shape[0]

        @block.sync
        def _(sp):
            sp.dma_start(table[:], page_table.rearrange("(a b) n -> a (b n)", a=1)).then_inc(table_in, 16)
            for i, x in enumerate((q_tm[TP:T], k_tm)):
                sp.dma_start(qk_in[:, i, :], x).then_inc(const_in, 16)
            for dst, name in ((ident, "ident"), (ones, "ones"), (mask, "as_mask"), (sel, "as_sel"), (own, "as_own")):
                sp.dma_start(dst[:], consts[name]).then_inc(const_in, 16)
            sp.dma_start(biases[:], bias_dram).then_inc(const_in, 16)
            sp.dma_start(gate[:], gate_fm[:, TP:T].rearrange("(c p) t -> p c t", p=P)).then_inc(const_in, 16)
            sp.wait_ge(table_in, 16)
            with sp.Fori(0, NTURN) as it:
                for i in range(2):
                    pages = [sp.value_load(table[0:1, bass.ds((4 * it + 2 * i + s) * NPAGE + g, 1)], min_val=0, max_val=n_pool - 1)
                             for g in range(NPAGE) for s in range(2)]
                    sp.wait_ge(new_logits, 2 * it + 1)
                    for u, page in enumerate(pages):
                        sp.dma_start(k_page[i][:, u, :], caches["k"][bass.ds(page, 1)].rearrange("a t n -> (a t) n")).then_inc(k_in[i][u // 2], 16)
                    sp.wait_ge(outputs, 2 * it + i if i else 2 * it + 1)
                    for u, page in enumerate(pages):
                        sp.dma_start(v_page[i][:, u, :], caches["v"][bass.ds(page, 1)].rearrange("a t n -> (a t) n")).then_inc(v_in[i], 16)
                    sp.dma_start(v_new[i][:], v_tm[bass.ds((2 * it + i) * 2 * LS, 2 * LS)].rearrange("(s j) n -> j s n", s=2)).then_inc(v_in[i], 16)
            sp.wait_ge(small_read, 6 * NTURN + 1)
            sp.dma_start(mix_fm[0:WA, TP:T].rearrange("(c p) t -> p c t", p=P), mix[:]).then_inc(mix_left, 16)
            sp.wait_ge(mix_left, 16)

        @block.gpsimd
        def _(pool):
            for i in range(2):
                nc.gpsimd.memset(q_now[i][:], 0.0).then_inc(cleared, 1)
            pool.wait_ge(cleared, 2)
            pool.wait_ge(new_held, 1)
            with pool.Fori(0, NTURN) as it:
                for i in range(2):
                    pool.wait_ge(new_logits, 2 * it + 1)
                    for s in range(2):
                        for e in range(2):
                            rows = slice(DA * e, DA * e + DA)
                            at = s * (P + ROWS) + e * LS
                            dst = q_now[i][:].rearrange("p (c x) -> p c x", c=HP)[rows, :, at:at + LS]
                            pool.sem_inc(cleared, 1)
                            ins = nc.gpsimd.tensor_copy(dst, qT[rows, :, bass.ds((4 * it + 2 * i + s) * LS, LS)])
                    ins.then_inc(q_set, 1)

        @block.tensor
        def _(pe):
            pe.sem_inc(new_logits, 1)
            pe.sem_inc(page_logits, 4)
            pe.sem_inc(outputs, 1)
            pe.wait_ge(const_in, NCONST)
            for i in range(2):
                for c in range(HP):
                    mm = pe.transpose(turn[i][:, c, 0:TS], qk_in[:, i, c * P:c * P + P], ident[0:TS, 0:TS])
                mm.then_inc(new_turned, 1)
            pe.wait_ge(prep, 1)
            pe.matmul(small[:, 0:LS], bias_row[:].rearrange("o s h q -> o (s h q)"), ones[0:1, 0:LS], start=True, stop=True).then_inc(prep, 1)
            pe.wait_ge(new_held, 2)

            def logits(it, i):
                n = 2 * it + i
                for u in range(NU + 1):
                    if u < NU:
                        if u % 2 == 0:
                            pe.wait_ge(k_in[i][u // 2], 32 * it + 32)
                        pe.wait_ge(held_d if u % 2 else held_a, (NU + 2) * it + NPAGE * i + u // 2 + 1)
                        for c in range(HP):
                            mm = pe.transpose(turn[u % 2][:, c, :], k_page[i][:, u, c * P:c * P + P], ident[:])
                        mm.then_inc(turned, 1)
                    if u >= 1:
                        g, s = (u - 1) // 2, (u - 1) % 2
                        if u == 1:
                            pe.wait_ge(keep_step, 8 * it + 1)
                            pe.wait_ge(q_set, n + 1)
                        pe.wait_ge(held_d if s else held_a, (NU + 2) * it + NPAGE * i + g + 2)
                        for c in range(HP):
                            at = (2 * c + s) * P
                            mm = pe.matmul(z[i][g // 4][:, g % 4 * P:g % 4 * P + P], q_now[i][:, at:at + P], kT[:, (u - 1) % 4, c, :],
                                           start=(g % 4 == 0 and s == 0 and c == 0), stop=True, skip_group_check=True)
                        mm.then_inc(page_logits, 1)
                pe.wait_ge(small_read, 6 * it + i + 1)
                for s in range(2):
                    for c in range(HP):
                        at = (2 * c + s) * P
                        mm = pe.matmul(small[:, 0:LS], q_now[i][:, at:at + P], kT_new[:, c, bass.ds((2 * n + s) * LS, LS)],
                                       start=(s == 0 and c == 0), stop=(s == 1 and c == HP - 1))
                mm.then_inc(new_logits, 1)

            def weighted(it, i):
                n = 2 * it + i
                pe.wait_ge(soft_step, 4 * n + 5)
                for half in range(2):
                    pe.wait_ge(held_d if half else held_a, (NU + 2) * it + NU + i + 1)
                    for c in range(4):
                        g = 4 * half + c
                        mm = pe.transpose(turn[half][:, c, :], w[:, g * P:g * P + P], ident[:])
                    mm.then_inc(turned, 1)
                pe.wait_ge(small_read, 6 * it + 3 + 2 * i)
                pe.transpose(small[0:LS, 0:P], w[:, PAST:ALL], ident[:]).then_inc(turned, 1)
                pe.wait_ge(v_in[i], 16 * (NU + 1) * it + 16 * (NU + 1))
                pe.wait_ge(held_a, (NU + 2) * it + NU + i + 2)
                pe.wait_ge(held_d, (NU + 2) * it + NU + i + 2)
                pe.wait_ge(small_read, 6 * it + 4 + 2 * i)
                pe.wait_ge(mined, n + 1)
                for s in range(2):
                    rows = slice(s * ROWS, s * ROWS + ROWS)
                    for g in range(NPAGE):
                        pe.matmul(o[rows, :], wT[:, g, rows], v_page[i][:, 2 * g + s, :], start=(g == 0), stop=False, skip_group_check=True)
                    mm = pe.matmul(o[rows, :], wT_new[:, rows], v_new[i][:, s, :],
                                   start=False, stop=True, skip_group_check=True)
                mm.then_inc(outputs, 1)
                pe.wait_ge(mined, n + 2)
                for c in range(HP):
                    mm = pe.matmul(small[:, c * 2 * LS:(c + 1) * 2 * LS], mine[:, c * P:c * P + P], sel[:], start=(c == 0), stop=True,
                                   skip_group_check=True)
                mm.then_inc(turned, 1)

            with pe.Fori(0, NTURN) as it:
                logits(it, 0)
                logits(it, 1)
                weighted(it, 0)
                weighted(it, 1)

        TURNED = 2 * NU + 2 * 4
        in_turn = lambda i, half: 2 * NU + 4 * i + half

        @block.scalar
        def _(act):
            load_exp_ln(nc)
            act.sem_inc(held_a, 1)
            act.sem_inc(soft_step, 1)
            for i, dst in enumerate((qT, kT_new)):
                act.wait_ge(new_turned, i + 1)
                nc.scalar.activation(dst[:], turn[i][:, :, 0:TS], ACT.Copy, scale=DA ** -0.5 if i == 0 else 1.0).then_inc(new_held, 1)
            act.wait_ge(prep, 3)

            def softplus(it, i):
                n = 2 * it + i
                s = soft[i]
                act.wait_ge(page_logits, NU * n + NU + 4)
                act.wait_ge(keep_step, 8 * it + 1)
                act.wait_ge(soft_step, 4 * n + 1)
                nc.scalar.activation(s[:, 0:512], z[i][0][:], ACT.Abs, bias=bias[:])
                yield
                nc.scalar.activation(s[:, 512:PAST], z[i][1][:], ACT.Abs, bias=bias[:])
                act.wait_ge(small_read, 6 * it + i + 2)
                nc.scalar.activation(s[:, PAST:ALL], zm[i][:], ACT.Abs, bias=bias[:]).then_inc(soft_step, 1)
                yield
                act.wait_ge(soft_step, 4 * n + 2)
                nc.scalar.activation(s[:], s[:], ACT.Exp, scale=-1.0).then_inc(soft_step, 1)
                yield
                act.wait_ge(soft_step, 4 * n + 3)
                nc.scalar.activation(s[:], s[:], ACT.Ln, bias=1.0).then_inc(soft_step, 1)
                yield

            def weights(it, i):
                n = 2 * it + i
                act.wait_ge(keep_step, 4 * n + 5)
                act.wait_ge(outputs, n + 1)
                nc.scalar.activation(w[:], soft[i][:], ACT.Exp, bias=bias[:]).then_inc(soft_step, 1)

            def copy_weights(it, i):
                act.wait_ge(turned, TURNED * it + in_turn(i, 0) + 1)
                nc.scalar.copy(wT[:, 0:4, :], turn[0][:]).then_inc(held_a, 1)

            with act.Fori(0, NTURN) as it:
                parts = iter(())
                for i in range(2):
                    for u in range(0, NU, 2):
                        act.wait_ge(turned, TURNED * it + NU * i + u + 1)
                        act.wait_ge(page_logits, NU * (2 * it + i) + u + 1)
                        nc.scalar.copy(kT[:, u % 4, :, :], turn[0][:]).then_inc(held_a, 1)
                        next(parts, None)
                    parts = softplus(it, i)
                weights(it, 0)
                copy_weights(it, 0)
                for _ in parts:
                    pass
                weights(it, 1)
                copy_weights(it, 1)

        @block.vector
        def _(dve):
            dve.sem_inc(held_d, 1)
            dve.sem_inc(keep_step, 1)
            dve.sem_inc(small_read, 1)
            dve.sem_inc(mined, 1)
            dve.wait_ge(const_in, NCONST)
            dve.tensor_copy(bias_row[:], biases[:].unsqueeze(1).unsqueeze(3).to_broadcast([1, 2, HA, LS])).then_inc(prep, 1)
            dve.wait_ge(prep, 2)
            dve.tensor_copy(bias[:], small[:, 0:1]).then_inc(prep, 1)
            dve.wait_ge(prep, 3)

            def sums(it, i):
                n = 2 * it + i
                k, s, zz = keep[i], soft[i], z[i]
                dve.wait_ge(new_logits, n + 2)
                dve.wait_ge(soft_step, 8 * it + 1)
                dve.tensor_tensor(zm[i][:], small[:, 0:LS], mask[:], ALU.add).then_inc(small_read, 1)
                yield
                dve.wait_ge(small_read, 6 * it + i + 2)
                dve.wait_ge(soft_step, 4 * n + 2)
                dve.wait_ge(keep_step, 4 * n + 1)
                dve.tensor_scalar(k[:, 0:512], zz[0][:], bias[:], 0.0, ALU.add, ALU.max)
                yield
                dve.tensor_scalar(k[:, 512:PAST], zz[1][:], bias[:], 0.0, ALU.add, ALU.max)
                dve.tensor_scalar(k[:, PAST:ALL], zm[i][:], bias[:], 0.0, ALU.add, ALU.max).then_inc(keep_step, 1)
                yield
                dve.wait_ge(keep_step, 4 * n + 2)
                dve.wait_ge(soft_step, 4 * n + 4)
                dve.scalar_tensor_tensor(k[:], k[:], -1.0, s[:], ALU.mult, ALU.subtract).then_inc(keep_step, 1)
                yield
                dve.wait_ge(keep_step, 4 * n + 3)
                dve.tensor_tensor_scan(s[:, ::-1], ones[:, 0:1].to_broadcast([P, ALL]), k[:, ::-1], 0.0, ALU.mult, ALU.add).then_inc(keep_step, 1)
                yield
                dve.wait_ge(keep_step, 4 * n + 4)
                for j in range(2):
                    cols = slice(512 * j, 512 * j + 512)
                    dve.tensor_tensor(s[:, cols], zz[j][:], s[:, cols], ALU.add)
                    yield
                dve.tensor_tensor(s[:, PAST:ALL], zm[i][:], s[:, PAST:ALL], ALU.add).then_inc(keep_step, 1)

            def copy_weights(it, i):
                dve.wait_ge(turned, TURNED * it + in_turn(i, 1) + 1)
                dve.tensor_copy(wT[:, 4:8, :], turn[1][:]).then_inc(held_d, 1)
                dve.wait_ge(turned, TURNED * it + in_turn(i, 2) + 1)
                dve.tensor_copy(wT_new[:], small[0:LS, 0:P]).then_inc(small_read, 1)

            def finish(it, i):
                n = 2 * it + i
                dve.wait_ge(outputs, n + 2)
                dve.tensor_tensor(mine[:], o[:], own[:], ALU.mult).then_inc(mined, 1)
                dve.wait_ge(turned, TURNED * it + in_turn(i, 3) + 1)
                cols = bass.ds(n * 2 * LS, 2 * LS)
                dve.tensor_tensor(mix[:, :, cols], small[:, 0:HP * 2 * LS].rearrange("p (c t) -> p c t", c=HP), gate[:, :, cols],
                                  ALU.mult).then_inc(small_read, 1)

            with dve.Fori(0, NTURN) as it:
                parts = iter(())
                for i in range(2):
                    for u in range(1, NU, 2):
                        dve.wait_ge(turned, TURNED * it + NU * i + u + 1)
                        dve.wait_ge(page_logits, NU * (2 * it + i) + u + 1)
                        dve.tensor_copy(kT[:, u % 4, :, :], turn[1][:]).then_inc(held_d, 1)
                        next(parts, None)
                    for _ in parts:
                        pass
                    parts = sums(it, i)
                next(parts)
                copy_weights(it, 0)
                for _ in parts:
                    pass
                finish(it, 0)
                copy_weights(it, 1)
                finish(it, 1)



def hgrn(nc, q_fm, f_fm, v_tm, gate_fm, bounds, out_gain, state_in, state_prompt, state_samples, mix_fm, consts):
    with nc.cleanup_on_exit(), ExitStack() as ctx:
        sb = lambda n, s, d=F32: ctx.enter_context(nc.sbuf_tensor(f"hg_{n}", s, d))
        two = lambda n, s: [sb(f"{n}{i}", s) for i in range(2)]
        sem = lambda n: nc.alloc_semaphore(f"hg_{n}")
        ps = lambda n, s: ctx.enter_context(nc.psum_tensor(f"hg_{n}", s, F32))
        NL, NCH, NG = 7, TP // P, 2
        NSLOT = NL + 2
        NX = 3
        sc = [ps(f"sc{i}", [P, 4, P]) for i in range(4)]
        sx = ps("sx", [TS, TS])
        ku = ps("ku", [P, 4, P])
        o = [ps("o0", [P, 4, P]), ps("o1", [P, 4, P])]

        ident, ones = sb("ident", [P, P]), sb("ones", [P, P])
        level_mask = sb("level_mask", [P, NL + 1, P], I32)
        own = sb("own", [TS, NS])
        reset = sb("reset", [P, T])
        ab = sb("ab", [P, 2, HB])
        diff, lb, om = sb("diff", [P, HB]), sb("lb", [P, HB]), sb("om", [P, HB])
        gain, eps = sb("gain", [P, 1]), sb("eps", [P, 1])
        q = [sb(f"q{h}", [P, T]) for h in range(HB)]
        k = [sb(f"k{h}", [P, T]) for h in range(HB)]
        b = [sb(f"b{h}", [P, T]) for h in range(HB)]
        v, gate, s0 = two("v", [P, NT, P]), two("gate", [P, T]), two("s0", [P, NS, P])
        x = [sb(f"x{i}", [P, T]) for i in range(NX)]
        scores, scores_s = two("scores", [P, NCH, P]), two("scores_s", [TS, TS])
        eb, tail = two("eb", [P, T]), sb("tail", [P, T])
        qd, kd = two("qd", [P, T]), sb("kd", [P, T])
        kd_tm = sb("kd_tm", [P, NT, P])
        state = sb("state", [P, NCH + 1, P])
        vx = sb("vx", [TS, NS, P])
        s1, s_dec = sb("s1", [P, NS, P]), sb("s_dec", [P, NS, P])
        sq, rs = two("sq", [P, 4 * P]), two("rs", [P, 4 * P])
        on, mix = sb("on", [P, 4 * P]), sb("mix", [P, T])

        const_in, prep, cleared = sem("const_in"), sem("prep"), sem("cleared")
        f_in, q_in = ([sem(f"{n}{h}") for h in range(HB)] for n in ("f_in", "q_in"))
        v_in, gate_in, s0_in = ([sem(f"{n}{i}") for i in range(2)] for n in ("v_in", "g_in", "s_in"))
        sig_done, k_done, logf_done, b_done = sem("sig"), sem("k"), sem("logf"), sem("b")
        exponents, weights, weighted = sem("exponents"), sem("weights"), sem("weighted")
        scored, scored_s, picked, picked_s = sem("scored"), sem("scored_s"), sem("picked"), sem("picked_s")
        eb_done, tail_diff, tail_exp, qd_done, kd_done = sem("eb"), sem("tail_diff"), sem("tail_exp"), sem("qd"), sem("kd")
        turned, held, updates, updates_s, state_done = sem("turned"), sem("held"), sem("updates"), sem("updates_s"), sem("state")
        vx_done, dec_done, s1_done, s_left = sem("vx"), sem("dec"), sem("s1"), sem("s_left")
        o_done, sq_done, sum_done, ln_done, rs_done, on_done, mixed = (
            sem("o"), sem("sq"), sem("sum"), sem("ln"), sem("rs"), sem("on"), sem("mixed"))
        mix_left, state_left = sem("mix_left"), sem("state_left")
        block = ctx.enter_context(nc.Block())
        NCONST = 16 * 7

        def halves(t, l):
            m = P // 2 >> l
            n = T if 2 * m <= LS else TP
            return t[:, 0:n].rearrange("p (c two m) -> p c two m", two=2, m=m)

        def chunks(t):
            return t[:, 0:TP].rearrange("p (c n) -> p c n", n=P), t[:, TP:T].rearrange("p (c n) -> p c n", n=LS)

        def outputs_of(g):
            flat = ku[:].rearrange("p c n -> p (c n)")
            if g < NG:
                return o[g][:].rearrange("p c n -> p (c n)"), flat, slice(4 * P * g, 4 * P * (g + 1))
            return flat[:, 0:TS], flat[:, TS:2 * TS], slice(TP, T)

        def run(scores_slot, rest):
            last, now = iter(()), iter(())
            for h in range(HB + 1):
                last, now = now, (rest(h - 1) if h else iter(()))
                for slot in range(NSLOT):
                    if h < HB:
                        scores_slot(h, slot)
                    if slot == 0:
                        for _ in last:
                            pass
                    next(now, None)
            for _ in now:
                pass

        @block.sync
        def _(sp):
            for dst, src in ((ident[:], consts["ident"]), (ones[:], consts["ones"]), (level_mask[:], consts["level_mask"]),
                             (own[:], consts["own"]), (reset[:], consts["reset"])):
                sp.dma_start(dst, src).then_inc(const_in, 16)
            sp.dma_start(ab[:], bounds.rearrange("e (h k) -> k e h", k=P), allow_slow_non_contiguous=True).then_inc(const_in, 16)
            sp.dma_start(gain[:], out_gain.rearrange("(k a) -> k a", a=1), allow_slow_non_contiguous=True).then_inc(const_in, 16)
            for h in range(HB):
                rows = slice(h * P, h * P + P)
                sp.dma_start(k[h][:], f_fm[rows, :]).then_inc(f_in[h], 16)
                sp.dma_start(q[h][:], q_fm[rows, :]).then_inc(q_in[h], 16)

            def load(h):
                rows, s = slice(h * P, h * P + P), h % 2
                sp.dma_start(v[s][:, 0:NT - 1, :], v_tm[0:TP, rows].rearrange("(c p) n -> p c n", p=P)).then_inc(v_in[s], 16)
                sp.dma_start(v[s][0:TS, NT - 1, :], v_tm[TP:T, rows]).then_inc(v_in[s], 16)
                sp.dma_start(s0[s][:], state_in[:, h].rearrange("b k v -> k b v")).then_inc(s0_in[s], 16)
                sp.dma_start(gate[s][:], gate_fm[rows, :]).then_inc(gate_in[s], 16)

            load(0)
            load(1)
            for h in range(HB):
                sp.wait_ge(state_done, NCH * (h + 1))
                sp.dma_start(state_prompt[h], state[:, NCH, :]).then_inc(state_left, 16)
                sp.wait_ge(s1_done, NG * (h + 1))
                sp.dma_start(state_samples[:, h].rearrange("b k v -> k b v"), s1[:]).then_inc(s_left, 16)
                sp.wait_ge(mixed, 3 * (h + 1))
                sp.dma_start(mix_fm[WA + h * P:WA + h * P + P, :], mix[:]).then_inc(mix_left, 16)
                if h + 2 < HB:
                    load(h + 2)
            sp.wait_ge(mix_left, 16 * HB)
            sp.wait_ge(state_left, 16 * HB)
            sp.wait_ge(s_left, 16 * HB)

        @block.gpsimd
        def _(pool):
            def scores_slot(h, l):
                if l == 0:
                    pool.wait_ge(b_done, h + 1)
                if l == NL - 2:
                    pool.wait_ge(eb_done, h + 1)
                    pool.wait_ge(q_in[h], 16)
                    if h >= 2:
                        pool.wait_ge(o_done, 3 * (h - 1))
                    nc.gpsimd.tensor_tensor(qd[h % 2][:], q[h][:], eb[h % 2][:], ALU.mult).then_inc(qd_done, 1)
                if l < NL:
                    n = NL * h + l
                    if n >= NX:
                        before, level = divmod(n - NX, NL)
                        pool.wait_ge(scored, (NL + 1) * before + level + 1)
                    bb, xx = halves(b[h], l), halves(x[n % NX], l)
                    r = bb[:, :, 0, bb.shape[3] - 1:].to_broadcast([P, bb.shape[1], bb.shape[3]])
                    nc.gpsimd.tensor_tensor(xx[:, :, 0, :], r, bb[:, :, 0, :], ALU.subtract)
                    nc.gpsimd.tensor_tensor(xx[:, :, 1, :], bb[:, :, 1, :], r, ALU.subtract).then_inc(exponents, 1)

            def rest(h):
                s = h % 2
                pool.wait_ge(v_in[s], 32 * (h // 2) + 32)
                if h:
                    pool.wait_ge(updates_s, NG * h)
                nc.gpsimd.tensor_tensor(vx[:], v[s][0:TS, NT - 1, :].unsqueeze(1).to_broadcast([TS, NS, P]),
                                        own[:].unsqueeze(2).to_broadcast([TS, NS, P]), ALU.mult).then_inc(vx_done, 1)
                yield
                pool.wait_ge(s0_in[s], 16 * (h // 2) + 16)
                pool.wait_ge(eb_done, h + 1)
                if h:
                    pool.wait_ge(s1_done, NG * h)
                ends = chunks(eb[s])[1][:, :, LS - 1:].to_broadcast([P, NS, P])
                nc.gpsimd.tensor_tensor(s_dec[:], s0[s][:], ends, ALU.mult).then_inc(dec_done, 1)

            pool.wait_ge(const_in, NCONST)
            run(scores_slot, rest)

        @block.scalar
        def _(act):
            act.wait_ge(prep, 2)
            nc.scalar.activation(lb[:], diff[:], ACT.Sigmoid).then_inc(prep, 1)
            nc.scalar.activation(om[:], diff[:], ACT.Sigmoid, scale=-1.0).then_inc(prep, 1)
            for h in range(HB):
                act.wait_ge(f_in[h], 16)
                nc.scalar.activation(b[h][:], k[h][:], ACT.Sigmoid).then_inc(sig_done, 1)
                act.wait_ge(sig_done, 2 * h + 1)
                nc.scalar.activation(k[h][:], k[h][:], ACT.Sigmoid, scale=-1.0).then_inc(sig_done, 1)
            load_exp_ln(nc)
            act.wait_ge(prep, 4)

            def log_decays(h):
                act.wait_ge(sig_done, 2 * HB)
                nc.scalar.activation(b[h][:], b[h][:], ACT.Ln, scale=om[:, h:h + 1], bias=lb[:, h:h + 1]).then_inc(logf_done, 1)

            def scores_slot(h, l):
                if l < NL:
                    n = T if P >> l <= LS else TP
                    at = x[(NL * h + l) % NX][:, 0:n]
                    act.wait_ge(exponents, NL * h + l + 1)
                    nc.scalar.activation(at, at, ACT.Exp).then_inc(weights, 1)
                if l == 1:
                    if h >= 2:
                        act.wait_ge(state_done, NCH * (h - 1))
                        act.wait_ge(dec_done, h - 1)
                        act.wait_ge(qd_done, h - 1)
                    nc.scalar.activation(eb[h % 2][:], b[h][:], ACT.Exp).then_inc(eb_done, 1)
                if l == 2:
                    act.wait_ge(tail_diff, h + 1)
                    nc.scalar.activation(tail[:], tail[:], ACT.Exp).then_inc(tail_exp, 1)
                if l == 3 and h + 1 < HB:
                    log_decays(h + 1)

            def squares(h, g):
                src, _, tok = outputs_of(g)
                act.wait_ge(o_done, 3 * h + g + 1)
                if h or g == 2:
                    act.wait_ge(sum_done, 3 * h + g - 1 if g else 3 * h)
                nc.scalar.activation(sq[g % 2][:, 0:tok.stop - tok.start], src, ACT.Square).then_inc(sq_done, 1)

            def scales(h, g):
                _, ss, tok = outputs_of(g)
                r = rs[g % 2][:, 0:tok.stop - tok.start]
                act.wait_ge(sum_done, 3 * h + g + 1)
                if h or g == 2:
                    act.wait_ge(on_done, 3 * h + g - 1 if g else 3 * h)
                nc.scalar.activation(r, ss, ACT.Ln, scale=1.0 / DB, bias=eps[:]).then_inc(ln_done, 1)
                act.wait_ge(ln_done, 3 * h + g + 1)
                nc.scalar.activation(r, r, ACT.Exp, scale=-0.5).then_inc(rs_done, 1)

            def rest(h):
                if h:
                    act.wait_ge(updates_s, NG * h)
                for g in range(NG + 1):
                    act.wait_ge(turned, 3 * h + g + 1)
                    if g < NG:
                        nc.scalar.copy(kd_tm[:, 4 * g:4 * g + 4, :], ku[:]).then_inc(held, 1)
                    else:
                        nc.scalar.copy(kd_tm[0:TS, NT - 1, :], ku[0:TS, 0, :]).then_inc(held, 1)
                for _ in range(5):
                    yield
                squares(h, 0)
                squares(h, 1)
                yield
                scales(h, 0)
                yield
                scales(h, 1)
                yield
                squares(h, 2)
                yield
                scales(h, 2)

            log_decays(0)
            run(scores_slot, rest)

        @block.vector
        def _(dve):
            dve.wait_ge(const_in, NCONST)
            dve.tensor_tensor(diff[:], ab[:, 0, :], ab[:, 1, :], ALU.subtract).then_inc(prep, 1)
            nc.vector.memset(eps[:], EPS).then_inc(prep, 1)
            for s in range(2):
                nc.vector.memset(scores[s][:], 0.0)
                nc.vector.memset(scores_s[s][:], 0.0).then_inc(cleared, 1)
            dve.wait_ge(prep, 4)
            dve.wait_ge(cleared, 2)

            def keys(h):
                dve.wait_ge(sig_done, 2 * h + 2)
                dve.tensor_scalar(k[h][:], k[h][:], om[:, h:h + 1], None, ALU.mult).then_inc(k_done, 1)

            def sum_decays(h):
                dve.wait_ge(logf_done, h + 1)
                dve.tensor_tensor_scan(b[h][:], reset[:], b[h][:], 0.0, ALU.mult, ALU.add).then_inc(b_done, 1)

            def pick(h, l):
                mask = level_mask[:, l, :].unsqueeze(1).to_broadcast([P, 4, P])
                if h >= 2 and l == 0:
                    dve.wait_ge(o_done, 3 * (h - 1))
                dve.wait_ge(scored, (NL + 1) * h + l + 1)
                dve.wait_ge(picked, (NL + 1) * h + l)
                for g in range(NG):
                    ins = dve.copy_predicated(scores[h % 2][:, 4 * g:4 * g + 4, :], mask, sc[2 * (l % 2) + g][:])
                ins.then_inc(picked, 1)
                if l >= 4:
                    dve.wait_ge(scored_s, 4 * h + l - 3)
                    dve.wait_ge(picked_s, 4 * h + l - 4)
                    dve.copy_predicated(scores_s[h % 2][:], level_mask[0:TS, l, 0:TS], sx[:]).then_inc(picked_s, 1)

            def scores_slot(h, l):
                if l < NL:
                    xx = halves(x[(NL * h + l) % NX], l)
                    dve.wait_ge(weights, NL * h + l + 1)
                    dve.wait_ge(k_done, h + 1)
                    dve.wait_ge(q_in[h], 16)
                    dve.tensor_tensor(xx[:, :, 0, :], xx[:, :, 0, :], halves(k[h], l)[:, :, 0, :], ALU.mult)
                    dve.tensor_tensor(xx[:, :, 1, :], xx[:, :, 1, :], halves(q[h], l)[:, :, 1, :], ALU.mult).then_inc(weighted, 1)
                if l >= 1:
                    pick(h, l - 1)
                if l == 1:
                    if h:
                        dve.wait_ge(kd_done, h)
                    dve.wait_ge(b_done, h + 1)
                    for bb, tt, n in zip(chunks(b[h]), chunks(tail), (P, LS)):
                        ins = dve.tensor_tensor(tt, bb[:, :, n - 1:].to_broadcast([P, bb.shape[1], n]), bb, ALU.subtract)
                    ins.then_inc(tail_diff, 1)
                if l == 4 and h + 1 < HB:
                    sum_decays(h + 1)
                if l == 5:
                    dve.wait_ge(tail_exp, h + 1)
                    if h:
                        dve.wait_ge(turned, 3 * h)
                    dve.tensor_tensor(kd[:], k[h][:], tail[:], ALU.mult).then_inc(kd_done, 1)

            def finish(h, g):
                src, _, tok = outputs_of(g)
                n = tok.stop - tok.start
                dve.wait_ge(rs_done, 3 * h + g + 1)
                dve.wait_ge(mixed, 3 * h + g)
                dve.tensor_tensor(on[:, 0:n], src, rs[g % 2][:, 0:n], ALU.mult).then_inc(on_done, 1)
                dve.wait_ge(on_done, 3 * h + g + 1)
                dve.scalar_tensor_tensor(mix[:, tok], on[:, 0:n], gain[:, 0:1], gate[h % 2][:, tok], ALU.mult, ALU.mult).then_inc(mixed, 1)

            def rest(h):
                s = h % 2
                yield
                yield
                if h:
                    dve.wait_ge(state_left, 16 * h)
                    dve.wait_ge(o_done, 3 * h - 1)
                for c in range(NCH):
                    u = o[c // 4][:, c % 4, :]
                    if c % 4 == 0:
                        dve.wait_ge(updates, NG * h + c // 4 + 1)
                    if c == 0:
                        dve.tensor_copy(state[:, 1, :], u).then_inc(state_done, 1)
                    else:
                        dve.wait_ge(state_done, NCH * h + c)
                        dve.scalar_tensor_tensor(state[:, c + 1, :], state[:, c, :], eb[s][:, c * P + P - 1:c * P + P], u,
                                                 ALU.mult, ALU.add).then_inc(state_done, 1)
                yield
                for g in range(NG):
                    if g == 0:
                        dve.wait_ge(dec_done, h + 1)
                        if h:
                            dve.wait_ge(s_left, 16 * h)
                    dve.wait_ge(updates_s, NG * h + g + 1)
                    dve.tensor_tensor(s1[:, 4 * g:4 * g + 4, :], s_dec[:, 4 * g:4 * g + 4, :], ku[:], ALU.add).then_inc(s1_done, 1)
                    yield
                    if g == 0:
                        yield
                yield
                dve.wait_ge(gate_in[s], 16 * (h // 2) + 16)
                if h:
                    dve.wait_ge(mix_left, 16 * h)
                finish(h, 0)
                yield
                finish(h, 1)
                yield
                finish(h, 2)

            keys(0)
            sum_decays(0)
            for h in range(1, HB):
                keys(h)
            run(scores_slot, rest)

        @block.tensor
        def _(pe):
            pe.wait_ge(const_in, NCONST)

            def scores_slot(h, l):
                if l > NL:
                    return
                n = (NL + 1) * h + l
                if l < NL:
                    pe.wait_ge(weighted, NL * h + l + 1)
                if n >= 2:
                    pe.wait_ge(picked, n - 1)
                xl = x[(NL * h + l) % NX]
                lhs, rhs = (xl, xl) if l < NL else (k[h], q[h])
                for c in range(NCH):
                    tok = slice(c * P, c * P + P)
                    mm = pe.matmul(sc[2 * (l % 2) + c // 4][:, c % 4, :], lhs[:, tok], rhs[:, tok], start=True, stop=True)
                if l >= 4:
                    if h or l > 4:
                        pe.wait_ge(picked_s, 4 * h + l - 4)
                    pe.matmul(sx[:], lhs[:, TP:T], rhs[:, TP:T], start=True, stop=True).then_inc(scored_s, 1)
                    pe.wait_ge(scored_s, 4 * h + l - 3)
                    pe.sem_inc(scored, 1)
                else:
                    mm.then_inc(scored, 1)

            def rest(h):
                s = h % 2
                pe.wait_ge(kd_done, h + 1)
                if h:
                    pe.wait_ge(on_done, 3 * h)
                for g in range(NG + 1):
                    if g:
                        pe.wait_ge(held, 3 * h + g)
                    for c in range(4 if g < NG else 1):
                        n = P if g < NG else TS
                        at = 4 * g * P + c * P
                        mm = pe.transpose(ku[0:n, c, :], kd[:, at:at + n], ident[:])
                    mm.then_inc(turned, 1)
                yield
                pe.wait_ge(v_in[s], 32 * (h // 2) + 32)
                if h:
                    pe.wait_ge(mixed, 3 * h - 1)
                for g in range(NG):
                    pe.wait_ge(held, 3 * h + g + 1)
                    for c in range(4):
                        mm = pe.matmul(o[g][:, c, :], kd_tm[:, 4 * g + c, :], v[s][:, 4 * g + c, :], start=True, stop=True)
                    mm.then_inc(updates, 1)
                yield
                for g in range(NG):
                    if g == 0:
                        pe.wait_ge(held, 3 * h + 3)
                        pe.wait_ge(vx_done, h + 1)
                    else:
                        pe.wait_ge(s1_done, NG * h + 1)
                    pe.matmul(ku[:].rearrange("p c n -> p (c n)"), kd_tm[0:TS, NT - 1, :],
                              vx[:, 4 * g:4 * g + 4, :].rearrange("t c n -> t (c n)"), start=True, stop=True).then_inc(updates_s, 1)
                    yield
                    if g == 0:
                        yield
                pe.wait_ge(qd_done, h + 1)
                pe.wait_ge(picked, (NL + 1) * (h + 1))
                pe.wait_ge(state_done, NCH * (h + 1))
                for c in range(NCH):
                    tok = slice(c * P, c * P + P)
                    mm = pe.matmul(o[c // 4][:, c % 4, :], v[s][:, c, :], scores[s][:, c, :], start=True, stop=True)
                    if c:
                        mm = pe.matmul(o[c // 4][:, c % 4, :], state[:, c, :], qd[s][:, tok], start=False, stop=True, skip_group_check=True)
                    if c % 4 == 3:
                        mm.then_inc(o_done, 1)
                yield

                def sums(g):
                    _, ss, tok = outputs_of(g)
                    pe.wait_ge(sq_done, 3 * h + g + 1)
                    pe.matmul(ss, ones[:], sq[g % 2][:, 0:tok.stop - tok.start], start=True, stop=True).then_inc(sum_done, 1)

                pe.wait_ge(s1_done, NG * (h + 1))
                sums(0)
                yield
                pe.wait_ge(ln_done, 3 * h + 1)
                sums(1)
                yield
                pe.wait_ge(ln_done, 3 * h + 2)
                pe.wait_ge(picked_s, 4 * h + 4)
                pe.wait_ge(s0_in[s], 16 * (h // 2) + 16)
                out = outputs_of(NG)[0]
                pe.matmul(out, v[s][0:TS, NT - 1, :], scores_s[s][:], start=True, stop=True)
                for c in range(NS):
                    mm = pe.matmul(out[:, c * LS:c * LS + LS], s0[s][:, c, :], qd[s][:, TP + c * LS:TP + c * LS + LS],
                                   start=False, stop=True, skip_group_check=True)
                mm.then_inc(o_done, 1)
                yield
                sums(NG)

            run(scores_slot, rest)



def project_out(nc, tag, mix_fm, weight, x_of, y_of):
    with nc.cleanup_on_exit(), ExitStack() as ctx:
        sb = lambda n, s, d=F32: ctx.enter_context(nc.sbuf_tensor(f"{tag}_{n}", s, d))
        sem = lambda n: nc.alloc_semaphore(f"{tag}_{n}")
        K, NH = weight.shape[0] // P, D // 512
        NRAW = 4
        bank = [[ctx.enter_context(nc.psum_tensor(f"{tag}_bank{s}{n}", [P, 512], F32)) for n in range(NH)] for s in range(2)]
        raw = sb("raw", [P, NRAW, D])
        w_hi, w_lo = sb("w_hi", [P, K, D], F32R), sb("w_lo", [P, K, D], F32R)
        mix = sb("mix", [P, 2, K, P])
        m_hi, m_lo = sb("m_hi", [P, 2, K, P], F32R), sb("m_lo", [P, 2, K, P], F32R)
        xy = sb("xy", [P, 2, D])
        raw_in = [sem(f"raw{i}") for i in range(NRAW)]
        mix_in, x_in, y_left = ([sem(f"{n}{i}") for i in range(2)] for n in ("mix", "x", "left"))
        even_hi, even_split, odd_hi, odd_split = sem("even_hi"), sem("even_split"), sem("odd_hi"), sem("odd_split")
        m_hi_done, m_split = sem("m_hi"), sem("m_split")
        full, added = sem("full"), sem("added")
        block = ctx.enter_context(nc.Block())
        w_rows = weight.rearrange("(c p) n -> p c n", p=P)
        mix_cols = mix_fm.rearrange("(c p) t -> p c t", p=P)
        NTURN = (NT - 1) // 2

        def later(turn):
            return not isinstance(turn, int) or turn > 0

        def split_by(c):
            return (odd_split if c % 2 else even_split), c // 2 + 1

        @block.sync
        def _(sp):
            def load(t, slot, r, turn):
                if later(turn):
                    sp.wait_ge(m_split, t - 1)
                sp.dma_start(mix[:, slot, :, 0:r], mix_cols[:, :, bass.ds(t * P, r)]).then_inc(mix_in[slot], 16)
                if later(turn):
                    sp.wait_ge(y_left[slot], 16 * turn)
                sp.dma_start(xy[0:r, slot, :], x_of(t)).then_inc(x_in[slot], 16)

            load(0, 0, P, 0)
            load(1, 1, P, 0)
            for c in range(K):
                if c >= NRAW:
                    sp.wait_ge(*split_by(c - NRAW))
                sp.dma_start(raw[:, c % NRAW, :], w_rows[:, c, :]).then_inc(raw_in[c % NRAW], 16)
            with sp.Fori(1, NTURN) as it:
                for slot in range(2):
                    load(2 * it + slot, slot, P, it)
            load(NT - 1, 0, TS, NTURN)

        @block.gpsimd
        def _(pool):
            for c in range(1, K, 2):
                r, hi = raw[:, c % NRAW, :], w_hi[:, c, :]
                pool.wait_ge(raw_in[c % NRAW], 16 * (c // NRAW) + 16)
                nc.gpsimd.tensor_copy(hi, r).then_inc(odd_hi, 1)
                pool.wait_ge(odd_hi, c // 2 + 1)
                nc.gpsimd.tensor_tensor(w_lo[:, c, :], r, hi.bitcast(F32), ALU.subtract).then_inc(odd_split, 1)

        @block.tensor
        def _(pe):
            def chunk(slot, c, r):
                hi, lo = m_hi[:, slot, c, 0:r], m_lo[:, slot, c, 0:r]
                for j, (m, w) in enumerate(((hi, w_hi), (hi, w_lo), (lo, w_hi))):
                    for n in range(NH):
                        mm = pe.matmul(bank[slot][n][0:r, :], m, w[:, c, n * 512:n * 512 + 512],
                                       start=(c == 0 and j == 0), stop=(c == K - 1 and j == 2))
                return mm

            def product(t, slot, r):
                pe.wait_ge(m_split, t + 1)
                pe.wait_ge(added, t - 1)
                for c in range(K):
                    mm = chunk(slot, c, r)
                mm.then_inc(full, 1)

            pe.wait_ge(m_split, 2)
            for c in range(K):
                pe.wait_ge(*split_by(c))
                for slot in range(2):
                    mm = chunk(slot, c, P)
                    if c == K - 1:
                        mm.then_inc(full, 1)
            with pe.Fori(1, NTURN) as it:
                for slot in range(2):
                    product(2 * it + slot, slot, P)
            product(NT - 1, 0, TS)

        @block.scalar
        def _(act):
            def split_hi(t, slot, r, turn):
                act.wait_ge(mix_in[slot], 16 * turn + 16)
                if later(turn):
                    act.wait_ge(full, t - 1)
                nc.scalar.copy(m_hi[:, slot, :, 0:r], mix[:, slot, :, 0:r]).then_inc(m_hi_done, 1)

            def store(t, slot, r):
                act.wait_ge(added, t + 1)
                act.dma_start(y_of(t), xy[0:r, slot, :]).then_inc(y_left[slot], 16)

            split_hi(0, 0, P, 0)
            split_hi(1, 1, P, 0)
            for c in range(0, K, 2):
                act.wait_ge(raw_in[c % NRAW], 16 * (c // NRAW) + 16)
                nc.scalar.copy(w_hi[:, c, :], raw[:, c % NRAW, :]).then_inc(even_hi, 1)
            with act.Fori(1, NTURN) as it:
                for slot in range(2):
                    split_hi(2 * it + slot, slot, P, it)
                    store(2 * it + slot - 2, slot, P)
            split_hi(NT - 1, 0, TS, NTURN)
            store(NT - 3, 0, P)
            store(NT - 2, 1, P)
            store(NT - 1, 0, TS)
            act.wait_ge(y_left[0], 16 * NTURN + 16)
            act.wait_ge(y_left[1], 16 * NTURN)

        @block.vector
        def _(dve):
            def split_lo(t, slot, r):
                hi = m_hi[:, slot, :, 0:r]
                dve.wait_ge(m_hi_done, t + 1)
                dve.tensor_tensor(m_lo[:, slot, :, 0:r], mix[:, slot, :, 0:r], hi.bitcast(F32), ALU.subtract).then_inc(m_split, 1)

            def add(t, slot, r, turn):
                dve.wait_ge(full, t + 1)
                dve.wait_ge(x_in[slot], 16 * turn + 16)
                for n in range(NH):
                    cols = slice(n * 512, n * 512 + 512)
                    ins = dve.tensor_tensor(xy[0:r, slot, cols], bank[slot][n][0:r, :], xy[0:r, slot, cols], ALU.add)
                ins.then_inc(added, 1)

            split_lo(0, 0, P)
            split_lo(1, 1, P)
            for c in range(0, K, 2):
                dve.wait_ge(even_hi, c // 2 + 1)
                dve.tensor_tensor(w_lo[:, c, :], raw[:, c % NRAW, :], w_hi[:, c, :].bitcast(F32), ALU.subtract).then_inc(even_split, 1)
            with dve.Fori(1, NTURN) as it:
                for slot in range(2):
                    split_lo(2 * it + slot, slot, P)
                    add(2 * it + slot - 2, slot, P, it - 1)
            split_lo(NT - 1, 0, TS)
            add(NT - 3, 0, P, NTURN - 1)
            add(NT - 2, 1, P, NTURN - 1)
            add(NT - 1, 0, TS, NTURN)



def retention(nc, q_fm, k_fm, v_tm, g_tm, state_in, state_prompt, state_samples, mix_fm, consts):
    with nc.cleanup_on_exit(), ExitStack() as ctx:
        sb = lambda n, s, d=F32: ctx.enter_context(nc.sbuf_tensor(f"rt_{n}", s, d))
        sem = lambda n: nc.alloc_semaphore(f"rt_{n}")
        ps = lambda n, s: ctx.enter_context(nc.psum_tensor(f"rt_{n}", s, F32))
        NCH, J = TP // P, DK // P
        gamma = [1.0 - 2.0 ** (-5 - h) for h in range(HC)]
        sc, kt = ps("sc", [P, P]), ps("kt", [P, J, P])
        o = [ps("o0", [P, DV]), ps("o1", [P, DV])]
        u = [ps("u0", [P, DV]), ps("u1", [P, DV])]
        os_, tr = ps("os", [TS, DV]), ps("tr", [P, DV // P, P])

        ident = sb("ident", [P, P])
        decay, decay_s = sb("decay", [P, HC, P]), sb("decay_s", [TS, HC, TS])
        q_dec, q_dec_s = sb("q_dec", [P, HC, P]), sb("q_dec_s", [P, HC, TS])
        k_dec, k_dec_s = sb("k_dec", [P, HC]), sb("k_dec_s", [TS, HC])
        of_seq, own = sb("of_seq", [P, NS, TS]), sb("own", [TS, NS])
        eps = sb("eps", [P, 1])
        q, k = sb("q", [P, 2, HC, J, P]), sb("k", [P, 2, HC, J, P])
        v, g = sb("v", [P, 2, HC, DV]), sb("g", [P, 2, HC, DV])
        q_s, k_s = sb("q_s", [P, HC, J, TS]), sb("k_s", [P, HC, J, TS])
        v_s, g_s = sb("v_s", [TS, HC, DV]), sb("g_s", [TS, HC, DV])
        qd_s, kd_s = sb("qd_s", [P, HC, J, TS]), sb("kd_s", [TS, HC, J, P])
        scm_s, acc = sb("scm_s", [TS, 2, TS]), sb("acc", [TS, HC, DV])
        scm, kd, qd = sb("scm", [P, 2, P]), sb("kd", [P, 2, J, P]), sb("qd", [P, 2, J, P])
        qx, kx = sb("qx", [P, 2, J, TS]), sb("kx", [TS, 2, J, P])
        state = sb("state", [P, HC, J, DV])
        s0 = [sb(f"s0{h}", [P, J, DV]) for h in range(HC)]
        s1 = [sb(f"s1{i}", [P, J, DV]) for i in range(2)]
        square, ss, rs = sb("square", [P, DV]), sb("ss", [P, 2]), sb("rs", [P, 2])
        og = sb("og", [P, 2, DV])
        mix = sb("mix", [P, 2, DV // P, P])

        const_in, smp_in, zeroed = sem("const_in"), sem("smp_in"), sem("zeroed")
        chunk_in = [sem("chunk_in0"), sem("chunk_in1")]
        s0_in = [sem(f"s0_in{h}") for h in range(HC)]
        first_sc, first_scm, first_kt, first_kd, first_os, first_acc, first_qd = (
            sem(f"first_{n}") for n in ("sc", "scm", "kt", "kd", "os", "acc", "qd"))
        sc_done, scm_done, kt_done, kd_done, qd_done, qx_done, kx_done = (
            sem(n) for n in ("sc", "scm", "kt", "kd", "qd", "qx", "kx"))
        o_done, u_done, os_done, us_done = sem("o"), sem("u"), sem("os"), sem("us")
        sq_done, ln_done, rs_done, gated, state_done, acc_done, s1_done = (
            sem(n) for n in ("sq", "ln", "rs", "gated", "state", "acc", "s1"))
        tr_done, tr_read, state_left = (sem(n) for n in ("tr", "tr_read", "state_left"))
        mix_left, s1_left = ([sem(f"{n}{i}") for i in range(2)] for n in ("mix_left", "s1_left"))
        pool_go, pe_go = sem("pool_go"), sem("pe_go")
        block = ctx.enter_context(nc.Block())
        NB = 2 * HC
        NTURN = NCH // 2
        NSTEP = NB * NTURN
        q_cols, k_cols = (t.rearrange("(h j p) t -> p h j t", j=J, p=P) for t in (q_fm, k_fm))
        v_rows, g_rows = (t.rearrange("t (h n) -> t h n", n=DV) for t in (v_tm, g_tm))
        mix_cols = mix_fm.rearrange("(h r p) t -> p h r t", r=DV // P, p=P)
        tables = ((ident, "ident"), (decay, "ret_decay"), (decay_s, "ret_decay_s"), (q_dec, "ret_q"), (q_dec_s, "ret_q_s"),
                  (k_dec, "ret_k"), (k_dec_s, "ret_k_s"), (of_seq, "of_seq"), (own, "own"))
        NCONST = 16 * len(tables)

        @block.sync
        def _(sp):
            for dst, name in tables:
                sp.dma_start(dst[:], consts[name]).then_inc(const_in, 16)
            for h in range(HC):
                sp.dma_start(q_s[:, h], q_cols[:, h, :, TP:T]).then_inc(smp_in, 16)
                sp.dma_start(k_s[:, h], k_cols[:, h, :, TP:T]).then_inc(smp_in, 16)
            sp.dma_start(v_s[:], v_rows[TP:T]).then_inc(smp_in, 16)
            sp.dma_start(g_s[:], g_rows[TP:T]).then_inc(smp_in, 16)
            with sp.Fori(0, NTURN) as it:
                for slot in range(2):
                    chunk = 2 * it + slot
                    sp.wait_ge(state_done, HC * chunk + 1)
                    cols = bass.ds(chunk * P, P)
                    for h in range(HC):
                        sp.dma_start(q[:, slot, h], q_cols[:, h, :, cols]).then_inc(chunk_in[slot], 16)
                        sp.dma_start(k[:, slot, h], k_cols[:, h, :, cols]).then_inc(chunk_in[slot], 16)
                    sp.dma_start(v[:, slot], v_rows[cols]).then_inc(chunk_in[slot], 16)
                    sp.dma_start(g[:, slot], g_rows[cols]).then_inc(chunk_in[slot], 16)
                    for h in range(HC):
                        sp.wait_ge(s1_done, HC * chunk + h + 1)
                        sp.dma_start(s0[h][:], state_in[bass.ds(chunk, 1), h].rearrange("a (j k) v -> k (a j) v", k=P)).then_inc(s0_in[h], 16)
            sp.wait_ge(state_done, NSTEP + HC + 1)
            sp.dma_start(state_prompt.rearrange("h (j k) v -> k h j v", k=P), state[:]).then_inc(state_left, 16)
            sp.wait_ge(state_left, 16)
            for i in range(2):
                sp.wait_ge(s1_left[i], 16 * NSTEP // 2)

        @block.gpsimd
        def _(pool):
            nc.gpsimd.memset(state[:], 0.0).then_inc(zeroed, 1)
            pool.wait_ge(const_in, NCONST)
            pool.wait_ge(smp_in, 160)
            nc.gpsimd.tensor_tensor(qd_s[:], q_s[:], q_dec_s[:].unsqueeze(2).to_broadcast([P, HC, J, TS]), ALU.mult).then_inc(first_qd, 1)
            pool.wait_ge(first_qd, 1)
            pool.wait_ge(first_kd, HC)
            with pool.Fori(0, NTURN) as it:
                for i in range(NB + 1):
                    if i < NB:
                        h, slot, n = i % HC, i // HC, NB * it + i
                        if h == 0:
                            pool.wait_ge(chunk_in[slot], 160 * it + 160)
                        pool.wait_ge(us_done, n + 1)
                        pool.sem_inc(pool_go, 1)
                        nc.gpsimd.tensor_tensor(qd[:, i % 2], q[:, slot, h], q_dec[:, h].unsqueeze(1).to_broadcast([P, J, P]),
                                                ALU.mult).then_inc(qd_done, 1)
                        seq = bass.ds(2 * it + slot, 1)
                        nc.gpsimd.tensor_tensor(qx[:, i % 2], qd_s[:, h], of_seq[:, seq].to_broadcast([P, J, TS]),
                                                ALU.mult).then_inc(qx_done, 1)
                        nc.gpsimd.tensor_tensor(kx[:, i % 2], kd_s[:, h],
                                                own[:, seq].unsqueeze(2).to_broadcast([TS, J, P]), ALU.mult).then_inc(kx_done, 1)
                    if i >= 1:
                        h, slot, n = (i - 1) % HC, (i - 1) // HC, NB * it + i - 1
                        pool.wait_ge(s1_done, n + HC + 1)
                        pool.dma_start(state_samples[bass.ds(2 * it + slot, 1), h].rearrange("a (j k) v -> k (a j) v", k=P),
                                       s1[(i - 1) % 2][:]).then_inc(s1_left[(i - 1) % 2], 16)

        @block.tensor
        def _(pe):
            pe.wait_ge(const_in, NCONST)
            pe.wait_ge(smp_in, 160)
            for h in range(HC):
                if h:
                    pe.wait_ge(first_scm, h)
                for j in range(J):
                    mm = pe.matmul(sc[0:TS, 0:TS], k_s[:, h, j], q_s[:, h, j], start=(j == 0), stop=(j == J - 1))
                mm.then_inc(first_sc, 1)
                if h:
                    pe.wait_ge(first_kd, h)
                for j in range(J):
                    mm = pe.transpose(kt[0:TS, j], k_s[:, h, j], ident[:])
                mm.then_inc(first_kt, 1)
                pe.wait_ge(first_scm, h + 1)
                if h:
                    pe.wait_ge(first_acc, h)
                pe.matmul(os_[:], scm_s[:, h % 2], v_s[:, h], start=True, stop=True).then_inc(first_os, 1)
            pe.wait_ge(first_kd, HC)
            pe.wait_ge(first_acc, HC)
            pe.wait_ge(zeroed, 1)

            def turn_out(n, slot, r):
                pe.wait_ge(gated, n + 1)
                pe.wait_ge(tr_read, n)
                pe.sem_inc(pe_go, 1)
                for c in range(DV // P):
                    mm = pe.transpose(tr[:, c, 0:r], og[0:r, slot, c * P:c * P + P], ident[0:r, 0:r])
                mm.then_inc(tr_done, 1)

            with pe.Fori(0, NTURN) as it:
                for i in range(NB + 2):
                    if i < NB:
                        h, slot, n = i % HC, i // HC, NB * it + i
                        if h == 0:
                            pe.wait_ge(chunk_in[slot], 160 * it + 160)
                        pe.wait_ge(scm_done, n)
                        for j in range(J):
                            mm = pe.matmul(sc[:], k[:, slot, h, j], q[:, slot, h, j], start=(j == 0), stop=(j == J - 1))
                        mm.then_inc(sc_done, 1)
                        pe.wait_ge(kd_done, n)
                        pe.sem_inc(pe_go, 1)
                        for j in range(J):
                            mm = pe.transpose(kt[:, j], k[:, slot, h, j], ident[:])
                        mm.then_inc(kt_done, 1)
                    if i >= 2:
                        turn_out(NB * it + i - 2, i % 2, P)
                    if 1 <= i <= NB:
                        h, slot, n, m = (i - 1) % HC, (i - 1) // HC, NB * it + i - 1, (i - 1) % 2
                        pe.wait_ge(scm_done, n + 1)
                        pe.wait_ge(qd_done, n + 1)
                        if i >= 2:
                            pe.wait_ge(gated, n - 1)
                        pe.matmul(o[m][:], scm[:, m], v[:, slot, h], start=True, stop=False)
                        for j in range(J):
                            mm = pe.matmul(o[m][:], qd[:, m, j], state[:, h, j], start=False, stop=(j == J - 1))
                        mm.then_inc(o_done, 1)
                        pe.wait_ge(kd_done, n + 1)
                        pe.wait_ge(s1_done, n + HC)
                        for j in range(J):
                            mm = pe.matmul(u[j][:], kd[:, m, j], v[:, slot, h], start=True, stop=True)
                        mm.then_inc(u_done, 1)
                        pe.wait_ge(s0_in[h], 32 * it + 16 * slot + 16)
                        pe.wait_ge(qx_done, n + 1)
                        pe.wait_ge(acc_done, n)
                        for j in range(J):
                            mm = pe.matmul(os_[:], qx[:, m, j], s0[h][:, j], start=(j == 0), stop=(j == J - 1))
                        mm.then_inc(os_done, 1)
                        pe.wait_ge(kx_done, n + 1)
                        pe.wait_ge(state_done, n + HC + 2)
                        for j in range(J):
                            mm = pe.matmul(u[j][:], kx[:, m, j], v_s[:, h], start=True, stop=True)
                        mm.then_inc(us_done, 1)
            for h in range(HC):
                turn_out(NSTEP + h, h % 2, TS)

        @block.scalar
        def _(act):
            load_exp_ln(nc)
            act.wait_ge(const_in, NCONST)
            for h in range(HC):
                act.wait_ge(first_kt, h + 1)
                nc.scalar.activation(kd_s[:, h], kt[0:TS], ACT.Copy, scale=k_dec_s[:, h:h + 1]).then_inc(first_kd, 1)
            act.wait_ge(zeroed, 2)

            def norm(n, slot, r, src):
                nc.scalar.activation(square[0:r, :], src, ACT.Square, accum_out=ss[0:r, slot:slot + 1]).then_inc(sq_done, 1)
                act.wait_ge(sq_done, n + 1)
                nc.scalar.activation(ss[0:r, slot:slot + 1], ss[0:r, slot:slot + 1], ACT.Ln, scale=1.0 / DV, bias=eps[0:r, :]).then_inc(ln_done, 1)
                act.wait_ge(ln_done, n + 1)
                nc.scalar.activation(rs[0:r, slot:slot + 1], ss[0:r, slot:slot + 1], ACT.Exp, scale=-0.5).then_inc(rs_done, 1)

            def store(n, nth, slot, r, dst):
                act.wait_ge(tr_done, n + 1)
                act.wait_ge(mix_left[slot], 16 * nth)
                nc.scalar.copy(mix[:, slot, :, 0:r], tr[:, :, 0:r]).then_inc(tr_read, 1)
                act.wait_ge(tr_read, n + 1)
                act.dma_start(dst, mix[:, slot, :, 0:r]).then_inc(mix_left[slot], 16)

            with act.Fori(0, NTURN) as it:
                for i in range(NB + 2):
                    if i < NB:
                        h, n = i % HC, NB * it + i
                        act.wait_ge(kt_done, n + 1)
                        act.wait_ge(us_done, n + 1)
                        nc.scalar.activation(kd[:, i % 2], kt[:], ACT.Copy, scale=k_dec[:, h:h + 1]).then_inc(kd_done, 1)
                    if 1 <= i <= NB:
                        n, m = NB * it + i - 1, (i - 1) % 2
                        act.wait_ge(o_done, n + 1)
                        act.wait_ge(sq_done, n)
                        if i >= 2:
                            act.wait_ge(gated, n - 1)
                        norm(n, m, P, o[m][:])
                    if i >= 2:
                        h, slot, n = (i - 2) % HC, (i - 2) // HC, NB * it + i - 2
                        store(n, NB // 2 * it + (i - 2) // 2, i % 2, P, mix_cols[:, h, :, bass.ds((2 * it + slot) * P, P)])
            act.wait_ge(acc_done, NSTEP)
            for h in range(HC):
                act.wait_ge(sq_done, NSTEP + h)
                act.wait_ge(gated, NSTEP + h - 1)
                norm(NSTEP + h, h % 2, TS, acc[:, h])
                if h:
                    store(NSTEP + h - 1, (NSTEP + h - 1) // 2, (h - 1) % 2, TS, mix_cols[:, h - 1, :, TP:T])
            store(NSTEP + HC - 1, (NSTEP + HC - 1) // 2, (HC - 1) % 2, TS, mix_cols[:, HC - 1, :, TP:T])
            for i in range(2):
                act.wait_ge(mix_left[i], 16 * (NSTEP + HC) // 2)

        @block.vector
        def _(dve):
            nc.vector.memset(eps[:], EPS).then_inc(zeroed, 1)
            dve.sem_inc(us_done, 2)
            dve.sem_inc(state_done, HC + 1)
            dve.sem_inc(s1_done, HC)
            dve.wait_ge(const_in, NCONST)
            dve.wait_ge(smp_in, 160)
            dve.wait_ge(zeroed, 2)
            for h in range(HC):
                dve.wait_ge(first_sc, h + 1)
                dve.tensor_tensor(scm_s[:, h % 2], sc[0:TS, 0:TS], decay_s[:, h], ALU.mult).then_inc(first_scm, 1)
                dve.wait_ge(first_os, h + 1)
                dve.tensor_copy(acc[:, h], os_[:]).then_inc(first_acc, 1)
            dve.wait_ge(first_acc, HC)

            def gate(n, slot, r, src, silu):
                dve.wait_ge(rs_done, n + 1)
                dve.scalar_tensor_tensor(og[0:r, slot, :], src, rs[0:r, slot:slot + 1], silu, ALU.mult, ALU.mult).then_inc(gated, 1)

            with dve.Fori(0, NTURN) as it:
                for i in range(NB + 1):
                    if i < NB:
                        h, n = i % HC, NB * it + i
                        dve.wait_ge(sc_done, n + 1)
                        dve.wait_ge(us_done, n + 1)
                        dve.tensor_tensor(scm[:, i % 2], sc[:], decay[:, h], ALU.mult).then_inc(scm_done, 1)
                    if i >= 1:
                        h, slot, n, m = (i - 1) % HC, (i - 1) // HC, NB * it + i - 1, (i - 1) % 2
                        if i >= 3:
                            dve.wait_ge(tr_done, n - 1)
                        else:
                            dve.wait_ge(tr_done, NB * it)
                        gate(n, m, P, o[m][:], g[:, slot, h])
                        dve.wait_ge(u_done, n + 1)
                        dve.wait_ge(state_done, n + HC + 1)
                        for j in range(J):
                            ins = dve.scalar_tensor_tensor(state[:, h, j], state[:, h, j], gamma[h] ** P, u[j][:], ALU.mult, ALU.add)
                        ins.then_inc(state_done, 1)
                        dve.wait_ge(os_done, n + 1)
                        dve.wait_ge(acc_done, n)
                        dve.tensor_tensor(acc[:, h], acc[:, h], os_[:], ALU.add).then_inc(acc_done, 1)
                        dve.wait_ge(us_done, n + 3)
                        dve.wait_ge(s1_left[m], 16 * (NB // 2 * it + (i - 1) // 2))
                        for j in range(J):
                            ins = dve.scalar_tensor_tensor(s1[m][:, j], s0[h][:, j], gamma[h] ** LS, u[j][:], ALU.mult, ALU.add)
                        ins.then_inc(s1_done, 1)
            dve.wait_ge(acc_done, NSTEP)
            for h in range(HC):
                dve.wait_ge(tr_done, NSTEP + h - 1)
                gate(NSTEP + h, h % 2, TS, acc[:, h], g_s[:, h])



INPUTS = ["x_prompt", "x_sample", "cache_k", "cache_v", "page_table", "state_hgrn", "state_ret", "norm_g",
          "w_in_even", "w_out_even", "q_norm_g", "k_norm_g", "sb_logit_bias", "hgrn_lower_bounds",
          "hgrn_out_norm_g", "w_in_odd", "w_out_odd"]
OUTPUTS = {
    "y_prompt": (1, TP, D), "y_sample": (NS, LS, D),
    "k_prompt": (1, 1, TP, HA, DA), "v_prompt": (1, 1, TP, HA, DA),
    "k_sample": (1, NS, LS, HA, DA), "v_sample": (1, NS, LS, HA, DA),
    "hgrn_prompt": (1, 1, HB, DB, DB), "hgrn_sample": (1, NS, HB, DB, DB),
    "ret_prompt": (1, 1, HC, DK, DV), "ret_sample": (1, NS, HC, DK, DV),
}


def shape_tables():
    f = np.float32
    out = {"ident": np.eye(P, dtype=f)}
    pos = np.concatenate([np.arange(TP), np.tile(PAGE * NPAGE + np.arange(LS), NS)]).astype(f)
    inv = (1.0 / (f(10000.0) ** np.linspace(0.0, 1.0, DK // 2, dtype=f))).astype(f)
    angle = (inv[:, None] * pos[None, :]).astype(f).astype(np.float64)
    key, other = np.arange(P)[:, None], np.arange(P)[None, :]
    out["tri"] = (key >= other).astype(f)
    out["ones"] = np.ones((P, P), f)
    out["mask"] = np.where(key < other, f(0), f(MASKED)).astype(f)
    sk, sq = np.arange(TS)[:, None], np.arange(TS)[None, :]
    seen = (sk // LS == sq // LS) & (sk < sq)
    row = np.arange(P)
    row_s, row_h, row_q = row // (HA * LS), row // LS % HA, row % LS
    out["as_mask"] = np.where(np.arange(LS)[None] < row_q[:, None], f(0), f(MASKED)).astype(f)
    out["as_sel"] = (row_s[:, None] * LS + row_q[:, None] == np.arange(2 * LS)[None]).astype(f)
    out["as_own"] = (row_h[:, None] == np.arange(WA)[None] // DA).astype(f)
    level = np.zeros((P, 8, P), np.int32)
    for l in range(7):
        m = P // 2 >> l
        level[:, l] = (key // (2 * m) == other // (2 * m)) & (key // m % 2 == 0) & (other // m % 2 == 1)
    level[:, 7] = key == other
    out["level_mask"] = level
    out["own"] = (np.arange(TS)[:, None] // LS == np.arange(NS)[None, :]).astype(f)
    t = np.arange(T)
    out["reset"] = np.tile(np.where(t < TP, t % P != 0, (t - TP) % LS != 0).astype(f), (P, 1))
    lg = np.log1p(-np.exp2(-5.0 - np.arange(HC)))
    rel, rel_s = other - key, sq - sk
    out["ret_decay"] = np.stack([np.where(rel >= 0, np.exp(np.maximum(rel, 0) * g), 0) for g in lg], 1).astype(f)
    seen = (sk // LS == sq // LS) & (rel_s >= 0)
    out["ret_decay_s"] = np.stack([np.where(seen, np.exp(np.where(seen, rel_s, 0) * g), 0) for g in lg], 1).astype(f)
    i, i_s = np.arange(P), np.arange(TS) % LS
    out["ret_q"] = np.tile(np.exp((i + 1) * lg[:, None])[None], (P, 1, 1)).astype(f)
    out["ret_q_s"] = np.tile(np.exp((i_s + 1) * lg[:, None])[None], (P, 1, 1)).astype(f)
    out["ret_k"] = np.exp((P - 1 - i)[:, None] * lg[None]).astype(f)
    out["ret_k_s"] = np.exp((LS - 1 - i_s)[:, None] * lg[None]).astype(f)
    out["of_seq"] = np.tile(out["own"].T[None], (P, 1, 1)).astype(f)
    out["cos"], out["sin"] = np.cos(angle).astype(f), np.sin(angle).astype(f)
    return out


def build(nc, a, o, consts):
    dram = lambda n, s: nc.dram_tensor(n, s, F32).ap()
    q_tm = dram("q_tm", (T, WA))
    qb_fm, fb_fm, ga_fm, gb_fm = (dram(n, (WB, T)) for n in ("qb_fm", "fb_fm", "ga_fm", "gb_fm"))
    ib_tm = dram("ib_tm", (T, WB))
    tm2 = lambda t: t.rearrange("a b t h d -> (a b t) (h d)")
    k_p, v_p, k_s, v_s = (tm2(o[n]) for n in ("k_prompt", "v_prompt", "k_sample", "v_sample"))
    x_p, x_s = (a[n].rearrange("b t d -> (b t) d") for n in ("x_prompt", "x_sample"))

    def split_tm(prompt, sample):
        return lambda t, col: (prompt[t * P:t * P + P, bass.ds(col, WBLK)] if t < NT - 1
                               else sample[:, bass.ds(col, WBLK)])

    def whole_tm(x):
        return lambda t, col: x[t * P:t * P + rows_of(t), bass.ds(col, WBLK)]

    def rows_fm(x):
        tiles = x.rearrange("(r p) t -> r p t", p=P)
        return lambda row: tiles[row] if isinstance(row, int) else tiles[bass.ds(row, 1)].rearrange("a p t -> (a p) t")

    x_of = lambda t: x_p[t * P:t * P + P] if t < NT - 1 else x_s
    project_in(nc, "even", x_of, a["norm_g"][0].rearrange("(c p) -> p c", p=P), a["w_in_even"][0], [
        ("norm", 1, whole_tm(q_tm)), ("norm", 1, split_tm(k_p, k_s)), ("copy", 1, split_tm(v_p, v_s)),
        ("silu", 1, rows_fm(ga_fm)), ("silu", 1, rows_fm(qb_fm)), ("plain", 1, rows_fm(fb_fm)),
        ("copy", 1, whole_tm(ib_tm)), ("silu", 1, rows_fm(gb_fm))], consts, (a["q_norm_g"], a["k_norm_g"]))
    mix0 = dram("mix0", (WA + WB, T))
    attend_prompt(nc, q_tm, k_p, v_p, ga_fm, a["sb_logit_bias"], mix0, consts)
    attend_samples(nc, q_tm, k_s, v_s, ga_fm, a["sb_logit_bias"], a["cache_k"][0], a["cache_v"][0], a["page_table"],
                   mix0, consts)
    hgrn(nc, qb_fm, fb_fm, ib_tm, gb_fm, a["hgrn_lower_bounds"], a["hgrn_out_norm_g"][0], a["state_hgrn"][0],
         o["hgrn_prompt"][0, 0], o["hgrn_sample"][0], mix0, consts)
    tile = lambda prompt, sample: lambda t: sample if isinstance(t, int) and t == NT - 1 else prompt[bass.ds(t * P, P)]
    y1 = dram("y1", (T, D))
    project_out(nc, "out0", mix0, a["w_out_even"][0], tile(x_p, x_s), tile(y1, y1[TP:T]))

    q1_fm, k1_fm = dram("q1_fm", (HC * DK, T)), dram("k1_fm", (HC * DK, T))
    v1_tm, g1_tm = dram("v1_tm", (T, WC)), dram("g1_tm", (T, WC))

    def head_fm(x):
        return lambda row: x.rearrange("(h r) t -> h r t", r=DK)[bass.ds(row, 1)].rearrange("a (j p) t -> p (a j) t", p=P)

    npair = HC * DK // (2 * WBLK)
    project_in(nc, "odd", lambda t: y1[t * P:t * P + rows_of(t)], a["norm_g"][1].rearrange("(c p) -> p c", p=P),
               a["w_in_odd"][0], [("rotary", npair, head_fm(q1_fm)), ("rotary", npair, head_fm(k1_fm)),
                                  ("copy", WC // (2 * WBLK), whole_tm(v1_tm)), ("silu_tm", WC // (2 * WBLK), whole_tm(g1_tm))], consts)
    mix1 = dram("mix1", (WC, T))
    retention(nc, q1_fm, k1_fm, v1_tm, g1_tm, a["state_ret"][0], o["ret_prompt"][0, 0], o["ret_sample"][0], mix1, consts)
    y_p, y_s = (o[n].rearrange("b t d -> (b t) d") for n in ("y_prompt", "y_sample"))
    project_out(nc, "out1", mix1, a["w_out_odd"][0], tile(y1, y1[TP:T]), tile(y_p, y_s))


def make(nc, arrays):
    a = {n: nc.dram_tensor(f"in_{n}", arrays[f"in_{n}"].shape, mybir.dt.from_np(arrays[f"in_{n}"].dtype),
                           kind="ExternalInput").ap() for n in INPUTS}
    consts = {n[6:]: nc.dram_tensor(n, v.shape, mybir.dt.from_np(v.dtype), kind="ExternalInput").ap()
              for n, v in arrays.items() if n.startswith("table_")}
    o = {n: nc.dram_tensor(f"out_{n}", s, F32, kind="ExternalOutput").ap() for n, s in OUTPUTS.items()}
    build(nc, a, o, consts)


def layout(inputs):
    arrays = {f"in_{n}": np.ascontiguousarray(inputs[n]) for n in INPUTS}
    arrays |= {f"table_{n}": v for n, v in shape_tables().items()}
    return arrays


def kernel(**inputs):
    import concourse.bacc as bacc
    from concourse.bass_utils import run_bass_kernel_spmd

    nc = bacc.Bacc("TRN2", target_bir_lowering=False, num_devices=1)
    arrays = layout(inputs)
    make(nc, arrays)
    got = run_bass_kernel_spmd(nc, [arrays], core_ids=[0]).results[0]
    return tuple(got[f"out_{n}"] for n in OUTPUTS)
```

```python
from contextlib import ExitStack, contextmanager

import numpy as np

import concourse.bass as bass
from concourse import mybir

F32 = mybir.dt.float32
F32R = mybir.dt.float32r
I32 = mybir.dt.int32
ACT = mybir.ActivationFunctionType
ALU = mybir.AluOpType
AX_X = mybir.AxisListType.X

P = 128
D = 1024
KD = D // P
TP = 1024
NS, LS = 8, 8
TS = NS * LS
T = TP + TS
NT = TP // P + 1
HA, DA = 8, 64
WA = HA * DA
HB, DB = 4, 128
WB = HB * DB
HC, DK, DV = 4, 256, 512
WC = HC * DV
PAGE = 128
NPAGE = 8
W_EVEN = 4 * WA + 4 * WB
W_ODD = 2 * HC * DK + 2 * WC
EPS = 1e-6
MASKED = -1e30
CAP = 60.0

WBLK = 256
GROUPS = [(0, 364), (364, 362), (726, 362)]


@contextmanager
def repeat(engine, n):
    if n == 1:
        yield 0
    else:
        with engine.Fori(0, n) as i:
            yield i


def load_exp_ln(nc):
    nc.scalar.add_instruction(mybir.InstLoadActFuncSet(
        name=nc.get_next_instruction_name(), engine=mybir.EngineType.Activation, ins=[], outs=[], act_func_set_id=6))


def rows_of(t):
    return P if t < NT - 1 else TS



UNITS = {"norm": 2 * NT, "copy": 2 * NT, "silu_tm": 2 * NT, "silu": 12, "plain": 12, "rotary": 12}
BY_VECTOR = ("norm", "copy", "rotary")
NBANK = 6
NSTAGE = 3


def project_in(nc, tag, x_of, gain_dram, weight, segments, consts, qk_gain_dram=None):
    with nc.cleanup_on_exit(), ExitStack() as ctx:
        sb = lambda n, s, d=F32: ctx.enter_context(nc.sbuf_tensor(f"{tag}_{n}", s, d))
        sem = lambda n: nc.alloc_semaphore(f"{tag}_{n}")
        even = tag == "even"
        bank = [ctx.enter_context(nc.psum_tensor(f"{tag}_bank{i}", [P, 512], F32)) for i in range(NBANK)]
        turn = [ctx.enter_context(nc.psum_tensor(f"{tag}_turn{i}", [P, 4, P], F32)) for i in range(2)]

        h_hi = sb("h_hi", [P, KD, T], F32R)
        h_lo = sb("h_lo", [P, KD, T], F32R)
        x_in = sb("x_in", [P, 2, D])
        x_n = sb("x_n", [P, 2, D])
        square = sb("square", [P, D])
        ssum = sb("ssum", [P, NT])
        std = sb("std", [P, NT])
        rstd = sb("rstd", [P, NT])
        gain = sb("gain", [P, KD])
        h_f = sb("h_f", [P, 2, 4, P])
        ident = sb("ident", [P, P])
        eps = sb("eps", [P, 1])
        raw = sb("raw", [P, 2, KD // 2, WBLK])
        w_hi = sb("w_hi", [P, 2, KD, WBLK], F32R)
        w_lo = sb("w_lo", [P, 2, KD, WBLK], F32R)
        stage_tm = sb("stage_tm", [P, NSTAGE, WBLK])
        if even:
            stage_fm = sb("stage_fm", [P, 2, T])
            qk_gain = sb("qk_gain", [P, 2, DA])
            head_sq = sb("head_sq", [P, 2, WBLK])
            head_ss = sb("head_ss", [P, 2, 4])
            head_std = sb("head_std", [P, 2, 4])
            head_rstd = sb("head_rstd", [P, 2, 4])
            head_n = sb("head_n", [P, 2, WBLK])
        else:
            stage_rot = sb("stage_rot", [P, 2, 2, T])
            cos = sb("cos", [P, T])
            sin = sb("sin", [P, T])
            rot = sb("rot", [P, 4, 364])

        const_in = sem("const_in")
        x_load = [sem("x_load0"), sem("x_load1")]
        sumsq_done, std_done, rstd_done, xn_done = sem("sumsq"), sem("std"), sem("rstd"), sem("xn")
        turned, gained, hi_done, lo_done = sem("turned"), sem("gained"), sem("hi"), sem("lo")
        raw_in = [sem("raw0"), sem("raw1")]
        w_hi_done, w_split, w_used = sem("w_hi"), sem("w_split"), sem("w_used")
        w_at_hand = sem("w_at_hand")
        full = sem("full")
        free = sem("free")
        staged = sem("staged")
        left_tm = [sem(f"left_tm{i}") for i in range(NSTAGE)]
        left_fm = [sem("left_fm0"), sem("left_fm1")]
        eps_set = sem("eps_set")
        head_sq_done, head_ss_done, head_std_done, head_rstd_done, head_n_done = (
            sem("hsq"), sem("hss"), sem("hstd"), sem("hrstd"), sem("hn"))

        NBLK = 2 * sum(n for _, n, _ in segments)
        NCONST = 16 * 4
        w_rows = weight.rearrange("(c p) n -> p c n", p=P)
        block = ctx.enter_context(nc.Block())

        def starts():
            at = dict(unit=0, tm=0, fm=0, norm=0, staged=0)
            for kind, n, place in segments:
                yield kind, n, place, dict(at)
                at["unit"] += n * UNITS[kind]
                at["tm"] += n * UNITS[kind] * (kind in ("norm", "copy", "silu_tm"))
                at["fm"] += {"silu": 4, "plain": 4, "rotary": 2}.get(kind, 0) * n
                at["norm"] += n * UNITS[kind] * (kind == "norm")
                at["staged"] += {"norm": UNITS[kind], "rotary": 12}.get(kind, 0) * n

        @block.sync
        def _(sp):
            sp.dma_start(ident[:], consts["ident"]).then_inc(const_in, 16)
            sp.dma_start(gain[:], gain_dram, allow_slow_non_contiguous=True).then_inc(const_in, 16)
            if even:
                for i in range(2):
                    sp.dma_start(qk_gain[:, i, :], qk_gain_dram[i].to_broadcast([P, DA])).then_inc(const_in, 16)
            else:
                sp.dma_start(cos[:], consts["cos"]).then_inc(const_in, 16)
                sp.dma_start(sin[:], consts["sin"]).then_inc(const_in, 16)
            for t in range(NT):
                if t >= 2:
                    sp.wait_ge(xn_done, t - 1)
                sp.dma_start(x_in[0:rows_of(t), t % 2, :], x_of(t)).then_inc(x_load[t % 2], 16)
                if t in (1, 2):
                    sp.dma_start(raw[:, t - 1, :, :], w_rows[:, 4 * (t - 1):4 * t, 0:WBLK]).then_inc(raw_in[t - 1], 16)
            with sp.Fori(1, NBLK) as b:
                for half in range(2):
                    sp.wait_ge(w_split, 2 * b + half - 1)
                    sp.dma_start(raw[:, half, :, :],
                                 w_rows[:, half * 4:half * 4 + 4, bass.ds(b * WBLK, WBLK)]).then_inc(raw_in[half], 16)

        @block.gpsimd
        def _(pool):
            pool.sem_inc(w_used, 1)
            with pool.Fori(0, NBLK // 2) as pair:
                for slot in range(2):
                    pool.wait_ge(w_used, 2 * pair + slot + 1)
                    for half in range(2):
                        r = raw[:, half, :, :]
                        hi = w_hi[:, slot, half * 4:half * 4 + 4, :]
                        lo = w_lo[:, slot, half * 4:half * 4 + 4, :]
                        pool.wait_ge(raw_in[half], 32 * pair + 16 * slot + 16)
                        pool.sem_inc(w_at_hand, 1)
                        nc.gpsimd.tensor_copy(hi, r).then_inc(w_hi_done, 1)
                        pool.wait_ge(w_hi_done, 4 * pair + 2 * slot + half + 1)
                        nc.gpsimd.tensor_tensor(lo, r, hi.bitcast(F32), ALU.subtract).then_inc(w_split, 1)

        @block.tensor
        def _(pe):
            def transpose_tile(t):
                r = rows_of(t)
                pe.wait_ge(xn_done, t + 1)
                for k in range(2):
                    if t >= 1:
                        pe.wait_ge(gained, 2 * t + k - 1)
                    for c in range(4):
                        mm = pe.transpose(turn[k][:, c, 0:r], x_n[0:r, t % 2, (4 * k + c) * P:(4 * k + c + 1) * P],
                                          ident[0:r, 0:r])
                    mm.then_inc(turned, 1)

            def product(out, pairs, opens_block):
                for j, (stationary, moving) in enumerate(pairs):
                    mm = pe.matmul(out, stationary, moving, start=(j == 0), stop=(j == len(pairs) - 1))
                    if j == 0 and opens_block:
                        mm.then_inc(w_used, 1)
                return mm.then_inc(full, 1)

            def parts(h, w):
                return ((h[0], w[0]), (h[0], w[1]), (h[1], w[0]))

            def tiles_of(kind, j):
                if kind in ("norm", "copy", "silu_tm"):
                    return j + 1
                g0, gn = GROUPS[j // 2 if kind == "rotary" else j % 3]
                return -(-(g0 + gn) // P)

            def unit(kind, at, it, s, j):
                u = s * (UNITS[kind] // 2) + j
                pe.wait_ge(free, it * UNITS[kind] + (at["unit"] + u + 1))
                if kind in ("norm", "copy", "silu_tm"):
                    tok = slice(j * P, j * P + rows_of(j))
                    out = bank[u % NBANK][0:rows_of(j), 0:WBLK]
                    ops = [(h, w) for c in range(KD)
                           for h, w in parts((h_hi[:, c, tok], h_lo[:, c, tok]), (w_hi[:, s, c, :], w_lo[:, s, c, :]))]
                else:
                    g, f = (j // 2, j % 2) if kind == "rotary" else (j % 3, j // 3)
                    g0, gn = GROUPS[g]
                    out = bank[u % NBANK][:, 0:gn]
                    cols = slice(f * P, f * P + P)
                    ops = [(w, h) for c in range(KD)
                           for h, w in parts((h_hi[:, c, g0:g0 + gn], h_lo[:, c, g0:g0 + gn]),
                                             (w_hi[:, s, c, cols], w_lo[:, s, c, cols]))]
                product(out, ops, j == 0)

            pe.sem_inc(free, NBANK)
            pe.wait_ge(const_in, NCONST)
            first, first_n, _, first_at = next(starts())
            assert first_n == 1
            early = 0
            for t in range(NT):
                transpose_tile(t)
                while early < min(NBANK, UNITS[first] // 2) and tiles_of(first, early) <= t - 1:
                    if early == 0:
                        pe.wait_ge(w_split, 2)
                    pe.wait_ge(lo_done, 2 * tiles_of(first, early))
                    unit(first, first_at, 0, 0, early)
                    early += 1
            pe.wait_ge(lo_done, 2 * NT)

            pairs_before, was_by_vector = 0, True
            for kind, n, _, at in starts():
                if (kind in BY_VECTOR) != was_by_vector:
                    pe.wait_ge(free, at["unit"] + NBANK)
                was_by_vector = kind in BY_VECTOR
                with repeat(pe, n) as it:
                    for s in range(2):
                        pe.wait_ge(w_split, 4 * it + 4 * pairs_before + 2 * s + 2)
                        for j in range(UNITS[kind] // 2):
                            if pairs_before or s or j >= early:
                                unit(kind, at, it, s, j)
                pairs_before += n

        @block.scalar
        def _(act):
            for i in range(NSTAGE):
                act.sem_inc(left_tm[i], 16)
            for i in range(2):
                act.sem_inc(left_fm[i], 16)

            def cast_hi(t, k):
                r = rows_of(t)
                act.wait_ge(gained, 2 * t + k + 1)
                nc.scalar.copy(h_hi[:, 4 * k:4 * k + 4, t * P:t * P + r], h_f[:, k, :, 0:r]).then_inc(hi_done, 1)

            act.wait_ge(eps_set, 1)
            for t in range(NT):
                r = rows_of(t)
                act.wait_ge(x_load[t % 2], 16 * (t // 2 + 1))
                nc.scalar.activation(square[0:r, :], x_in[0:r, t % 2, :], ACT.Square,
                                     accum_out=ssum[0:r, t:t + 1]).then_inc(sumsq_done, 1)
                act.wait_ge(sumsq_done, t + 1)
                nc.scalar.activation(std[0:r, t:t + 1], ssum[0:r, t:t + 1], ACT.Sqrt,
                                     bias=eps[0:r, :], scale=1.0 / D).then_inc(std_done, 1)
                if t >= 1:
                    cast_hi(t - 1, 0)
                    cast_hi(t - 1, 1)
            cast_hi(NT - 1, 0)
            cast_hi(NT - 1, 1)

            for kind, n, place, at in starts():
                with repeat(act, n) as it:
                    for u in range(UNITS[kind]):
                        s, j = divmod(u, UNITS[kind] // 2)
                        r = rows_of(j) if kind in ("norm", "copy", "silu_tm") else P
                        src = bank[u % NBANK]
                        this = it * UNITS[kind] + (at["unit"] + u + 1)
                        slot = u % NSTAGE
                        if kind == "norm":
                            nth = it * UNITS[kind] + (at["norm"] + u + 1)
                            act.wait_ge(full, this)
                            act.wait_ge(head_ss_done, nth)
                            nc.scalar.activation(head_sq[0:r, u % 2, :], src[0:r, 0:WBLK], ACT.Square).then_inc(head_sq_done, 1)
                            act.wait_ge(head_ss_done, nth + 2)
                            nc.scalar.activation(head_std[0:r, u % 2, :], head_ss[0:r, u % 2, :], ACT.Sqrt,
                                                 bias=eps[0:r, :], scale=1.0 / DA).then_inc(head_std_done, 1)
                            act.wait_ge(staged, it * UNITS[kind] + (at["staged"] + u + 1) + 1)
                        elif kind == "copy":
                            act.wait_ge(free, this + NBANK)
                        elif kind == "silu_tm":
                            act.wait_ge(full, this)
                            act.wait_ge(left_tm[slot], it * (16 * UNITS[kind] // NSTAGE) + 16 * ((at["tm"] + u) // NSTAGE) + 16)
                            nc.scalar.activation(stage_tm[0:r, slot, :], src[0:r, 0:WBLK], ACT.Silu).then_inc(free, 1)
                            act.wait_ge(free, this + NBANK)
                        if kind in ("norm", "copy", "silu_tm"):
                            act.dma_start(place(j, it * 2 * WBLK + s * WBLK), stage_tm[0:r, slot, :]).then_inc(left_tm[slot], 16)
                        if kind in ("silu", "plain"):
                            f, g = j // 3, j % 3
                            row = 2 * s + f
                            slot = row % 2
                            g0, gn = GROUPS[g]
                            act.wait_ge(full, this)
                            if g == 0:
                                act.wait_ge(left_fm[slot], it * 32 + 16 * ((at["fm"] + row) // 2) + 16)
                            nc.scalar.activation(stage_fm[:, slot, g0:g0 + gn], src[:, 0:gn],
                                                 ACT.Silu if kind == "silu" else ACT.Copy).then_inc(free, 1)
                            if g == 2:
                                act.wait_ge(free, this + NBANK)
                                act.dma_start(place(it * 4 + row), stage_fm[:, slot, :]).then_inc(left_fm[slot], 16)
                        if kind == "rotary" and j == 5:
                            act.wait_ge(staged, it * 12 + (at["staged"] + 6 * s + 6) + 1)
                            act.dma_start(place(it * 2 + s), stage_rot[:, s, :, :]).then_inc(left_fm[s], 16)
            tm = sum(n * UNITS[k] for k, n, _ in segments if k in ("norm", "copy", "silu_tm"))
            fm = sum(n * {"silu": 4, "plain": 4, "rotary": 2}.get(k, 0) for k, n, _ in segments)
            for i in range(NSTAGE):
                act.wait_ge(left_tm[i], 16 * (tm // NSTAGE) + 16)
            for i in range(2):
                act.wait_ge(left_fm[i], 16 * (fm // 2) + 16)

        @block.vector
        def _(dve):
            nc.vector.memset(eps[:], EPS).then_inc(eps_set, 1)
            dve.sem_inc(head_ss_done, 2)
            dve.sem_inc(staged, 1)

            def gain_and_split(t):
                r = rows_of(t)
                for k in range(2):
                    dve.wait_ge(turned, 2 * t + k + 1)
                    if t >= 1:
                        dve.wait_ge(lo_done, 2 * t + k - 1)
                        dve.wait_ge(hi_done, 2 * t + k - 1)
                    dve.tensor_tensor(h_f[:, k, :, 0:r], turn[k][:, :, 0:r],
                                      gain[:, 4 * k:4 * k + 4].unsqueeze(2).to_broadcast([P, 4, r]), ALU.mult).then_inc(gained, 1)
                for k in range(2):
                    hi = h_hi[:, 4 * k:4 * k + 4, t * P:t * P + r]
                    dve.wait_ge(hi_done, 2 * t + k + 1)
                    dve.tensor_tensor(h_lo[:, 4 * k:4 * k + 4, t * P:t * P + r], h_f[:, k, :, 0:r],
                                      hi.bitcast(F32), ALU.subtract).then_inc(lo_done, 1)

            dve.wait_ge(const_in, NCONST)
            for t in range(NT):
                r = rows_of(t)
                dve.wait_ge(std_done, t + 1)
                dve.reciprocal(rstd[0:r, t:t + 1], std[0:r, t:t + 1]).then_inc(rstd_done, 1)
                dve.wait_ge(rstd_done, t + 1)
                if t >= 2:
                    dve.wait_ge(turned, 2 * t - 2)
                dve.tensor_scalar(x_n[0:r, t % 2, :], x_in[0:r, t % 2, :], rstd[0:r, t:t + 1], None,
                                  ALU.mult).then_inc(xn_done, 1)
                if t >= 1:
                    gain_and_split(t - 1)
            gain_and_split(NT - 1)

            norm_segments = 0
            for kind, n, _, at in starts():
                if kind in ("silu", "silu_tm", "plain"):
                    continue
                with repeat(dve, n) as it:
                    for u in range(UNITS[kind]):
                        s, j = divmod(u, UNITS[kind] // 2)
                        r = rows_of(j) if kind != "rotary" else P
                        src = bank[u % NBANK]
                        this = it * UNITS[kind] + (at["unit"] + u + 1)
                        slot = u % NSTAGE
                        slot_left = it * (16 * UNITS[kind] // NSTAGE) + 16 * ((at["tm"] + u) // NSTAGE) + 16
                        if kind == "norm":
                            nth = it * UNITS[kind] + (at["norm"] + u + 1)
                            heads = lambda x: x.rearrange("p (h d) -> p h d", d=DA)
                            dve.wait_ge(head_sq_done, nth)
                            dve.tensor_reduce(head_ss[0:r, u % 2, :], heads(head_sq[0:r, u % 2, :]), AX_X, ALU.add).then_inc(head_ss_done, 1)
                            dve.wait_ge(head_std_done, nth)
                            dve.reciprocal(head_rstd[0:r, u % 2, :], head_std[0:r, u % 2, :]).then_inc(head_rstd_done, 1)
                            dve.wait_ge(head_rstd_done, nth)
                            dve.tensor_tensor(heads(head_n[0:r, u % 2, :]), heads(src[0:r, 0:WBLK]),
                                              head_rstd[0:r, u % 2, :].unsqueeze(2).to_broadcast([r, 4, DA]), ALU.mult).then_inc(free, 1)
                            dve.wait_ge(free, this + NBANK)
                            dve.wait_ge(left_tm[slot], slot_left)
                            dve.tensor_tensor(heads(stage_tm[0:r, slot, :]), heads(head_n[0:r, u % 2, :]),
                                              qk_gain[0:r, norm_segments, :].unsqueeze(1).to_broadcast([r, 4, DA]), ALU.mult).then_inc(staged, 1)
                        elif kind == "copy":
                            dve.wait_ge(full, this)
                            dve.wait_ge(left_tm[slot], slot_left)
                            dve.tensor_copy(stage_tm[0:r, slot, :], src[0:r, 0:WBLK]).then_inc(free, 1)
                        elif j % 2 == 1:
                            g0, gn = GROUPS[j // 2]
                            scale = 1.0 if at["unit"] < HC * DK // (2 * WBLK) * UNITS[kind] else DK ** -0.5
                            c, sn = cos[:, g0:g0 + gn], sin[:, g0:g0 + gn]
                            x1, x2 = bank[(u - 1) % NBANK][:, 0:gn], src[:, 0:gn]
                            before = it * 12 + (at["staged"] + 6 * s + (j // 2) * 2)
                            dve.wait_ge(full, this)
                            dve.wait_ge(staged, before + 1)
                            dve.scalar_tensor_tensor(rot[:, 0, 0:gn], x1, scale, c, ALU.mult, ALU.mult)
                            dve.scalar_tensor_tensor(rot[:, 1, 0:gn], x1, scale, sn, ALU.mult, ALU.mult).then_inc(free, 1)
                            dve.scalar_tensor_tensor(rot[:, 2, 0:gn], x2, scale, sn, ALU.mult, ALU.mult)
                            dve.scalar_tensor_tensor(rot[:, 3, 0:gn], x2, scale, c, ALU.mult, ALU.mult).then_inc(free, 1)
                            dve.wait_ge(free, this + NBANK)
                            if j == 1:
                                dve.wait_ge(left_fm[s], it * 16 + 16 * (at["fm"] // 2) + 16)
                            dve.tensor_tensor(stage_rot[:, s, 0, g0:g0 + gn], rot[:, 0, 0:gn], rot[:, 2, 0:gn], ALU.subtract).then_inc(staged, 1)
                            dve.tensor_tensor(stage_rot[:, s, 1, g0:g0 + gn], rot[:, 3, 0:gn], rot[:, 1, 0:gn], ALU.add).then_inc(staged, 1)
                if kind == "norm":
                    norm_segments += 1



class Pages:

    def __init__(self, nc, ctx, cache_k, cache_v, page_table):
        sb = lambda n, s, d=F32: ctx.enter_context(nc.sbuf_tensor(n, s, d))
        self.NU = 2 * NPAGE
        self.table = sb("page_table", [1, NS * NPAGE], I32)
        self.k = [sb(f"k_page{i}", [P, self.NU, WA]) for i in range(2)]
        self.v = [sb(f"v_page{i}", [P, self.NU, WA]) for i in range(2)]
        self.table_in = nc.alloc_semaphore("table_in")
        self.k_in = [[nc.alloc_semaphore(f"k_in{i}{g}") for g in range(NPAGE)] for i in range(2)]
        self.v_in = [nc.alloc_semaphore(f"v_in{i}") for i in range(2)]
        self.page_table = page_table
        self.cache_k, self.cache_v = (c.rearrange("g t h d -> g t (h d)") for c in (cache_k, cache_v))

    def load_table(self, sp):
        sp.dma_start(self.table[:], self.page_table.rearrange("(a b) n -> a (b n)", a=1)).then_inc(self.table_in, 16)
        sp.wait_ge(self.table_in, 16)

    def load(self, sp, step, keys):
        i = step % 2
        cache, dst = (self.cache_k, self.k[i]) if keys else (self.cache_v, self.v[i])
        for u in range(self.NU):
            entry = (2 * step + u % 2) * NPAGE + u // 2
            page = sp.value_load(self.table[0:1, entry:entry + 1], min_val=0, max_val=cache.shape[0] - 1)
            sp.dma_start(dst[:, u, :], cache[bass.ds(page, 1)].rearrange("a t n -> (a t) n")).then_inc(
                self.k_in[i][u // 2] if keys else self.v_in[i], 16)


def attend(nc, q_tm, k_prompt, v_prompt, k_samples, v_samples, gate_fm, bias_dram, cache_k, cache_v, page_table, mix_fm, consts):
    with nc.cleanup_on_exit(), ExitStack() as ctx:
        pages = Pages(nc, ctx, cache_k, cache_v, page_table)
        attend_prompt(nc, q_tm, k_prompt, v_prompt, gate_fm, bias_dram, mix_fm, consts, pages)
        attend_samples(nc, q_tm, k_samples, v_samples, gate_fm, bias_dram, mix_fm, consts, pages)



def attend_prompt(nc, q_tm, k_tm, v_tm, gate_fm, bias_dram, mix_fm, consts, pages):
    with nc.cleanup_on_exit(), ExitStack() as ctx:
        sb = lambda n, s, d=F32: ctx.enter_context(nc.sbuf_tensor(f"ap_{n}", s, d))
        sem = lambda n: nc.alloc_semaphore(f"ap_{n}")
        NQ = 512
        NZ, NK, NC, LAG = 6, 3, 5, 4
        PV = LAG + 2
        z = [ctx.enter_context(nc.psum_tensor(f"ap_z{i}", [P, NQ], F32)) for i in range(NZ)]
        o = [ctx.enter_context(nc.psum_tensor(f"ap_o{i}", [P, NQ], F32)) for i in range(2)]
        turn = [x[:].rearrange("p (c n) -> p c n", n=P) for x in z]
        ident, tri, minus, mask = sb("ident", [P, P]), sb("tri", [P, P]), sb("minus", [P, P]), sb("mask", [P, P])
        qk_in = sb("qk_in", [P, 2, 8, P])
        v_in, v = sb("v_in", [P, 8, P]), sb("v", [P, 8, P])
        gate = sb("gate", [P, TP])
        qk_hi, qk_lo = sb("qk_hi", [P, 2, TP], F32R), sb("qk_lo", [P, 2, TP], F32R)
        tri_r = sb("tri_r", [P, P], F32R)
        biases = sb("biases", [P, HA])
        bias = sb("bias", [P, 2])
        soft = sb("soft", [P, NK, NQ])
        drop, carry = sb("drop", [P, NK, NQ]), sb("carry", [P, NC, NQ])
        k_hi, k_lo = sb("k_hi", [P, NK, NQ], F32R), sb("k_lo", [P, NK, NQ], F32R)
        w = sb("w", [P, 3, NQ])

        head_steps = [(1, kb, max(0, kb - 4) * P) for kb in range(7, -1, -1)] + [(0, kb, kb * P) for kb in range(3, -1, -1)]
        steps = [(e, half, kb, lo) for e in range(2) for half, kb, lo in head_steps]
        NSTEP = len(steps)
        opens = [kb == (7 if half else 3) for _, half, kb, _ in steps]
        closes = [kb == 0 for _, _, kb, _ in steps]
        run = [2 * e + 1 - half for e, half, _, _ in steps]
        run_end = [i + 1 for i in range(NSTEP) if closes[i]]

        const_in = sem("const_in")
        qk_load, v_load, gate_load = sem("qk_load"), sem("v_load"), sem("gate_load")
        turned, turn_hi, turn_read, tri_split = sem("turned"), sem("turn_hi"), sem("turn_read"), sem("tri_split")
        drop_hi, drop_split = sem("drop_hi"), sem("drop_split")
        v_held, bias_held = sem("v_held"), sem("bias_held")
        logits, capped, exp_done, soft_done = sem("logits"), sem("capped"), sem("exp"), sem("soft")
        drop_done, carry_done, minus_set = sem("drop"), sem("carry"), sem("minus_set")
        summed, w_done, pv_done = sem("summed"), sem("w"), sem("pv")
        mixed, mix_left = sem("mixed"), sem("mix_left")
        block = ctx.enter_context(nc.Block())
        NPAIR = HA // 2
        v_tiles = v_tm.rearrange("(t p) n -> p t n", p=P)
        q_tiles = q_tm[0:TP].rearrange("(t p) n -> p t n", p=P)
        k_tiles = k_tm.rearrange("(t p) n -> p t n", p=P)

        def turned_to(x, i):
            return x[:, i // 2, 4 * (i % 2) * P:4 * (i % 2 + 1) * P].rearrange("p (c n) -> p c n", n=P)

        @block.sync
        def _(sp):
            for dst, name in ((ident, "ident"), (tri, "tri"), (mask, "mask")):
                sp.dma_start(dst[:], consts[name]).then_inc(const_in, 16)
            sp.dma_start(biases[:], bias_dram.to_broadcast([P, HA])).then_inc(const_in, 16)
            for p in range(NPAIR):
                cols = slice(p * P, p * P + P)
                sp.wait_ge(turned, 4 * p + 1)
                sp.dma_start(qk_in[:, 0, :, :], q_tiles[:, :, cols]).then_inc(qk_load, 16)
                sp.dma_start(qk_in[:, 1, :, :], k_tiles[:, :, cols]).then_inc(qk_load, 16)
                sp.wait_ge(v_held, p + 1)
                sp.dma_start(v_in[:], v_tiles[:, :, cols]).then_inc(v_load, 16)
                sp.wait_ge(mixed, 4 * p + 2)
                sp.wait_ge(mix_left, 16 * p + 16)
                sp.dma_start(gate[:], gate_fm[cols, 0:TP]).then_inc(gate_load, 16)
                if p == 0:
                    pages.load_table(sp)
                pages.load(sp, p % 2, keys=p < 2)
            sp.wait_ge(mix_left, 16 * NPAIR + 16)

        @block.gpsimd
        def _(pool):
            with pool.Fori(0, NPAIR) as p:
                for i in range(NSTEP):
                    lo, m = steps[i][3], i % NK
                    pool.wait_ge(drop_done, NSTEP * p + i + 2)
                    pool.wait_ge(drop_hi, NSTEP * p + i + 1)
                    nc.gpsimd.tensor_tensor(k_lo[:, m, lo:NQ], drop[:, m, lo:NQ], k_hi[:, m, lo:NQ].bitcast(F32),
                                            ALU.subtract).then_inc(drop_split, 1)

        @block.tensor
        def _(pe):
            pe.sem_inc(turned, 1)
            pe.sem_inc(pv_done, 1)
            pe.sem_inc(summed, 1)
            pe.wait_ge(const_in, 64)
            pe.wait_ge(tri_split, 1)
            pe.wait_ge(minus_set, 1)
            with pe.Fori(0, NPAIR) as p:
                pe.wait_ge(qk_load, 32 * p + 32)
                for i in range(4):
                    pe.wait_ge(w_done, NSTEP * p + NZ)
                    for c in range(4):
                        mm = pe.transpose(turn[i][:, c, :], qk_in[:, i // 2, 4 * (i % 2) + c, :], ident[:])
                    mm.then_inc(turned, 1)
                pe.wait_ge(turn_read, 4 * p + 4)
                pe.wait_ge(v_held, p + 2)
                for i in range(NSTEP + PV):
                    if i < NSTEP:
                        e, half, kb, lo = steps[i]
                        rows = slice(DA * e, DA * e + DA)
                        pe.wait_ge(w_done, NSTEP * p + i + 1)
                        diagonal = kb >= 4 * half
                        keys, queries = slice(kb * P, kb * P + P), slice(half * NQ + lo, (half + 1) * NQ)
                        for j, (kk, qq) in enumerate(((qk_hi, qk_hi), (qk_hi, qk_lo), (qk_lo, qk_hi))):
                            mm = pe.matmul(z[i % NZ][:, lo:NQ], kk[rows, 1, keys], qq[rows, 0, queries], start=(j == 0), stop=(j == 2))
                        if diagonal:
                            mm = pe.matmul(z[i % NZ][:, lo:lo + P], ident[:], mask[:], start=False, stop=True,
                                           skip_group_check=True)
                        mm.then_inc(logits, 1)
                    j = i - LAG
                    if 0 <= j < NSTEP:
                        lo = steps[j][3]
                        pe.wait_ge(drop_split, NSTEP * p + j + 1)
                        for part in (k_hi, k_lo):
                            mm = pe.matmul(z[j % NZ][:, lo:NQ], tri_r[:], part[:, j % NK, lo:NQ], start=False, stop=True,
                                           skip_group_check=True)
                        if not opens[j]:
                            before = steps[j - 1][3]
                            pe.wait_ge(carry_done, NSTEP * p + j)
                            mm = pe.matmul(z[j % NZ][:, before:NQ], minus[:], carry[:, (j - 1) % NC, before:NQ],
                                           start=False, stop=True, skip_group_check=True)
                        mm.then_inc(summed, 1)
                    j = i - PV
                    if 0 <= j < NSTEP:
                        e, half, kb, lo = steps[j]
                        rows = slice(DA * e, DA * e + DA)
                        pe.wait_ge(w_done, NSTEP * p + (j + 1 + NZ))
                        if opens[j]:
                            pe.wait_ge(mixed, 4 * p + run[j] + 1)
                        pe.matmul(o[run[j] % 2][rows, lo:NQ], v[:, kb, rows], w[:, j % 3, lo:NQ], start=opens[j],
                                  stop=closes[j], skip_group_check=True).then_inc(pv_done, 1)

        @block.scalar
        def _(act):
            load_exp_ln(nc)
            act.sem_inc(w_done, NZ)
            act.wait_ge(const_in, 64)
            nc.scalar.activation(tri_r[:], tri[:], ACT.Copy, scale=-1.0).then_inc(tri_split, 1)
            with act.Fori(0, NPAIR) as p:
                for i in range(4):
                    act.wait_ge(turned, 4 * p + i + 2)
                    if i == 0:
                        act.wait_ge(pv_done, NSTEP * p + 1)
                    nc.scalar.activation(turned_to(qk_hi, i), turn[i], ACT.Copy, scale=DA ** -0.5 if i < 2 else 1.0).then_inc(turn_hi, 1)
                act.wait_ge(bias_held, p + 1)
                for i in range(NSTEP + LAG):
                    if i < NSTEP:
                        at = soft[:, i % NK, steps[i][3]:NQ]
                        act.wait_ge(capped, NSTEP * p + i + 1)
                        nc.scalar.activation(at, at, ACT.Exp).then_inc(exp_done, 1)
                        act.wait_ge(exp_done, NSTEP * p + i + 1)
                        nc.scalar.activation(at, at, ACT.Ln, bias=1.0).then_inc(soft_done, 1)
                    j = i - LAG
                    if j >= 0:
                        e, _, _, lo = steps[j]
                        act.wait_ge(summed, NSTEP * p + j + 2)
                        act.wait_ge(pv_done, NSTEP * p + max(0, j - 2) + 1)
                        nc.scalar.activation(w[:, j % 3, lo:NQ], z[j % NZ][:, lo:NQ], ACT.Exp,
                                             bias=bias[:, e:e + 1]).then_inc(w_done, 1)
                    j = i - 1
                    if 0 <= j < NSTEP:
                        lo = steps[j][3]
                        act.wait_ge(drop_done, NSTEP * p + j + 2)
                        act.wait_ge(summed, NSTEP * p + max(0, j - NK + 1) + 1)
                        nc.scalar.copy(k_hi[:, j % NK, lo:NQ], drop[:, j % NK, lo:NQ]).then_inc(drop_hi, 1)
                act.wait_ge(mixed, 4 * p + 4 + 2)
                act.dma_start(mix_fm[bass.ds(p * P, P), 0:TP], gate[:]).then_inc(mix_left, 16)

        @block.vector
        def _(dve):
            nc.vector.memset(minus[:], -1.0).then_inc(minus_set, 1)
            dve.sem_inc(mixed, 2)
            dve.sem_inc(v_held, 1)
            dve.sem_inc(drop_done, 1)
            dve.sem_inc(mix_left, 16)
            dve.wait_ge(const_in, 64)
            with dve.Fori(0, NPAIR) as p:
                dve.wait_ge(v_load, 16 * p + 16)
                dve.wait_ge(pv_done, NSTEP * p + 1)
                dve.tensor_copy(v[:], v_in[:]).then_inc(v_held, 1)
                dve.wait_ge(w_done, NSTEP * p + NZ)
                dve.tensor_copy(bias[:], biases[:, bass.ds(2 * p, 2)]).then_inc(bias_held, 1)
                for i in range(4):
                    hi = turned_to(qk_hi, i).bitcast(F32)
                    dve.wait_ge(turn_hi, 4 * p + i + 1)
                    dve.scalar_tensor_tensor(turned_to(qk_lo, i), turn[i], DA ** -0.5 if i < 2 else 1.0, hi,
                                             ALU.mult, ALU.subtract).then_inc(turn_read, 1)
                dve.wait_ge(bias_held, p + 1)
                for i in range(NSTEP + PV):
                    if i < NSTEP:
                        e, _, _, lo = steps[i]
                        dve.wait_ge(logits, NSTEP * p + i + 1)
                        dve.wait_ge(drop_done, NSTEP * p + max(0, i - NK + 1) + 1)
                        dve.tensor_scalar(soft[:, i % NK, lo:NQ], z[i % NZ][:, lo:NQ], bias[:, e:e + 1], CAP,
                                          ALU.add, ALU.min).then_inc(capped, 1)
                    j = i - 1
                    if 0 <= j < NSTEP:
                        e, _, _, lo = steps[j]
                        dve.wait_ge(soft_done, NSTEP * p + j + 1)
                        dve.wait_ge(drop_split, NSTEP * p + j - NK + 1) if j >= NK else dve.wait_ge(summed, NSTEP * p + 1)
                        dve.scalar_tensor_tensor(drop[:, j % NK, lo:NQ], z[j % NZ][:, lo:NQ], bias[:, e:e + 1], soft[:, j % NK, lo:NQ],
                                                 ALU.add, ALU.max).then_inc(drop_done, 1)
                        dve.wait_ge(drop_done, NSTEP * p + j + 2)
                        dve.wait_ge(summed, NSTEP * p + max(0, j - NC + 2) + 1)
                        if opens[j]:
                            dve.tensor_copy(carry[:, j % NC, lo:NQ], drop[:, j % NK, lo:NQ]).then_inc(carry_done, 1)
                        else:
                            before = steps[j - 1][3]
                            dve.wait_ge(carry_done, NSTEP * p + j)
                            if lo < before:
                                dve.tensor_copy(carry[:, j % NC, lo:before], drop[:, j % NK, lo:before])
                            dve.tensor_tensor(carry[:, j % NC, before:NQ], carry[:, (j - 1) % NC, before:NQ],
                                              drop[:, j % NK, before:NQ], ALU.add).then_inc(carry_done, 1)
                    j = i - PV
                    if j >= 0 and closes[j]:
                        e, half, _, _ = steps[j]
                        rows = slice(DA * e, DA * e + DA)
                        cols = slice(half * NQ, half * NQ + NQ)
                        dve.wait_ge(pv_done, NSTEP * p + j + 2)
                        if run[j] == 0:
                            dve.wait_ge(gate_load, 16 * p + 16)
                            dve.wait_ge(mix_left, 16 * p + 16)
                        dve.tensor_tensor(gate[rows, cols], o[run[j] % 2][rows, :], gate[rows, cols], ALU.mult).then_inc(mixed, 1)



def attend_samples(nc, q_tm, k_tm, v_tm, gate_fm, bias_dram, mix_fm, consts, pages):
    with nc.cleanup_on_exit(), ExitStack() as ctx:
        sb = lambda n, s, d=F32: ctx.enter_context(nc.sbuf_tensor(f"as_{n}", s, d))
        sem = lambda n: nc.alloc_semaphore(f"as_{n}")
        ps = lambda n, s: ctx.enter_context(nc.psum_tensor(f"as_{n}", s, F32))
        HP = HA // 2
        ROWS, NU = HA * LS, 2 * NPAGE
        PAST = NPAGE * PAGE
        ALL = PAST + LS
        z = [[ps(f"z{i}{j}", [P, 512]) for j in range(2)] for i in range(2)]
        turn = [ps("turn0", [P, HP, P]), ps("turn1", [P, HP, P])]
        o = ps("o", [P, WA])
        small = ps("small", [P, 512])
        ident, ones = sb("ident", [P, P]), sb("ones", [P, P])
        mask, sel, own = sb("mask", [P, LS]), sb("sel", [P, 2 * LS]), sb("own", [P, WA])
        biases, bias_row, bias = sb("biases", [1, HA]), sb("bias_row", [1, 2, HA, LS]), sb("bias", [P, 1])
        qk_in = sb("qk_in", [TS, 2, WA])
        qT, kT_new = sb("qT", [P, HP, TS]), sb("kT_new", [P, HP, TS])
        q_now = [sb(f"q_now{i}", [P, HP * (2 * P + 2 * LS)]) for i in range(2)]
        gate, mix = sb("gate", [P, HP, TS]), sb("mix", [P, HP, TS])
        k_page, v_page, k_in, v_in = pages.k, pages.v, pages.k_in, pages.v_in
        v_new = [sb(f"v_new{i}", [LS, 2, WA]) for i in range(2)]
        kT = sb("kT", [P, 4, HP, P])
        soft = [sb(f"soft{i}", [P, ALL]) for i in range(2)]
        keep = [sb(f"keep{i}", [P, ALL]) for i in range(2)]
        w = sb("w", [P, ALL])
        zm = [sb(f"zm{i}", [P, LS]) for i in range(2)]
        wT, wT_new = sb("wT", [P, NPAGE, P]), sb("wT_new", [LS, P])
        mine = sb("mine", [P, WA])

        first_in, const_in = sem("first_in"), sem("const_in")
        prep, new_in = sem("prep"), [sem("new_in0"), sem("new_in1")]
        new_turned, new_held = sem("new_turned"), sem("new_held")
        cleared, q_set = sem("cleared"), sem("q_set")
        turned = sem("turned")
        held_a, held_d = sem("held_a"), sem("held_d")
        page_logits = sem("page_logits")
        new_logits = sem("new_logits")
        small_read = sem("small_read")
        soft_step, keep_step = sem("soft_step"), sem("keep_step")
        outputs, mined, mix_left = sem("outputs"), sem("mined"), sem("mix_left")
        block = ctx.enter_context(nc.Block())
        NFIRST, NCONST = 16 * 5, 16 * 4
        NTURN = NS // 4

        @block.sync
        def _(sp):
            for i, x in enumerate((q_tm[TP:T], k_tm)):
                sp.dma_start(qk_in[:, i, :], x).then_inc(first_in, 16)
            for dst, name in ((ident, "ident"), (ones, "ones")):
                sp.dma_start(dst[:], consts[name]).then_inc(first_in, 16)
            sp.dma_start(biases[:], bias_dram).then_inc(first_in, 16)
            for dst, name in ((mask, "as_mask"), (sel, "as_sel"), (own, "as_own")):
                sp.dma_start(dst[:], consts[name]).then_inc(const_in, 16)
            sp.dma_start(gate[:], gate_fm[:, TP:T].rearrange("(c p) t -> p c t", p=P)).then_inc(const_in, 16)
            for n in range(NS // 2):
                i = n % 2
                if n >= 2:
                    sp.wait_ge(new_logits, n)
                    pages.load(sp, n, keys=True)
                    sp.wait_ge(outputs, n)
                    pages.load(sp, n, keys=False)
                sp.dma_start(v_new[i][:], v_tm[n * 2 * LS:(n + 1) * 2 * LS].rearrange("(s j) n -> j s n", s=2)).then_inc(new_in[i], 16)
            sp.wait_ge(small_read, 6 * NTURN + 1)
            sp.dma_start(mix_fm[0:WA, TP:T].rearrange("(c p) t -> p c t", p=P), mix[:]).then_inc(mix_left, 16)
            sp.wait_ge(mix_left, 16)

        @block.gpsimd
        def _(pool):
            for i in range(2):
                nc.gpsimd.memset(q_now[i][:], 0.0).then_inc(cleared, 1)
            pool.wait_ge(cleared, 2)
            pool.wait_ge(new_held, 1)
            with pool.Fori(0, NTURN) as it:
                for i in range(2):
                    pool.wait_ge(new_logits, 2 * it + 1)
                    for s in range(2):
                        for e in range(2):
                            rows = slice(DA * e, DA * e + DA)
                            at = s * (P + ROWS) + e * LS
                            dst = q_now[i][:].rearrange("p (c x) -> p c x", c=HP)[rows, :, at:at + LS]
                            pool.sem_inc(cleared, 1)
                            ins = nc.gpsimd.tensor_copy(dst, qT[rows, :, bass.ds((4 * it + 2 * i + s) * LS, LS)])
                    ins.then_inc(q_set, 1)

        @block.tensor
        def _(pe):
            pe.sem_inc(new_logits, 1)
            pe.sem_inc(page_logits, 4)
            pe.sem_inc(outputs, 1)
            pe.wait_ge(first_in, NFIRST)
            for i in range(2):
                for c in range(HP):
                    mm = pe.transpose(turn[i][:, c, 0:TS], qk_in[:, i, c * P:c * P + P], ident[0:TS, 0:TS])
                mm.then_inc(new_turned, 1)
            pe.wait_ge(prep, 1)
            pe.matmul(small[:, 0:LS], bias_row[:].rearrange("o s h q -> o (s h q)"), ones[0:1, 0:LS], start=True, stop=True).then_inc(prep, 1)
            pe.wait_ge(new_held, 2)

            def logits(it, i):
                n = 2 * it + i
                for u in range(NU + 1):
                    if u < NU:
                        if u % 2 == 0:
                            pe.wait_ge(k_in[i][u // 2], 32 * it + 32)
                        pe.wait_ge(held_d if u % 2 else held_a, (NU + 2) * it + NPAGE * i + u // 2 + 1)
                        for c in range(HP):
                            mm = pe.transpose(turn[u % 2][:, c, :], k_page[i][:, u, c * P:c * P + P], ident[:])
                        mm.then_inc(turned, 1)
                    if u >= 1:
                        g, s = (u - 1) // 2, (u - 1) % 2
                        if u == 1:
                            pe.wait_ge(keep_step, 8 * it + 1)
                            pe.wait_ge(q_set, n + 1)
                        pe.wait_ge(held_d if s else held_a, (NU + 2) * it + NPAGE * i + g + 2)
                        for c in range(HP):
                            at = (2 * c + s) * P
                            mm = pe.matmul(z[i][g // 4][:, g % 4 * P:g % 4 * P + P], q_now[i][:, at:at + P], kT[:, (u - 1) % 4, c, :],
                                           start=(g % 4 == 0 and s == 0 and c == 0), stop=True, skip_group_check=True)
                        mm.then_inc(page_logits, 1)
                pe.wait_ge(small_read, 6 * it + i + 1)
                for s in range(2):
                    for c in range(HP):
                        at = (2 * c + s) * P
                        mm = pe.matmul(small[:, 0:LS], q_now[i][:, at:at + P], kT_new[:, c, bass.ds((2 * n + s) * LS, LS)],
                                       start=(s == 0 and c == 0), stop=(s == 1 and c == HP - 1))
                mm.then_inc(new_logits, 1)

            def weighted(it, i):
                n = 2 * it + i
                pe.wait_ge(soft_step, 4 * n + 5)
                for half in range(2):
                    pe.wait_ge(held_d if half else held_a, (NU + 2) * it + NU + i + 1)
                    for c in range(4):
                        g = 4 * half + c
                        mm = pe.transpose(turn[half][:, c, :], w[:, g * P:g * P + P], ident[:])
                    mm.then_inc(turned, 1)
                pe.wait_ge(small_read, 6 * it + 3 + 2 * i)
                pe.transpose(small[0:LS, 0:P], w[:, PAST:ALL], ident[:]).then_inc(turned, 1)
                pe.wait_ge(v_in[i], 16 * NU * it + 16 * NU)
                pe.wait_ge(new_in[i], 16 * it + 16)
                pe.wait_ge(held_a, (NU + 2) * it + NU + i + 2)
                pe.wait_ge(held_d, (NU + 2) * it + NU + i + 2)
                pe.wait_ge(small_read, 6 * it + 4 + 2 * i)
                pe.wait_ge(mined, n + 1)
                for s in range(2):
                    rows = slice(s * ROWS, s * ROWS + ROWS)
                    for g in range(NPAGE):
                        pe.matmul(o[rows, :], wT[:, g, rows], v_page[i][:, 2 * g + s, :], start=(g == 0), stop=False, skip_group_check=True)
                    mm = pe.matmul(o[rows, :], wT_new[:, rows], v_new[i][:, s, :],
                                   start=False, stop=True, skip_group_check=True)
                mm.then_inc(outputs, 1)
                pe.wait_ge(mined, n + 2)
                pe.wait_ge(const_in, NCONST)
                for c in range(HP):
                    mm = pe.matmul(small[:, c * 2 * LS:(c + 1) * 2 * LS], mine[:, c * P:c * P + P], sel[:], start=(c == 0), stop=True,
                                   skip_group_check=True)
                mm.then_inc(turned, 1)

            with pe.Fori(0, NTURN) as it:
                logits(it, 0)
                logits(it, 1)
                weighted(it, 0)
                weighted(it, 1)

        TURNED = 2 * NU + 2 * 4
        in_turn = lambda i, half: 2 * NU + 4 * i + half

        @block.scalar
        def _(act):
            load_exp_ln(nc)
            act.sem_inc(held_a, 1)
            act.sem_inc(soft_step, 1)
            for i, dst in enumerate((qT, kT_new)):
                act.wait_ge(new_turned, i + 1)
                nc.scalar.activation(dst[:], turn[i][:, :, 0:TS], ACT.Copy, scale=DA ** -0.5 if i == 0 else 1.0).then_inc(new_held, 1)
            act.wait_ge(prep, 3)

            def softplus(it, i):
                n = 2 * it + i
                s = soft[i]
                act.wait_ge(page_logits, NU * n + NU + 4)
                act.wait_ge(keep_step, 8 * it + 1)
                act.wait_ge(soft_step, 4 * n + 1)
                nc.scalar.activation(s[:, 0:512], z[i][0][:], ACT.Abs, bias=bias[:])
                yield
                nc.scalar.activation(s[:, 512:PAST], z[i][1][:], ACT.Abs, bias=bias[:])
                act.wait_ge(small_read, 6 * it + i + 2)
                nc.scalar.activation(s[:, PAST:ALL], zm[i][:], ACT.Abs, bias=bias[:]).then_inc(soft_step, 1)
                yield
                act.wait_ge(soft_step, 4 * n + 2)
                nc.scalar.activation(s[:], s[:], ACT.Exp, scale=-1.0).then_inc(soft_step, 1)
                yield
                act.wait_ge(soft_step, 4 * n + 3)
                nc.scalar.activation(s[:], s[:], ACT.Ln, bias=1.0).then_inc(soft_step, 1)
                yield

            def weights(it, i):
                n = 2 * it + i
                act.wait_ge(keep_step, 4 * n + 5)
                act.wait_ge(outputs, n + 1)
                nc.scalar.activation(w[:], soft[i][:], ACT.Exp, bias=bias[:]).then_inc(soft_step, 1)

            def copy_weights(it, i):
                act.wait_ge(turned, TURNED * it + in_turn(i, 0) + 1)
                nc.scalar.copy(wT[:, 0:4, :], turn[0][:]).then_inc(held_a, 1)

            with act.Fori(0, NTURN) as it:
                parts = iter(())
                for i in range(2):
                    for u in range(0, NU, 2):
                        act.wait_ge(turned, TURNED * it + NU * i + u + 1)
                        act.wait_ge(page_logits, NU * (2 * it + i) + u + 1)
                        nc.scalar.copy(kT[:, u % 4, :, :], turn[0][:]).then_inc(held_a, 1)
                        next(parts, None)
                    parts = softplus(it, i)
                weights(it, 0)
                copy_weights(it, 0)
                for _ in parts:
                    pass
                weights(it, 1)
                copy_weights(it, 1)

        @block.vector
        def _(dve):
            dve.sem_inc(held_d, 1)
            dve.sem_inc(keep_step, 1)
            dve.sem_inc(small_read, 1)
            dve.sem_inc(mined, 1)
            dve.wait_ge(first_in, NFIRST)
            dve.tensor_copy(bias_row[:], biases[:].unsqueeze(1).unsqueeze(3).to_broadcast([1, 2, HA, LS])).then_inc(prep, 1)
            dve.wait_ge(prep, 2)
            dve.tensor_copy(bias[:], small[:, 0:1]).then_inc(prep, 1)
            dve.wait_ge(prep, 3)
            dve.wait_ge(const_in, NCONST)

            def sums(it, i):
                n = 2 * it + i
                k, s, zz = keep[i], soft[i], z[i]
                dve.wait_ge(new_logits, n + 2)
                dve.wait_ge(soft_step, 8 * it + 1)
                dve.tensor_tensor(zm[i][:], small[:, 0:LS], mask[:], ALU.add).then_inc(small_read, 1)
                yield
                dve.wait_ge(small_read, 6 * it + i + 2)
                dve.wait_ge(soft_step, 4 * n + 2)
                dve.wait_ge(keep_step, 4 * n + 1)
                dve.tensor_scalar(k[:, 0:512], zz[0][:], bias[:], 0.0, ALU.add, ALU.max)
                yield
                dve.tensor_scalar(k[:, 512:PAST], zz[1][:], bias[:], 0.0, ALU.add, ALU.max)
                dve.tensor_scalar(k[:, PAST:ALL], zm[i][:], bias[:], 0.0, ALU.add, ALU.max).then_inc(keep_step, 1)
                yield
                dve.wait_ge(keep_step, 4 * n + 2)
                dve.wait_ge(soft_step, 4 * n + 4)
                dve.scalar_tensor_tensor(k[:], k[:], -1.0, s[:], ALU.mult, ALU.subtract).then_inc(keep_step, 1)
                yield
                dve.wait_ge(keep_step, 4 * n + 3)
                dve.tensor_tensor_scan(s[:, ::-1], ones[:, 0:1].to_broadcast([P, ALL]), k[:, ::-1], 0.0, ALU.mult, ALU.add).then_inc(keep_step, 1)
                yield
                dve.wait_ge(keep_step, 4 * n + 4)
                for j in range(2):
                    cols = slice(512 * j, 512 * j + 512)
                    dve.tensor_tensor(s[:, cols], zz[j][:], s[:, cols], ALU.add)
                    yield
                dve.tensor_tensor(s[:, PAST:ALL], zm[i][:], s[:, PAST:ALL], ALU.add).then_inc(keep_step, 1)

            def copy_weights(it, i):
                dve.wait_ge(turned, TURNED * it + in_turn(i, 1) + 1)
                dve.tensor_copy(wT[:, 4:8, :], turn[1][:]).then_inc(held_d, 1)
                dve.wait_ge(turned, TURNED * it + in_turn(i, 2) + 1)
                dve.tensor_copy(wT_new[:], small[0:LS, 0:P]).then_inc(small_read, 1)

            def finish(it, i):
                n = 2 * it + i
                dve.wait_ge(outputs, n + 2)
                dve.tensor_tensor(mine[:], o[:], own[:], ALU.mult).then_inc(mined, 1)
                dve.wait_ge(turned, TURNED * it + in_turn(i, 3) + 1)
                cols = bass.ds(n * 2 * LS, 2 * LS)
                dve.tensor_tensor(mix[:, :, cols], small[:, 0:HP * 2 * LS].rearrange("p (c t) -> p c t", c=HP), gate[:, :, cols],
                                  ALU.mult).then_inc(small_read, 1)

            with dve.Fori(0, NTURN) as it:
                parts = iter(())
                for i in range(2):
                    for u in range(1, NU, 2):
                        dve.wait_ge(turned, TURNED * it + NU * i + u + 1)
                        dve.wait_ge(page_logits, NU * (2 * it + i) + u + 1)
                        dve.tensor_copy(kT[:, u % 4, :, :], turn[1][:]).then_inc(held_d, 1)
                        next(parts, None)
                    for _ in parts:
                        pass
                    parts = sums(it, i)
                next(parts)
                copy_weights(it, 0)
                for _ in parts:
                    pass
                finish(it, 0)
                copy_weights(it, 1)
                finish(it, 1)



def hgrn(nc, q_fm, f_fm, v_tm, gate_fm, bounds, out_gain, state_in, state_prompt, state_samples, mix_fm, consts):
    with nc.cleanup_on_exit(), ExitStack() as ctx:
        sb = lambda n, s, d=F32: ctx.enter_context(nc.sbuf_tensor(f"hg_{n}", s, d))
        two = lambda n, s: [sb(f"{n}{i}", s) for i in range(2)]
        sem = lambda n: nc.alloc_semaphore(f"hg_{n}")
        ps = lambda n, s: ctx.enter_context(nc.psum_tensor(f"hg_{n}", s, F32))
        NL, NCH, NG = 7, TP // P, 2
        NSLOT = NL + 2
        NX = 4
        sc = [ps(f"sc{i}", [P, 4, P]) for i in range(4)]
        sx = ps("sx", [TS, TS])
        ku = ps("ku", [P, 4, P])
        o = [ps("o0", [P, 4, P]), ps("o1", [P, 4, P])]

        ident, ones = sb("ident", [P, P]), sb("ones", [P, P])
        level_mask = sb("level_mask", [P, NL + 1, P], I32)
        own = sb("own", [TS, NS])
        reset = sb("reset", [P, T])
        ab = sb("ab", [P, 2, HB])
        diff, lb, om = sb("diff", [P, HB]), sb("lb", [P, HB]), sb("om", [P, HB])
        gain, eps = sb("gain", [P, 1]), sb("eps", [P, 1])
        q = [sb(f"q{h}", [P, T]) for h in range(HB)]
        k = [sb(f"k{h}", [P, T]) for h in range(HB)]
        b = [sb(f"b{h}", [P, T]) for h in range(HB)]
        v, gate, s0 = two("v", [P, NT, P]), two("gate", [P, T]), two("s0", [P, NS, P])
        x = [sb(f"x{i}", [P, T]) for i in range(NX)]
        scores, scores_s = two("scores", [P, NCH, P]), two("scores_s", [TS, TS])
        eb, tail = two("eb", [P, T]), sb("tail", [P, T])
        qd, kd = two("qd", [P, T]), sb("kd", [P, T])
        kd_tm = sb("kd_tm", [P, NT, P])
        state = sb("state", [P, NCH + 1, P])
        vx = sb("vx", [TS, NS, P])
        s1, s_dec = sb("s1", [P, NS, P]), sb("s_dec", [P, NS, P])
        sq, rs = two("sq", [P, 4 * P]), two("rs", [P, 4 * P])
        on, mix = sb("on", [P, 4 * P]), sb("mix", [P, T])

        const_in, ab_in, prep, cleared = sem("const_in"), sem("ab_in"), sem("prep"), sem("cleared")
        f_in, q_in = ([sem(f"{n}{h}") for h in range(HB)] for n in ("f_in", "q_in"))
        v_in, gate_in, s0_in = ([sem(f"{n}{i}") for i in range(2)] for n in ("v_in", "g_in", "s_in"))
        sig_done, k_done, logf_done, b_done = sem("sig"), sem("k"), sem("logf"), sem("b")
        exponents, weights, weighted = sem("exponents"), sem("weights"), sem("weighted")
        scored, scored_s, picked, picked_s = sem("scored"), sem("scored_s"), sem("picked"), sem("picked_s")
        eb_done, tail_diff, tail_exp, qd_done, kd_done = sem("eb"), sem("tail_diff"), sem("tail_exp"), sem("qd"), sem("kd")
        turned, held, updates, updates_s, state_done = sem("turned"), sem("held"), sem("updates"), sem("updates_s"), sem("state")
        vx_done, dec_done, s1_done, s_left = sem("vx"), sem("dec"), sem("s1"), sem("s_left")
        o_done, sq_done, sum_done, ln_done, rs_done, on_done, mixed = (
            sem("o"), sem("sq"), sem("sum"), sem("ln"), sem("rs"), sem("on"), sem("mixed"))
        mix_left, state_left = sem("mix_left"), sem("state_left")
        block = ctx.enter_context(nc.Block())
        NCONST = 16 * 6

        def halves(t, l):
            m = P // 2 >> l
            n = T if 2 * m <= LS else TP
            return t[:, 0:n].rearrange("p (c two m) -> p c two m", two=2, m=m)

        def chunks(t):
            return t[:, 0:TP].rearrange("p (c n) -> p c n", n=P), t[:, TP:T].rearrange("p (c n) -> p c n", n=LS)

        def outputs_of(g):
            flat = ku[:].rearrange("p c n -> p (c n)")
            if g < NG:
                return o[g][:].rearrange("p c n -> p (c n)"), flat, slice(4 * P * g, 4 * P * (g + 1))
            return flat[:, 0:TS], flat[:, TS:2 * TS], slice(TP, T)

        def run(scores_slot, rest):
            last, now = iter(()), iter(())
            for h in range(HB + 1):
                last, now = now, (rest(h - 1) if h else iter(()))
                for slot in range(NSLOT):
                    if h < HB:
                        scores_slot(h, slot)
                    if slot == 0:
                        for _ in last:
                            pass
                    next(now, None)
            for _ in now:
                pass

        @block.sync
        def _(sp):
            rows = lambda h: slice(h * P, h * P + P)
            sp.dma_start(ab[:], bounds.rearrange("e (h k) -> k e h", k=P), allow_slow_non_contiguous=True).then_inc(ab_in, 16)
            for h in range(HB):
                sp.dma_start(k[h][:], f_fm[rows(h), :]).then_inc(f_in[h], 16)
            sp.dma_start(reset[:], consts["reset"]).then_inc(const_in, 16)
            sp.dma_start(q[0][:], q_fm[rows(0), :]).then_inc(q_in[0], 16)
            for dst, src in ((ident[:], consts["ident"]), (ones[:], consts["ones"]), (level_mask[:], consts["level_mask"]),
                             (own[:], consts["own"])):
                sp.dma_start(dst, src).then_inc(const_in, 16)
            sp.dma_start(gain[:], out_gain.rearrange("(k a) -> k a", a=1), allow_slow_non_contiguous=True).then_inc(const_in, 16)
            for h in range(1, HB):
                sp.dma_start(q[h][:], q_fm[rows(h), :]).then_inc(q_in[h], 16)

            def load(h):
                rows, s = slice(h * P, h * P + P), h % 2
                sp.dma_start(v[s][:, 0:NT - 1, :], v_tm[0:TP, rows].rearrange("(c p) n -> p c n", p=P)).then_inc(v_in[s], 16)
                sp.dma_start(v[s][0:TS, NT - 1, :], v_tm[TP:T, rows]).then_inc(v_in[s], 16)
                sp.dma_start(s0[s][:], state_in[:, h].rearrange("b k v -> k b v")).then_inc(s0_in[s], 16)
                sp.dma_start(gate[s][:], gate_fm[rows, :]).then_inc(gate_in[s], 16)

            load(0)
            load(1)
            for h in range(HB):
                sp.wait_ge(state_done, NCH * (h + 1))
                sp.dma_start(state_prompt[h], state[:, NCH, :]).then_inc(state_left, 16)
                sp.wait_ge(s1_done, NG * (h + 1))
                sp.dma_start(state_samples[:, h].rearrange("b k v -> k b v"), s1[:]).then_inc(s_left, 16)
                sp.wait_ge(mixed, 3 * (h + 1))
                sp.dma_start(mix_fm[WA + h * P:WA + h * P + P, :], mix[:]).then_inc(mix_left, 16)
                if h + 2 < HB:
                    load(h + 2)
            sp.wait_ge(mix_left, 16 * HB)
            sp.wait_ge(state_left, 16 * HB)
            sp.wait_ge(s_left, 16 * HB)

        @block.gpsimd
        def _(pool):
            def scores_slot(h, l):
                if l == 0:
                    pool.wait_ge(b_done, h + 1)
                if l == NL - 2:
                    pool.wait_ge(eb_done, h + 1)
                    pool.wait_ge(q_in[h], 16)
                    if h >= 2:
                        pool.wait_ge(o_done, 3 * (h - 1))
                    nc.gpsimd.tensor_tensor(qd[h % 2][:], q[h][:], eb[h % 2][:], ALU.mult).then_inc(qd_done, 1)
                if l < NL:
                    n = NL * h + l
                    if n >= NX:
                        before, level = divmod(n - NX, NL)
                        pool.wait_ge(scored, (NL + 1) * before + level + 1)
                    bb, xx = halves(b[h], l), halves(x[n % NX], l)
                    r = bb[:, :, 0, bb.shape[3] - 1:].to_broadcast([P, bb.shape[1], bb.shape[3]])
                    nc.gpsimd.tensor_tensor(xx[:, :, 0, :], r, bb[:, :, 0, :], ALU.subtract)
                    nc.gpsimd.tensor_tensor(xx[:, :, 1, :], bb[:, :, 1, :], r, ALU.subtract).then_inc(exponents, 1)

            def rest(h):
                s = h % 2
                pool.wait_ge(v_in[s], 32 * (h // 2) + 32)
                if h:
                    pool.wait_ge(updates_s, NG * h)
                nc.gpsimd.tensor_tensor(vx[:], v[s][0:TS, NT - 1, :].unsqueeze(1).to_broadcast([TS, NS, P]),
                                        own[:].unsqueeze(2).to_broadcast([TS, NS, P]), ALU.mult).then_inc(vx_done, 1)
                yield
                pool.wait_ge(s0_in[s], 16 * (h // 2) + 16)
                pool.wait_ge(eb_done, h + 1)
                if h:
                    pool.wait_ge(s1_done, NG * h)
                ends = chunks(eb[s])[1][:, :, LS - 1:].to_broadcast([P, NS, P])
                nc.gpsimd.tensor_tensor(s_dec[:], s0[s][:], ends, ALU.mult).then_inc(dec_done, 1)

            pool.wait_ge(const_in, NCONST)
            run(scores_slot, rest)

        @block.scalar
        def _(act):
            act.wait_ge(prep, 2)
            nc.scalar.activation(lb[:], diff[:], ACT.Sigmoid).then_inc(prep, 1)
            nc.scalar.activation(om[:], diff[:], ACT.Sigmoid, scale=-1.0).then_inc(prep, 1)
            for h in range(HB):
                act.wait_ge(f_in[h], 16)
                nc.scalar.activation(b[h][:], k[h][:], ACT.Sigmoid).then_inc(sig_done, 1)
                act.wait_ge(sig_done, 2 * h + 1)
                nc.scalar.activation(k[h][:], k[h][:], ACT.Sigmoid, scale=-1.0).then_inc(sig_done, 1)
            load_exp_ln(nc)
            act.wait_ge(prep, 4)

            def log_decays(h):
                act.wait_ge(sig_done, 2 * HB)
                nc.scalar.activation(b[h][:], b[h][:], ACT.Ln, scale=om[:, h:h + 1], bias=lb[:, h:h + 1]).then_inc(logf_done, 1)

            def weigh(n):
                at = x[n % NX][:, 0:T if P >> n % NL <= LS else TP]
                act.wait_ge(exponents, n + 1)
                nc.scalar.activation(at, at, ACT.Exp).then_inc(weights, 1)

            def scores_slot(h, l):
                if l < NL and NL * h + l + 2 < NL * HB:
                    weigh(NL * h + l + 2)
                if l == 1:
                    if h >= 2:
                        act.wait_ge(state_done, NCH * (h - 1))
                        act.wait_ge(dec_done, h - 1)
                        act.wait_ge(qd_done, h - 1)
                    nc.scalar.activation(eb[h % 2][:], b[h][:], ACT.Exp).then_inc(eb_done, 1)
                if l == 2:
                    act.wait_ge(tail_diff, h + 1)
                    nc.scalar.activation(tail[:], tail[:], ACT.Exp).then_inc(tail_exp, 1)
                if l == 3 and h + 1 < HB:
                    log_decays(h + 1)

            def squares(h, g):
                src, _, tok = outputs_of(g)
                act.wait_ge(o_done, 3 * h + g + 1)
                if h or g == 2:
                    act.wait_ge(sum_done, 3 * h + g - 1 if g else 3 * h)
                nc.scalar.activation(sq[g % 2][:, 0:tok.stop - tok.start], src, ACT.Square).then_inc(sq_done, 1)

            def scales(h, g):
                _, ss, tok = outputs_of(g)
                r = rs[g % 2][:, 0:tok.stop - tok.start]
                act.wait_ge(sum_done, 3 * h + g + 1)
                if h or g == 2:
                    act.wait_ge(on_done, 3 * h + g - 1 if g else 3 * h)
                nc.scalar.activation(r, ss, ACT.Ln, scale=1.0 / DB, bias=eps[:]).then_inc(ln_done, 1)
                act.wait_ge(ln_done, 3 * h + g + 1)
                nc.scalar.activation(r, r, ACT.Exp, scale=-0.5).then_inc(rs_done, 1)

            def rest(h):
                if h:
                    act.wait_ge(updates_s, NG * h)
                for g in range(NG + 1):
                    if g == NG:
                        yield
                    act.wait_ge(turned, 3 * h + g + 1)
                    if g < NG:
                        nc.scalar.copy(kd_tm[:, 4 * g:4 * g + 4, :], ku[:]).then_inc(held, 1)
                    else:
                        nc.scalar.copy(kd_tm[0:TS, NT - 1, :], ku[0:TS, 0, :]).then_inc(held, 1)
                for _ in range(4):
                    yield
                squares(h, 0)
                squares(h, 1)
                yield
                scales(h, 0)
                yield
                scales(h, 1)
                yield
                squares(h, 2)
                yield
                scales(h, 2)

            log_decays(0)
            weigh(0)
            weigh(1)
            run(scores_slot, rest)

        @block.vector
        def _(dve):
            dve.wait_ge(ab_in, 16)
            dve.tensor_tensor(diff[:], ab[:, 0, :], ab[:, 1, :], ALU.subtract).then_inc(prep, 1)
            nc.vector.memset(eps[:], EPS).then_inc(prep, 1)
            for s in range(2):
                nc.vector.memset(scores[s][:], 0.0)
                nc.vector.memset(scores_s[s][:], 0.0).then_inc(cleared, 1)
            dve.wait_ge(prep, 4)
            dve.wait_ge(cleared, 2)

            def keys(h):
                dve.wait_ge(sig_done, 2 * h + 2)
                dve.tensor_scalar(k[h][:], k[h][:], om[:, h:h + 1], None, ALU.mult).then_inc(k_done, 1)

            def sum_decays(h):
                dve.wait_ge(logf_done, h + 1)
                dve.tensor_tensor_scan(b[h][:], reset[:], b[h][:], 0.0, ALU.mult, ALU.add).then_inc(b_done, 1)

            def pick(h, l):
                mask = level_mask[:, l, :].unsqueeze(1).to_broadcast([P, 4, P])
                if h >= 2 and l == 0:
                    dve.wait_ge(o_done, 3 * (h - 1))
                dve.wait_ge(scored, (NL + 1) * h + l + 1)
                dve.wait_ge(picked, (NL + 1) * h + l)
                for g in range(NG):
                    ins = dve.copy_predicated(scores[h % 2][:, 4 * g:4 * g + 4, :], mask, sc[2 * (l % 2) + g][:])
                ins.then_inc(picked, 1)
                if l >= 4:
                    dve.wait_ge(scored_s, 4 * h + l - 3)
                    dve.wait_ge(picked_s, 4 * h + l - 4)
                    dve.copy_predicated(scores_s[h % 2][:], level_mask[0:TS, l, 0:TS], sx[:]).then_inc(picked_s, 1)

            def weight(h, l):
                if h < HB:
                    xx = halves(x[(NL * h + l) % NX], l)
                    dve.wait_ge(weights, NL * h + l + 1)
                    dve.wait_ge(k_done, h + 1)
                    dve.wait_ge(q_in[h], 16)
                    dve.tensor_tensor(xx[:, :, 0, :], xx[:, :, 0, :], halves(k[h], l)[:, :, 0, :], ALU.mult)
                    dve.tensor_tensor(xx[:, :, 1, :], xx[:, :, 1, :], halves(q[h], l)[:, :, 1, :], ALU.mult).then_inc(weighted, 1)

            def scores_slot(h, l):
                if l + 1 < NL:
                    weight(h, l + 1)
                elif l == NSLOT - 1:
                    weight(h + 1, 0)
                if l >= 1:
                    pick(h, l - 1)
                if l == 1:
                    if h:
                        dve.wait_ge(kd_done, h)
                    dve.wait_ge(b_done, h + 1)
                    for bb, tt, n in zip(chunks(b[h]), chunks(tail), (P, LS)):
                        ins = dve.tensor_tensor(tt, bb[:, :, n - 1:].to_broadcast([P, bb.shape[1], n]), bb, ALU.subtract)
                    ins.then_inc(tail_diff, 1)
                if l == 4 and h + 1 < HB:
                    sum_decays(h + 1)
                if l == 5:
                    dve.wait_ge(tail_exp, h + 1)
                    if h:
                        dve.wait_ge(turned, 3 * h)
                    dve.tensor_tensor(kd[:], k[h][:], tail[:], ALU.mult).then_inc(kd_done, 1)

            def finish(h, g):
                src, _, tok = outputs_of(g)
                n = tok.stop - tok.start
                dve.wait_ge(rs_done, 3 * h + g + 1)
                dve.wait_ge(mixed, 3 * h + g)
                dve.tensor_tensor(on[:, 0:n], src, rs[g % 2][:, 0:n], ALU.mult).then_inc(on_done, 1)
                dve.wait_ge(on_done, 3 * h + g + 1)
                dve.scalar_tensor_tensor(mix[:, tok], on[:, 0:n], gain[:, 0:1], gate[h % 2][:, tok], ALU.mult, ALU.mult).then_inc(mixed, 1)

            def rest(h):
                s = h % 2
                yield
                yield
                if h:
                    dve.wait_ge(state_left, 16 * h)
                    dve.wait_ge(o_done, 3 * h - 1)
                for c in range(NCH):
                    u = o[c // 4][:, c % 4, :]
                    if c % 4 == 0:
                        dve.wait_ge(updates, NG * h + c // 4 + 1)
                    if c == 0:
                        dve.tensor_copy(state[:, 1, :], u).then_inc(state_done, 1)
                    else:
                        dve.wait_ge(state_done, NCH * h + c)
                        dve.scalar_tensor_tensor(state[:, c + 1, :], state[:, c, :], eb[s][:, c * P + P - 1:c * P + P], u,
                                                 ALU.mult, ALU.add).then_inc(state_done, 1)
                yield
                for g in range(NG):
                    if g == 0:
                        dve.wait_ge(dec_done, h + 1)
                        if h:
                            dve.wait_ge(s_left, 16 * h)
                    dve.wait_ge(updates_s, NG * h + g + 1)
                    dve.tensor_tensor(s1[:, 4 * g:4 * g + 4, :], s_dec[:, 4 * g:4 * g + 4, :], ku[:], ALU.add).then_inc(s1_done, 1)
                    yield
                    if g == 0:
                        yield
                yield
                dve.wait_ge(gate_in[s], 16 * (h // 2) + 16)
                if h:
                    dve.wait_ge(mix_left, 16 * h)
                finish(h, 0)
                yield
                finish(h, 1)
                yield
                finish(h, 2)

            keys(0)
            dve.wait_ge(const_in, NCONST)
            sum_decays(0)
            weight(0, 0)
            for h in range(1, HB):
                keys(h)
            run(scores_slot, rest)

        @block.tensor
        def _(pe):
            pe.wait_ge(const_in, NCONST)

            def scores_slot(h, l):
                if l > NL:
                    return
                n = (NL + 1) * h + l
                if l < NL:
                    pe.wait_ge(weighted, NL * h + l + 1)
                if n >= 2:
                    pe.wait_ge(picked, n - 1)
                xl = x[(NL * h + l) % NX]
                lhs, rhs = (xl, xl) if l < NL else (k[h], q[h])
                for c in range(NCH):
                    tok = slice(c * P, c * P + P)
                    mm = pe.matmul(sc[2 * (l % 2) + c // 4][:, c % 4, :], lhs[:, tok], rhs[:, tok], start=True, stop=True)
                if l >= 4:
                    if h or l > 4:
                        pe.wait_ge(picked_s, 4 * h + l - 4)
                    pe.matmul(sx[:], lhs[:, TP:T], rhs[:, TP:T], start=True, stop=True).then_inc(scored_s, 1)
                    pe.wait_ge(scored_s, 4 * h + l - 3)
                    pe.sem_inc(scored, 1)
                else:
                    mm.then_inc(scored, 1)

            def rest(h):
                s = h % 2
                pe.wait_ge(kd_done, h + 1)
                if h:
                    pe.wait_ge(on_done, 3 * h)
                for g in range(NG + 1):
                    if g == NG:
                        yield
                    if g:
                        pe.wait_ge(held, 3 * h + g)
                    for c in range(4 if g < NG else 1):
                        n = P if g < NG else TS
                        at = 4 * g * P + c * P
                        mm = pe.transpose(ku[0:n, c, :], kd[:, at:at + n], ident[:])
                    mm.then_inc(turned, 1)
                pe.wait_ge(v_in[s], 32 * (h // 2) + 32)
                if h:
                    pe.wait_ge(mixed, 3 * h - 1)
                for g in range(NG):
                    pe.wait_ge(held, 3 * h + g + 1)
                    for c in range(4):
                        mm = pe.matmul(o[g][:, c, :], kd_tm[:, 4 * g + c, :], v[s][:, 4 * g + c, :], start=True, stop=True)
                    mm.then_inc(updates, 1)
                yield
                for g in range(NG):
                    if g == 0:
                        pe.wait_ge(held, 3 * h + 3)
                        pe.wait_ge(vx_done, h + 1)
                    else:
                        pe.wait_ge(s1_done, NG * h + 1)
                    pe.matmul(ku[:].rearrange("p c n -> p (c n)"), kd_tm[0:TS, NT - 1, :],
                              vx[:, 4 * g:4 * g + 4, :].rearrange("t c n -> t (c n)"), start=True, stop=True).then_inc(updates_s, 1)
                    yield
                    if g == 0:
                        yield
                pe.wait_ge(qd_done, h + 1)
                pe.wait_ge(picked, (NL + 1) * (h + 1))
                pe.wait_ge(state_done, NCH * (h + 1))
                for c in range(NCH):
                    tok = slice(c * P, c * P + P)
                    mm = pe.matmul(o[c // 4][:, c % 4, :], v[s][:, c, :], scores[s][:, c, :], start=True, stop=True)
                    if c:
                        mm = pe.matmul(o[c // 4][:, c % 4, :], state[:, c, :], qd[s][:, tok], start=False, stop=True, skip_group_check=True)
                    if c % 4 == 3:
                        mm.then_inc(o_done, 1)
                yield

                def sums(g):
                    _, ss, tok = outputs_of(g)
                    pe.wait_ge(sq_done, 3 * h + g + 1)
                    pe.matmul(ss, ones[:], sq[g % 2][:, 0:tok.stop - tok.start], start=True, stop=True).then_inc(sum_done, 1)

                pe.wait_ge(s1_done, NG * (h + 1))
                sums(0)
                yield
                pe.wait_ge(ln_done, 3 * h + 1)
                sums(1)
                yield
                pe.wait_ge(ln_done, 3 * h + 2)
                pe.wait_ge(picked_s, 4 * h + 4)
                pe.wait_ge(s0_in[s], 16 * (h // 2) + 16)
                out = outputs_of(NG)[0]
                pe.matmul(out, v[s][0:TS, NT - 1, :], scores_s[s][:], start=True, stop=True)
                for c in range(NS):
                    mm = pe.matmul(out[:, c * LS:c * LS + LS], s0[s][:, c, :], qd[s][:, TP + c * LS:TP + c * LS + LS],
                                   start=False, stop=True, skip_group_check=True)
                mm.then_inc(o_done, 1)
                yield
                sums(NG)

            run(scores_slot, rest)



def project_out(nc, tag, mix_fm, weight, x_of, y_of):
    with nc.cleanup_on_exit(), ExitStack() as ctx:
        sb = lambda n, s, d=F32: ctx.enter_context(nc.sbuf_tensor(f"{tag}_{n}", s, d))
        sem = lambda n: nc.alloc_semaphore(f"{tag}_{n}")
        K, NH = weight.shape[0] // P, D // 512
        NRAW = 4
        bank = [[ctx.enter_context(nc.psum_tensor(f"{tag}_bank{s}{n}", [P, 512], F32)) for n in range(NH)] for s in range(2)]
        raw = sb("raw", [P, NRAW, D])
        w_hi, w_lo = sb("w_hi", [P, K, D], F32R), sb("w_lo", [P, K, D], F32R)
        mix = sb("mix", [P, 2, K, P])
        m_hi, m_lo = sb("m_hi", [P, 2, K, P], F32R), sb("m_lo", [P, 2, K, P], F32R)
        xy = sb("xy", [P, 2, D])
        raw_in = [sem(f"raw{i}") for i in range(NRAW)]
        mix_in, x_in, y_left = ([sem(f"{n}{i}") for i in range(2)] for n in ("mix", "x", "left"))
        even_hi, even_split, odd_hi, odd_split = sem("even_hi"), sem("even_split"), sem("odd_hi"), sem("odd_split")
        m_hi_done, m_split = sem("m_hi"), sem("m_split")
        full, added = sem("full"), sem("added")
        block = ctx.enter_context(nc.Block())
        w_rows = weight.rearrange("(c p) n -> p c n", p=P)
        mix_cols = mix_fm.rearrange("(c p) t -> p c t", p=P)
        NTURN = (NT - 1) // 2

        def later(turn):
            return not isinstance(turn, int) or turn > 0

        def split_by(c):
            return (odd_split if c % 2 else even_split), c // 2 + 1

        @block.sync
        def _(sp):
            def load(t, slot, r, turn):
                if later(turn):
                    sp.wait_ge(m_split, t - 1)
                sp.dma_start(mix[:, slot, :, 0:r], mix_cols[:, :, bass.ds(t * P, r)]).then_inc(mix_in[slot], 16)

            for c in range(K):
                if c >= NRAW:
                    sp.wait_ge(*split_by(c - NRAW))
                sp.dma_start(raw[:, c % NRAW, :], w_rows[:, c, :]).then_inc(raw_in[c % NRAW], 16)
                if c < 2:
                    load(c, c, P, 0)
                if c >= K - 2:
                    load(c - K + 4, c - K + 2, P, 1)
            with sp.Fori(2, NTURN) as it:
                for slot in range(2):
                    load(2 * it + slot, slot, P, it)
            load(NT - 1, 0, TS, NTURN)

        @block.gpsimd
        def _(pool):
            def load(t, slot, r, turn):
                if later(turn):
                    pool.wait_ge(y_left[slot], 16 * turn)
                pool.dma_start(xy[0:r, slot, :], x_of(t)).then_inc(x_in[slot], 16)

            for c in range(1, K, 2):
                if c < 4:
                    load(c // 2, c // 2, P, 0)
                r, hi = raw[:, c % NRAW, :], w_hi[:, c, :]
                pool.wait_ge(raw_in[c % NRAW], 16 * (c // NRAW) + 16)
                nc.gpsimd.tensor_copy(hi, r).then_inc(odd_hi, 1)
                pool.wait_ge(odd_hi, c // 2 + 1)
                nc.gpsimd.tensor_tensor(w_lo[:, c, :], r, hi.bitcast(F32), ALU.subtract).then_inc(odd_split, 1)
            with pool.Fori(1, NTURN) as it:
                for slot in range(2):
                    load(2 * it + slot, slot, P, it)
            load(NT - 1, 0, TS, NTURN)

        @block.tensor
        def _(pe):
            def chunk(slot, c, r):
                hi, lo = m_hi[:, slot, c, 0:r], m_lo[:, slot, c, 0:r]
                for j, (m, w) in enumerate(((hi, w_hi), (hi, w_lo), (lo, w_hi))):
                    for n in range(NH):
                        mm = pe.matmul(bank[slot][n][0:r, :], m, w[:, c, n * 512:n * 512 + 512],
                                       start=(c == 0 and j == 0), stop=(c == K - 1 and j == 2))
                return mm

            def product(t, slot, r):
                pe.wait_ge(m_split, t + 1)
                pe.wait_ge(added, t - 1)
                for c in range(K):
                    mm = chunk(slot, c, r)
                mm.then_inc(full, 1)

            pe.wait_ge(m_split, 2)
            for c in range(K):
                pe.wait_ge(*split_by(c))
                for slot in range(2):
                    mm = chunk(slot, c, P)
                    if c == K - 1:
                        mm.then_inc(full, 1)
            with pe.Fori(1, NTURN) as it:
                for slot in range(2):
                    product(2 * it + slot, slot, P)
            product(NT - 1, 0, TS)

        @block.scalar
        def _(act):
            def split_hi(t, slot, r, turn):
                act.wait_ge(mix_in[slot], 16 * turn + 16)
                if later(turn):
                    act.wait_ge(full, t - 1)
                nc.scalar.copy(m_hi[:, slot, :, 0:r], mix[:, slot, :, 0:r]).then_inc(m_hi_done, 1)

            def store(t, slot, r):
                act.wait_ge(added, t + 1)
                act.dma_start(y_of(t), xy[0:r, slot, :]).then_inc(y_left[slot], 16)

            split_hi(0, 0, P, 0)
            split_hi(1, 1, P, 0)
            for c in range(0, K, 2):
                act.wait_ge(raw_in[c % NRAW], 16 * (c // NRAW) + 16)
                nc.scalar.copy(w_hi[:, c, :], raw[:, c % NRAW, :]).then_inc(even_hi, 1)
            with act.Fori(1, NTURN) as it:
                for slot in range(2):
                    split_hi(2 * it + slot, slot, P, it)
                    store(2 * it + slot - 2, slot, P)
            split_hi(NT - 1, 0, TS, NTURN)
            store(NT - 3, 0, P)
            store(NT - 2, 1, P)
            store(NT - 1, 0, TS)
            act.wait_ge(y_left[0], 16 * NTURN + 16)
            act.wait_ge(y_left[1], 16 * NTURN)

        @block.vector
        def _(dve):
            def split_lo(t, slot, r):
                hi = m_hi[:, slot, :, 0:r]
                dve.wait_ge(m_hi_done, t + 1)
                dve.tensor_tensor(m_lo[:, slot, :, 0:r], mix[:, slot, :, 0:r], hi.bitcast(F32), ALU.subtract).then_inc(m_split, 1)

            def add(t, slot, r, turn):
                dve.wait_ge(full, t + 1)
                dve.wait_ge(x_in[slot], 16 * turn + 16)
                for n in range(NH):
                    cols = slice(n * 512, n * 512 + 512)
                    ins = dve.tensor_tensor(xy[0:r, slot, cols], bank[slot][n][0:r, :], xy[0:r, slot, cols], ALU.add)
                ins.then_inc(added, 1)

            split_lo(0, 0, P)
            split_lo(1, 1, P)
            for c in range(0, K, 2):
                dve.wait_ge(even_hi, c // 2 + 1)
                dve.tensor_tensor(w_lo[:, c, :], raw[:, c % NRAW, :], w_hi[:, c, :].bitcast(F32), ALU.subtract).then_inc(even_split, 1)
            with dve.Fori(1, NTURN) as it:
                for slot in range(2):
                    split_lo(2 * it + slot, slot, P)
                    add(2 * it + slot - 2, slot, P, it - 1)
            split_lo(NT - 1, 0, TS)
            add(NT - 3, 0, P, NTURN - 1)
            add(NT - 2, 1, P, NTURN - 1)
            add(NT - 1, 0, TS, NTURN)



def retention(nc, q_fm, k_fm, v_tm, g_tm, state_in, state_prompt, state_samples, mix_fm, consts):
    with nc.cleanup_on_exit(), ExitStack() as ctx:
        sb = lambda n, s, d=F32: ctx.enter_context(nc.sbuf_tensor(f"rt_{n}", s, d))
        sem = lambda n: nc.alloc_semaphore(f"rt_{n}")
        ps = lambda n, s: ctx.enter_context(nc.psum_tensor(f"rt_{n}", s, F32))
        NCH, J = TP // P, DK // P
        gamma = [1.0 - 2.0 ** (-5 - h) for h in range(HC)]
        sc, kt = ps("sc", [P, P]), ps("kt", [P, J, P])
        o = [ps("o0", [P, DV]), ps("o1", [P, DV])]
        u = [ps("u0", [P, DV]), ps("u1", [P, DV])]
        os_, tr = ps("os", [TS, DV]), ps("tr", [P, DV // P, P])

        def tables(name, rows, shapes):
            whole = sb(name, [rows, sum(int(np.prod(x)) for x in shapes)])
            parts, at = [], 0
            for x in shapes:
                part = whole[:, at:at + int(np.prod(x))]
                parts.append(part if len(x) == 1 else part.rearrange("p (a b) -> p a b", a=x[0]))
                at += int(np.prod(x))
            return whole, parts

        table_p, (ident, decay, q_dec, q_dec_s, of_seq, k_dec) = tables("table_p", P, [(P,), (HC, P), (HC, P), (HC, TS), (NS, TS), (HC,)])
        table_s, (decay_s, own, k_dec_s) = tables("table_s", TS, [(HC, TS), (NS,), (HC,)])
        eps = sb("eps", [P, 1])
        q, k = sb("q", [P, 2, HC, J, P]), sb("k", [P, 2, HC, J, P])
        v, g = sb("v", [P, 2, HC, DV]), sb("g", [P, 2, HC, DV])
        q_s, k_s = sb("q_s", [P, HC, J, TS]), sb("k_s", [P, HC, J, TS])
        v_s, g_s = sb("v_s", [TS, HC, DV]), sb("g_s", [TS, HC, DV])
        vs_hi, vs_lo = sb("vs_hi", [TS, HC, DV], F32R), sb("vs_lo", [TS, HC, DV], F32R)
        ks_hi, ks_lo = sb("ks_hi", [TS, HC, J, P], F32R), sb("ks_lo", [TS, HC, J, P], F32R)
        v_hi, v_lo = sb("v_hi", [P, 2, DV], F32R), sb("v_lo", [P, 2, DV], F32R)
        scm_hi, scm_lo = sb("scm_hi", [P, 2, P], F32R), sb("scm_lo", [P, 2, P], F32R)
        kd_hi, kd_lo = sb("kd_hi", [P, 2, J, P], F32R), sb("kd_lo", [P, 2, J, P], F32R)
        qd_s, kd_s = sb("qd_s", [P, HC, J, TS]), sb("kd_s", [TS, HC, J, P])
        scm_s, acc = sb("scm_s", [TS, 2, TS]), sb("acc", [TS, HC, DV])
        scm, kd, qd = sb("scm", [P, 2, P]), sb("kd", [P, 2, J, P]), sb("qd", [P, 2, J, P])
        qx, kx_hi, kx_lo = sb("qx", [P, 2, J, TS]), sb("kx_hi", [TS, 2, J, P], F32R), sb("kx_lo", [TS, 2, J, P], F32R)
        state = sb("state", [P, HC, J, DV])
        s0 = [sb(f"s0{h}", [P, J, DV]) for h in range(HC)]
        s1 = [sb(f"s1{i}", [P, J, DV]) for i in range(2)]
        square, ss, rs = sb("square", [P, DV]), sb("ss", [P, 2]), sb("rs", [P, 2])
        og = sb("og", [P, 2, DV])
        mix = sb("mix", [P, 2, DV // P, P])

        const_in, smp_in, zeroed = sem("const_in"), sem("smp_in"), sem("zeroed")
        chunk_in = [sem("chunk_in0"), sem("chunk_in1")]
        s0_in = [sem(f"s0_in{h}") for h in range(HC)]
        first_sc, first_scm, first_kt, first_kd, first_os, first_acc, first_qd = (
            sem(f"first_{n}") for n in ("sc", "scm", "kt", "kd", "os", "acc", "qd"))
        sc_done, scm_done, kt_done, kd_done, qd_done, qx_done, kx_done = (
            sem(n) for n in ("sc", "scm", "kt", "kd", "qd", "qx", "kx"))
        o_done, u_done, os_done, us_done = sem("o"), sem("u"), sem("os"), sem("us")
        sq_done, ln_done, rs_done, gated, state_done, acc_done, s1_done = (
            sem(n) for n in ("sq", "ln", "rs", "gated", "state", "acc", "s1"))
        tr_done, tr_read, state_left = (sem(n) for n in ("tr", "tr_read", "state_left"))
        mix_left, s1_left = ([sem(f"{n}{i}") for i in range(2)] for n in ("mix_left", "s1_left"))
        pool_go, pe_go = sem("pool_go"), sem("pe_go")
        first_hi, first_split, v_rounded, v_split = sem("first_hi"), sem("first_split"), sem("v_rounded"), sem("v_split")
        scm_rounded, scm_split, kd_rounded, kd_split = sem("scm_rounded"), sem("scm_split"), sem("kd_rounded"), sem("kd_split")
        block = ctx.enter_context(nc.Block())
        NB = 2 * HC
        NTURN = NCH // 2
        NSTEP = NB * NTURN
        q_cols, k_cols = (t.rearrange("(c p) t -> p c t", p=P) for t in (q_fm, k_fm))
        v_rows, g_rows = (t.rearrange("t (h n) -> t h n", n=DV) for t in (v_tm, g_tm))
        mix_cols = mix_fm.rearrange("(h r p) t -> p h r t", r=DV // P, p=P)
        NCONST = 32

        @block.sync
        def _(sp):
            for dst, src in ((q_s, q_cols), (k_s, k_cols)):
                sp.dma_start(dst[:].rearrange("p h j t -> p (h j) t"), src[:, :, TP:T]).then_inc(smp_in, 16)
            sp.dma_start(v_s[:], v_rows[TP:T]).then_inc(smp_in, 16)
            sp.dma_start(g_s[:], g_rows[TP:T]).then_inc(smp_in, 16)
            with sp.Fori(0, NTURN) as it:
                for slot in range(2):
                    chunk = 2 * it + slot
                    sp.wait_ge(state_done, HC * chunk + 1)
                    sp.wait_ge(s1_done, HC * chunk + 1)
                    cols = bass.ds(chunk * P, P)
                    for dst, src in ((q, q_cols), (k, k_cols)):
                        sp.dma_start(dst[:, slot].rearrange("p h j t -> p (h j) t"), src[:, :, cols]).then_inc(chunk_in[slot], 16)
                    sp.dma_start(v[:, slot], v_rows[cols]).then_inc(chunk_in[slot], 16)
                    sp.dma_start(g[:, slot], g_rows[cols]).then_inc(chunk_in[slot], 16)
                    for h in range(HC):
                        sp.wait_ge(s1_done, HC * chunk + h + 1)
                        sp.dma_start(s0[h][:], state_in[bass.ds(chunk, 1), h].rearrange("a (j k) v -> k (a j) v", k=P)).then_inc(s0_in[h], 16)
            sp.wait_ge(state_done, NSTEP + HC + 1)
            sp.dma_start(state_prompt.rearrange("h (j k) v -> k h j v", k=P), state[:]).then_inc(state_left, 16)
            sp.wait_ge(state_left, 16)
            for i in range(2):
                sp.wait_ge(s1_left[i], 16 * NSTEP // 2 + 1)

        @block.gpsimd
        def _(pool):
            nc.gpsimd.memset(state[:], 0.0).then_inc(zeroed, 1)
            pool.wait_ge(const_in, NCONST)
            pool.wait_ge(smp_in, 64)
            nc.gpsimd.tensor_tensor(qd_s[:], q_s[:], q_dec_s.unsqueeze(2).to_broadcast([P, HC, J, TS]), ALU.mult).then_inc(first_qd, 1)
            pool.wait_ge(first_qd, 1)
            pool.wait_ge(first_split, 2)
            with pool.Fori(0, NTURN) as it:
                for i in range(NB):
                    if i < NB:
                        h, slot, n = i % HC, i // HC, NB * it + i
                        if h == 0:
                            pool.wait_ge(chunk_in[slot], 64 * it + 64)
                        pool.wait_ge(us_done, n + 1)
                        pool.sem_inc(pool_go, 1)
                        nc.gpsimd.tensor_tensor(qd[:, i % 2], q[:, slot, h], q_dec[:, h].unsqueeze(1).to_broadcast([P, J, P]),
                                                ALU.mult).then_inc(qd_done, 1)
                        seq = bass.ds(2 * it + slot, 1)
                        nc.gpsimd.tensor_tensor(qx[:, i % 2], qd_s[:, h], of_seq[:, seq].to_broadcast([P, J, TS]),
                                                ALU.mult).then_inc(qx_done, 1)
                        for kx, ks in ((kx_hi, ks_hi), (kx_lo, ks_lo)):
                            nc.gpsimd.tensor_tensor(kx[:, i % 2], ks[:, h].bitcast(F32),
                                                    own[:, seq].unsqueeze(2).to_broadcast([TS, J, P]), ALU.mult).then_inc(kx_done, 1)
                        pool.wait_ge(v_rounded, n + 1)
                        nc.gpsimd.tensor_tensor(v_lo[:, i % 2], v[:, slot, h], v_hi[:, i % 2].bitcast(F32), ALU.subtract).then_inc(v_split, 1)

        @block.tensor
        def _(pe):
            pe.sem_inc(tr_done, 1)
            pe.wait_ge(const_in, NCONST)
            pe.wait_ge(smp_in, 64)
            for h in range(HC):
                if h:
                    pe.wait_ge(first_scm, h)
                for j in range(J):
                    mm = pe.matmul(sc[0:TS, 0:TS], k_s[:, h, j], q_s[:, h, j], start=(j == 0), stop=(j == J - 1))
                mm.then_inc(first_sc, 1)
                if h:
                    pe.wait_ge(first_kd, h)
                for j in range(J):
                    mm = pe.transpose(kt[0:TS, j], k_s[:, h, j], ident)
                mm.then_inc(first_kt, 1)
                pe.wait_ge(first_scm, h + 1)
                if h:
                    pe.wait_ge(first_acc, h)
                pe.matmul(os_[:], scm_s[:, h % 2], v_s[:, h], start=True, stop=True).then_inc(first_os, 1)
            pe.wait_ge(first_kd, HC)
            pe.wait_ge(first_acc, HC)
            pe.wait_ge(zeroed, 1)

            def product(out, m, v, more=False):
                for j, (a, b) in enumerate(((m[0], v[0]), (m[0], v[1]), (m[1], v[0]))):
                    mm = pe.matmul(out, a, b, start=(j == 0), stop=(j == 2 and not more))
                return mm

            def turn_out(n, slot, r):
                pe.wait_ge(gated, n + 2)
                pe.wait_ge(tr_read, n + 1)
                pe.sem_inc(pe_go, 1)
                for c in range(DV // P):
                    mm = pe.transpose(tr[:, c, 0:r], og[0:r, slot, c * P:c * P + P], ident[0:r, 0:r])
                mm.then_inc(tr_done, 1)

            with pe.Fori(0, NTURN) as it:
                for i in range(NB + 2):
                    if i < NB:
                        h, slot, n = i % HC, i // HC, NB * it + i
                        if h == 0:
                            pe.wait_ge(chunk_in[slot], 64 * it + 64)
                        pe.wait_ge(scm_done, n + 1)
                        for j in range(J):
                            mm = pe.matmul(sc[:], k[:, slot, h, j], q[:, slot, h, j], start=(j == 0), stop=(j == J - 1))
                        mm.then_inc(sc_done, 1)
                        pe.wait_ge(kd_done, n + 1)
                        pe.sem_inc(pe_go, 1)
                        for j in range(J):
                            mm = pe.transpose(kt[:, j], k[:, slot, h, j], ident)
                        mm.then_inc(kt_done, 1)
                    if i >= 2:
                        turn_out(NB * it + i - 2, i % 2, P)
                    if 1 <= i <= NB:
                        h, slot, n, m = (i - 1) % HC, (i - 1) // HC, NB * it + i - 1, (i - 1) % 2
                        pe.wait_ge(scm_split, n + 1)
                        pe.wait_ge(v_split, n + 1)
                        pe.wait_ge(qd_done, n + 1)
                        if i >= 2:
                            pe.wait_ge(gated, n)
                        values = v_hi[:, m], v_lo[:, m]
                        product(o[m][:], (scm_hi[:, m], scm_lo[:, m]), values, more=True)
                        for j in range(J):
                            mm = pe.matmul(o[m][:], qd[:, m, j], state[:, h, j], start=False, stop=(j == J - 1))
                        mm.then_inc(o_done, 1)
                        pe.wait_ge(kd_split, n + 1)
                        pe.wait_ge(s1_done, n + HC)
                        for j in range(J):
                            mm = product(u[j][:], (kd_hi[:, m, j], kd_lo[:, m, j]), values)
                        mm.then_inc(u_done, 1)
                        pe.wait_ge(s0_in[h], 32 * it + 16 * slot + 16)
                        pe.wait_ge(qx_done, n + 1)
                        pe.wait_ge(acc_done, n + 1)
                        for j in range(J):
                            mm = pe.matmul(os_[:], qx[:, m, j], s0[h][:, j], start=(j == 0), stop=(j == J - 1))
                        mm.then_inc(os_done, 1)
                        pe.wait_ge(kx_done, 2 * n + 2)
                        pe.wait_ge(state_done, n + HC + 2)
                        for j in range(J):
                            mm = product(u[j][:], (kx_hi[:, m, j], kx_lo[:, m, j]), (vs_hi[:, h], vs_lo[:, h]))
                        mm.then_inc(us_done, 1)
            for h in range(HC):
                turn_out(NSTEP + h, h % 2, TS)

        @block.scalar
        def _(act):
            act.dma_start(table_s[:], consts["ret_s"]).then_inc(const_in, 16)
            act.dma_start(table_p[:], consts["ret_p"]).then_inc(const_in, 16)
            load_exp_ln(nc)
            act.sem_inc(tr_read, 1)
            act.sem_inc(kd_done, 1)
            act.sem_inc(sq_done, 1)
            for i in range(2):
                act.sem_inc(mix_left[i], 1)
                act.sem_inc(s1_left[i], 1)
            act.wait_ge(const_in, NCONST)
            act.wait_ge(smp_in, 64)
            for h in range(HC):
                act.wait_ge(first_kt, h + 1)
                nc.scalar.activation(kd_s[:, h], kt[0:TS], ACT.Copy, scale=k_dec_s[:, h:h + 1]).then_inc(first_kd, 1)
            nc.scalar.copy(vs_hi[:], v_s[:]).then_inc(first_hi, 1)
            act.wait_ge(first_kd, HC)
            nc.scalar.copy(ks_hi[:], kd_s[:]).then_inc(first_hi, 1)
            act.wait_ge(zeroed, 2)

            def norm(n, slot, r, src):
                nc.scalar.activation(square[0:r, :], src, ACT.Square, accum_out=ss[0:r, slot:slot + 1]).then_inc(sq_done, 1)
                act.wait_ge(sq_done, n + 2)
                nc.scalar.activation(ss[0:r, slot:slot + 1], ss[0:r, slot:slot + 1], ACT.Ln, scale=1.0 / DV, bias=eps[0:r, :]).then_inc(ln_done, 1)
                act.wait_ge(ln_done, n + 1)
                nc.scalar.activation(rs[0:r, slot:slot + 1], ss[0:r, slot:slot + 1], ACT.Exp, scale=-0.5).then_inc(rs_done, 1)

            def store(n, nth, slot, r, dst):
                act.wait_ge(tr_done, n + 2)
                act.wait_ge(mix_left[slot], 16 * nth + 1)
                nc.scalar.copy(mix[:, slot, :, 0:r], tr[:, :, 0:r]).then_inc(tr_read, 1)
                act.wait_ge(tr_read, n + 2)
                act.dma_start(dst, mix[:, slot, :, 0:r]).then_inc(mix_left[slot], 16)

            with act.Fori(0, NTURN) as it:
                for i in range(NB + 2):
                    if i < NB:
                        h, n = i % HC, NB * it + i
                        act.wait_ge(kt_done, n + 1)
                        act.wait_ge(us_done, n + 1)
                        if h == 0:
                            act.wait_ge(chunk_in[i // HC], 64 * it + 64)
                        nc.scalar.copy(v_hi[:, i % 2], v[:, i // HC, h]).then_inc(v_rounded, 1)
                        nc.scalar.activation(kd[:, i % 2], kt[:], ACT.Copy, scale=k_dec[:, h:h + 1]).then_inc(kd_done, 1)
                        act.wait_ge(kd_done, n + 2)
                        nc.scalar.copy(kd_hi[:, i % 2], kd[:, i % 2]).then_inc(kd_rounded, 1)
                        act.wait_ge(scm_done, n + 2)
                        nc.scalar.copy(scm_hi[:, i % 2], scm[:, i % 2]).then_inc(scm_rounded, 1)
                    if 1 <= i <= NB:
                        n, m = NB * it + i - 1, (i - 1) % 2
                        act.wait_ge(o_done, n + 1)
                        act.wait_ge(sq_done, n + 1)
                        if i >= 2:
                            act.wait_ge(gated, n)
                        norm(n, m, P, o[m][:])
                    if i >= 2:
                        h, slot, n = (i - 2) % HC, (i - 2) // HC, NB * it + i - 2
                        store(n, NB // 2 * it + (i - 2) // 2, i % 2, P, mix_cols[:, h, :, bass.ds((2 * it + slot) * P, P)])
                        act.wait_ge(s1_done, n + HC + 1)
                        act.dma_start(state_samples[bass.ds(2 * it + slot, 1), h].rearrange("a (j k) v -> k (a j) v", k=P),
                                      s1[i % 2][:]).then_inc(s1_left[i % 2], 16)
            act.wait_ge(acc_done, NSTEP + 1)
            for h in range(HC):
                act.wait_ge(sq_done, NSTEP + h + 1)
                act.wait_ge(gated, NSTEP + h)
                norm(NSTEP + h, h % 2, TS, acc[:, h])
                if h:
                    store(NSTEP + h - 1, (NSTEP + h - 1) // 2, (h - 1) % 2, TS, mix_cols[:, h - 1, :, TP:T])
            store(NSTEP + HC - 1, (NSTEP + HC - 1) // 2, (HC - 1) % 2, TS, mix_cols[:, HC - 1, :, TP:T])
            for i in range(2):
                act.wait_ge(mix_left[i], 16 * (NSTEP + HC) // 2 + 1)

        @block.vector
        def _(dve):
            nc.vector.memset(eps[:], EPS).then_inc(zeroed, 1)
            dve.sem_inc(us_done, 2)
            dve.sem_inc(scm_done, 1)
            dve.sem_inc(gated, 1)
            dve.sem_inc(acc_done, 1)
            dve.sem_inc(state_done, HC + 1)
            dve.sem_inc(s1_done, HC)
            dve.wait_ge(const_in, NCONST)
            dve.wait_ge(smp_in, 64)
            dve.wait_ge(zeroed, 2)
            for h in range(HC):
                dve.wait_ge(first_sc, h + 1)
                dve.tensor_tensor(scm_s[:, h % 2], sc[0:TS, 0:TS], decay_s[:, h], ALU.mult).then_inc(first_scm, 1)
                dve.wait_ge(first_os, h + 1)
                dve.tensor_copy(acc[:, h], os_[:]).then_inc(first_acc, 1)
            dve.wait_ge(first_acc, HC)
            for n, (lo, x, hi) in enumerate(((vs_lo, v_s, vs_hi), (ks_lo, kd_s, ks_hi))):
                dve.wait_ge(first_hi, n + 1)
                dve.tensor_tensor(lo[:], x[:], hi[:].bitcast(F32), ALU.subtract).then_inc(first_split, 1)

            def gate(n, slot, r, src, silu):
                dve.wait_ge(rs_done, n + 1)
                dve.scalar_tensor_tensor(og[0:r, slot, :], src, rs[0:r, slot:slot + 1], silu, ALU.mult, ALU.mult).then_inc(gated, 1)

            with dve.Fori(0, NTURN) as it:
                for i in range(NB + 1):
                    if i < NB:
                        h, n = i % HC, NB * it + i
                        dve.wait_ge(sc_done, n + 1)
                        dve.wait_ge(us_done, n + 1)
                        dve.tensor_tensor(scm[:, i % 2], sc[:], decay[:, h], ALU.mult).then_inc(scm_done, 1)
                        dve.wait_ge(kd_rounded, n + 1)
                        dve.tensor_tensor(kd_lo[:, i % 2], kd[:, i % 2], kd_hi[:, i % 2].bitcast(F32), ALU.subtract).then_inc(kd_split, 1)
                        dve.wait_ge(scm_rounded, n + 1)
                        dve.tensor_tensor(scm_lo[:, i % 2], scm[:, i % 2], scm_hi[:, i % 2].bitcast(F32), ALU.subtract).then_inc(scm_split, 1)
                    if i >= 1:
                        h, slot, n, m = (i - 1) % HC, (i - 1) // HC, NB * it + i - 1, (i - 1) % 2
                        dve.wait_ge(u_done, n + 1)
                        dve.wait_ge(state_done, n + HC + 1)
                        for j in range(J):
                            ins = dve.scalar_tensor_tensor(state[:, h, j], state[:, h, j], gamma[h] ** P, u[j][:], ALU.mult, ALU.add)
                        ins.then_inc(state_done, 1)
                        if i >= 3:
                            dve.wait_ge(tr_done, n)
                        else:
                            dve.wait_ge(tr_done, NB * it + 1)
                        gate(n, m, P, o[m][:], g[:, slot, h])
                        dve.wait_ge(os_done, n + 1)
                        dve.wait_ge(acc_done, n + 1)
                        dve.tensor_tensor(acc[:, h], acc[:, h], os_[:], ALU.add).then_inc(acc_done, 1)
                        dve.wait_ge(us_done, n + 3)
                        dve.wait_ge(s1_left[m], 16 * (NB // 2 * it + (i - 1) // 2) + 1)
                        for j in range(J):
                            ins = dve.scalar_tensor_tensor(s1[m][:, j], s0[h][:, j], gamma[h] ** LS, u[j][:], ALU.mult, ALU.add)
                        ins.then_inc(s1_done, 1)
            dve.wait_ge(acc_done, NSTEP + 1)
            for h in range(HC):
                dve.wait_ge(tr_done, NSTEP + h)
                gate(NSTEP + h, h % 2, TS, acc[:, h], g_s[:, h])



INPUTS = ["x_prompt", "x_sample", "cache_k", "cache_v", "page_table", "state_hgrn", "state_ret", "norm_g",
          "w_in_even", "w_out_even", "q_norm_g", "k_norm_g", "sb_logit_bias", "hgrn_lower_bounds",
          "hgrn_out_norm_g", "w_in_odd", "w_out_odd"]
OUTPUTS = {
    "y_prompt": (1, TP, D), "y_sample": (NS, LS, D),
    "k_prompt": (1, 1, TP, HA, DA), "v_prompt": (1, 1, TP, HA, DA),
    "k_sample": (1, NS, LS, HA, DA), "v_sample": (1, NS, LS, HA, DA),
    "hgrn_prompt": (1, 1, HB, DB, DB), "hgrn_sample": (1, NS, HB, DB, DB),
    "ret_prompt": (1, 1, HC, DK, DV), "ret_sample": (1, NS, HC, DK, DV),
}


def shape_tables():
    f = np.float32
    out = {"ident": np.eye(P, dtype=f)}
    pos = np.concatenate([np.arange(TP), np.tile(PAGE * NPAGE + np.arange(LS), NS)]).astype(f)
    inv = (1.0 / (f(10000.0) ** np.linspace(0.0, 1.0, DK // 2, dtype=f))).astype(f)
    angle = (inv[:, None] * pos[None, :]).astype(f).astype(np.float64)
    key, other = np.arange(P)[:, None], np.arange(P)[None, :]
    out["tri"] = (key >= other).astype(f)
    out["ones"] = np.ones((P, P), f)
    out["mask"] = np.where(key < other, f(0), f(MASKED)).astype(f)
    row = np.arange(P)
    row_s, row_h, row_q = row // (HA * LS), row // LS % HA, row % LS
    out["as_mask"] = np.where(np.arange(LS)[None] < row_q[:, None], f(0), f(MASKED)).astype(f)
    out["as_sel"] = (row_s[:, None] * LS + row_q[:, None] == np.arange(2 * LS)[None]).astype(f)
    out["as_own"] = (row_h[:, None] == np.arange(WA)[None] // DA).astype(f)
    level = np.zeros((P, 8, P), np.int32)
    for l in range(7):
        m = P // 2 >> l
        level[:, l] = (key // (2 * m) == other // (2 * m)) & (key // m % 2 == 0) & (other // m % 2 == 1)
    level[:, 7] = key == other
    out["level_mask"] = level
    out["own"] = (np.arange(TS)[:, None] // LS == np.arange(NS)[None, :]).astype(f)
    t = np.arange(T)
    out["reset"] = np.tile(np.where(t < TP, t % P != 0, (t - TP) % LS != 0).astype(f), (P, 1))
    lg = np.log1p(-np.exp2(-5.0 - np.arange(HC)))
    sk, sq = np.arange(TS)[:, None], np.arange(TS)[None, :]
    rel, rel_s = other - key, sq - sk
    decay = np.stack([np.where(rel >= 0, np.exp(np.maximum(rel, 0) * g), 0) for g in lg], 1)
    seen = (sk // LS == sq // LS) & (rel_s >= 0)
    decay_s = np.stack([np.where(seen, np.exp(np.where(seen, rel_s, 0) * g), 0) for g in lg], 1)
    i, i_s = np.arange(P), np.arange(TS) % LS
    rows = lambda x, n=P: np.broadcast_to(x, (n, *x.shape)).reshape(n, -1)
    flat = lambda x: x.reshape(x.shape[0], -1)
    out["ret_p"] = np.concatenate([out["ident"], flat(decay), rows(np.exp((i + 1) * lg[:, None])), rows(np.exp((i_s + 1) * lg[:, None])),
                                   rows(out["own"].T), np.exp((P - 1 - i)[:, None] * lg[None])], 1).astype(f)
    out["ret_s"] = np.concatenate([flat(decay_s), out["own"], np.exp((LS - 1 - i_s)[:, None] * lg[None])], 1).astype(f)
    out["cos"], out["sin"] = np.cos(angle).astype(f), np.sin(angle).astype(f)
    return out


def build(nc, a, o, consts):
    dram = lambda n, s: nc.dram_tensor(n, s, F32).ap()
    q_tm = dram("q_tm", (T, WA))
    qb_fm, fb_fm, ga_fm, gb_fm = (dram(n, (WB, T)) for n in ("qb_fm", "fb_fm", "ga_fm", "gb_fm"))
    ib_tm = dram("ib_tm", (T, WB))
    tm2 = lambda t: t.rearrange("a b t h d -> (a b t) (h d)")
    k_p, v_p, k_s, v_s = (tm2(o[n]) for n in ("k_prompt", "v_prompt", "k_sample", "v_sample"))
    x_p, x_s = (a[n].rearrange("b t d -> (b t) d") for n in ("x_prompt", "x_sample"))

    def split_tm(prompt, sample):
        return lambda t, col: (prompt[t * P:t * P + P, bass.ds(col, WBLK)] if t < NT - 1
                               else sample[:, bass.ds(col, WBLK)])

    def whole_tm(x):
        return lambda t, col: x[t * P:t * P + rows_of(t), bass.ds(col, WBLK)]

    def rows_fm(x):
        tiles = x.rearrange("(r p) t -> r p t", p=P)
        return lambda row: tiles[row] if isinstance(row, int) else tiles[bass.ds(row, 1)].rearrange("a p t -> (a p) t")

    x_of = lambda t: x_p[t * P:t * P + P] if t < NT - 1 else x_s
    project_in(nc, "even", x_of, a["norm_g"][0].rearrange("(c p) -> p c", p=P), a["w_in_even"][0], [
        ("norm", 1, whole_tm(q_tm)), ("norm", 1, split_tm(k_p, k_s)), ("copy", 1, split_tm(v_p, v_s)),
        ("silu", 1, rows_fm(ga_fm)), ("silu", 1, rows_fm(qb_fm)), ("plain", 1, rows_fm(fb_fm)),
        ("copy", 1, whole_tm(ib_tm)), ("silu", 1, rows_fm(gb_fm))], consts, (a["q_norm_g"], a["k_norm_g"]))
    mix0 = dram("mix0", (WA + WB, T))
    attend(nc, q_tm, k_p, v_p, k_s, v_s, ga_fm, a["sb_logit_bias"], a["cache_k"][0], a["cache_v"][0], a["page_table"],
           mix0, consts)
    hgrn(nc, qb_fm, fb_fm, ib_tm, gb_fm, a["hgrn_lower_bounds"], a["hgrn_out_norm_g"][0], a["state_hgrn"][0],
         o["hgrn_prompt"][0, 0], o["hgrn_sample"][0], mix0, consts)
    tile = lambda prompt, sample: lambda t: sample if isinstance(t, int) and t == NT - 1 else prompt[bass.ds(t * P, P)]
    y1 = dram("y1", (T, D))
    project_out(nc, "out0", mix0, a["w_out_even"][0], tile(x_p, x_s), tile(y1, y1[TP:T]))

    q1_fm, k1_fm = dram("q1_fm", (HC * DK, T)), dram("k1_fm", (HC * DK, T))
    v1_tm, g1_tm = dram("v1_tm", (T, WC)), dram("g1_tm", (T, WC))

    def head_fm(x, first=0):
        return lambda row: x.rearrange("(h r) t -> h r t", r=DK)[bass.ds(row + first, 1)].rearrange("a (j p) t -> p (a j) t", p=P)

    npair = HC * DK // (2 * WBLK)
    project_in(nc, "odd", lambda t: y1[t * P:t * P + rows_of(t)], a["norm_g"][1].rearrange("(c p) -> p c", p=P),
               a["w_in_odd"][0], [("rotary", 1, head_fm(q1_fm)), ("rotary", npair - 1, head_fm(q1_fm, 2)), ("rotary", npair, head_fm(k1_fm)),
                                  ("copy", WC // (2 * WBLK), whole_tm(v1_tm)), ("silu_tm", WC // (2 * WBLK), whole_tm(g1_tm))], consts)
    mix1 = dram("mix1", (WC, T))
    retention(nc, q1_fm, k1_fm, v1_tm, g1_tm, a["state_ret"][0], o["ret_prompt"][0, 0], o["ret_sample"][0], mix1, consts)
    y_p, y_s = (o[n].rearrange("b t d -> (b t) d") for n in ("y_prompt", "y_sample"))
    project_out(nc, "out1", mix1, a["w_out_odd"][0], tile(y1, y1[TP:T]), tile(y_p, y_s))


def make(nc, arrays):
    a = {n: nc.dram_tensor(f"in_{n}", arrays[f"in_{n}"].shape, mybir.dt.from_np(arrays[f"in_{n}"].dtype),
                           kind="ExternalInput").ap() for n in INPUTS}
    consts = {n[6:]: nc.dram_tensor(n, v.shape, mybir.dt.from_np(v.dtype), kind="ExternalInput").ap()
              for n, v in arrays.items() if n.startswith("table_")}
    o = {n: nc.dram_tensor(f"out_{n}", s, F32, kind="ExternalOutput").ap() for n, s in OUTPUTS.items()}
    build(nc, a, o, consts)


def layout(inputs):
    arrays = {f"in_{n}": np.ascontiguousarray(inputs[n]) for n in INPUTS}
    arrays |= {f"table_{n}": v for n, v in shape_tables().items()}
    return arrays


def kernel(**inputs):
    import concourse.bacc as bacc
    from concourse.bass_utils import run_bass_kernel_spmd

    nc = bacc.Bacc("TRN2", target_bir_lowering=False, num_devices=1)
    arrays = layout(inputs)
    make(nc, arrays)
    got = run_bass_kernel_spmd(nc, [arrays], core_ids=[0]).results[0]
    return tuple(got[f"out_{n}"] for n in OUTPUTS)
```
